# Optimizing a Trainium2 kernel written in Bass

```python
import jax, jax.numpy as jnp
from jax import lax
import numpy as np

D_MODEL = 1024
BATCH = 1
SEQ = 512
DEPTH = 1
DEC_BATCH = 8
DEC_SEQ = 4
PAST_LEN = 4096
PAGE_SIZE = 128

D_MIX = D_MODEL
D_CONV = D_MIX // 2
CONV_GROUPS = 8
CONV_W = 3
D_MLSTM = D_MIX - D_CONV
MLSTM_HEADS = 4
MLSTM_DH = D_MLSTM // MLSTM_HEADS
MLSTM_CHUNK = 64
D_IN = 3 * D_CONV + 4 * D_MLSTM + 2 * MLSTM_HEADS
PEER_HEADS = 8
PEER_NKEYS = 128
PEER_NEXP = PEER_NKEYS * PEER_NKEYS
PEER_DKEY = 256
PEER_DHALF = PEER_DKEY // 2
PEER_TOPK = 16
PEER_BLOCK = 256
EPS = 1e-6

kernel_name = "hybrid_conv_mlstm_peer_adaln_step"

def group_rmsnorm(x, n_groups, g):
    shp = x.shape
    xf = x.astype(jnp.float32).reshape(shp[:-1] + (n_groups, shp[-1] // n_groups))
    y = xf * lax.rsqrt(jnp.mean(xf * xf, axis=-1, keepdims=True) + EPS)
    return (y.reshape(shp) * g).astype(x.dtype)

def rmsnorm(x, g):
    return group_rmsnorm(x, 1, g)

def mlstm_chunk(carry, inp):
    C, n, m = carry
    q, k, v, li, lf = inp
    L = q.shape[2]
    b = jnp.cumsum(lf, axis=-1)
    a = b + m[..., None]
    causal = jnp.tril(jnp.ones((L, L), dtype=bool))
    dmat = jnp.where(causal, b[..., :, None] - b[..., None, :] + li[..., None, :], -jnp.inf)
    mt = jnp.maximum(a, jnp.max(dmat, axis=-1))
    w_inter = jnp.exp(a - mt)
    s = jnp.einsum('bhtd,bhsd->bhts', q, k) * jnp.exp(dmat - mt[..., None])
    num = w_inter[..., None] * jnp.einsum('bhtk,bhkv->bhtv', q, C) + jnp.einsum('bhts,bhsv->bhtv', s, v)
    den = w_inter * jnp.einsum('bhtk,bhk->bht', q, n) + jnp.sum(s, axis=-1)
    h = num / jnp.maximum(jnp.abs(den), jnp.exp(-mt))[..., None]
    bl = b[..., -1]
    gl = bl[..., None] - b + li
    m_new = jnp.maximum(bl + m, jnp.max(gl, axis=-1))
    w_old = jnp.exp(bl + m - m_new)
    w_s = jnp.exp(gl - m_new[..., None])
    C_new = w_old[..., None, None] * C + jnp.einsum('bhs,bhsk,bhsv->bhkv', w_s, k, v)
    n_new = w_old[..., None] * n + jnp.einsum('bhs,bhsk->bhk', w_s, k)
    return (C_new, n_new, m_new), h

def mlstm_sequence(q, k, v, li, lf, state):
    L = q.shape[2]
    chunk = MLSTM_CHUNK if (L % MLSTM_CHUNK == 0) else L
    if chunk == L:
        return mlstm_chunk(state, (q, k, v, li, lf))
    nc = L // chunk
    def to_chunks(t):
        t = t.reshape(t.shape[:2] + (nc, chunk) + t.shape[3:])
        return jnp.moveaxis(t, 2, 0)
    xs = (to_chunks(q), to_chunks(k), to_chunks(v), to_chunks(li), to_chunks(lf))
    new_state, hs = lax.scan(mlstm_chunk, state, xs)
    hs = jnp.moveaxis(hs, 0, 2)
    return new_state, hs.reshape(hs.shape[:2] + (L, hs.shape[-1]))

def token_mixer(h, conv_state, C0, n0, m0, w_in, w_conv, b_i, b_f, g_conv, g_mlstm, w_out):
    bsz, L, _ = h.shape
    z = h @ w_in
    sizes = [D_CONV] * 3 + [D_MLSTM] * 4 + [MLSTM_HEADS] * 2
    splits = [int(s) for s in np.cumsum(sizes)[:-1]]
    xc, bg, cg, q, k, v, o, ig, fg = jnp.split(z, splits, axis=-1)
    u = cg * xc
    full = jnp.concatenate([conv_state.astype(u.dtype), u], axis=1)
    conv = w_conv[0] * full[:, 0:L]
    for j in range(1, CONV_W):
        conv = conv + w_conv[j] * full[:, j:j + L]
    y_conv = bg * conv
    new_conv = full[:, L:]
    def heads(t):
        return t.reshape(bsz, L, MLSTM_HEADS, MLSTM_DH).transpose(0, 2, 1, 3).astype(jnp.float32)
    qh = heads(q)
    kh = heads(k) * (MLSTM_DH ** -0.5)
    vh = heads(v)
    li = (ig + b_i).astype(jnp.float32).transpose(0, 2, 1)
    lf = jax.nn.log_sigmoid((fg + b_f).astype(jnp.float32)).transpose(0, 2, 1)
    state = (C0.astype(jnp.float32), n0.astype(jnp.float32), m0.astype(jnp.float32))
    (Cn, nn_, mn), hm = mlstm_sequence(qh, kh, vh, li, lf, state)
    hm = hm.transpose(0, 2, 1, 3).reshape(bsz, L, D_MLSTM)
    hm = jax.nn.sigmoid(o.astype(jnp.float32)) * hm
    y_m = group_rmsnorm(hm, MLSTM_HEADS, g_mlstm).astype(h.dtype)
    y = jnp.concatenate([group_rmsnorm(y_conv, CONV_GROUPS, g_conv), y_m], axis=-1) @ w_out
    return y, new_conv, Cn, nn_, mn

def peer(h, w_pq, sub_keys, u_tab, v_tab):
    bsz, L, D = h.shape
    T = bsz * L
    nb = -(-T // PEER_BLOCK)
    xf = jnp.pad(h.reshape(T, D), ((0, nb * PEER_BLOCK - T), (0, 0))).reshape(nb, PEER_BLOCK, D)
    def block(xb):
        q = (xb @ w_pq).reshape(PEER_BLOCK, PEER_HEADS, 2, PEER_DHALF).astype(jnp.float32)
        s = jnp.einsum('thpd,phnd->thpn', q, sub_keys.astype(jnp.float32))
        s1, i1 = lax.top_k(s[:, :, 0], PEER_TOPK)
        s2, i2 = lax.top_k(s[:, :, 1], PEER_TOPK)
        cand = (s1[..., :, None] + s2[..., None, :]).reshape(PEER_BLOCK, PEER_HEADS, PEER_TOPK * PEER_TOPK)
        cidx = (i1[..., :, None] * PEER_NKEYS + i2[..., None, :]).reshape(PEER_BLOCK, PEER_HEADS, PEER_TOPK * PEER_TOPK)
        top, pos = lax.top_k(cand, PEER_TOPK)
        eidx = jnp.take_along_axis(cidx, pos, axis=-1)
        gate = jax.nn.softmax(top, axis=-1)
        a = jnp.einsum('thkd,td->thk', u_tab[eidx], xb).astype(jnp.float32)
        act = (jax.nn.gelu(a) * gate).astype(xb.dtype)
        return jnp.einsum('thk,thkd->td', act, v_tab[eidx])
    out = lax.map(block, xf).reshape(nb * PEER_BLOCK, D)[:T]
    return out.reshape(bsz, L, D)

def run_stack(x, c, st_conv, st_C, st_n, st_m, w_mod, b_mod, g_mix, w_in, w_conv, b_i, b_f,
              g_conv, g_mlstm, w_out, g_ffn, w_pq, sub_keys, u_tab, v_tab, g_final):
    convs, Cs, ns, ms = [], [], [], []
    for l in range(DEPTH):
        mod = jax.nn.silu(c) @ w_mod[l] + b_mod[l]
        sh1, sc1, gt1, sh2, sc2, gt2 = jnp.split(mod[:, None, :], 6, axis=-1)
        h = rmsnorm(x, g_mix[l]) * (1 + sc1) + sh1
        mix, cv, Cn, nn_, mn = token_mixer(h, st_conv[l], st_C[l], st_n[l], st_m[l], w_in[l], w_conv[l],
                                         b_i[l], b_f[l], g_conv[l], g_mlstm[l], w_out[l])
        x = x + gt1 * mix
        h = rmsnorm(x, g_ffn[l]) * (1 + sc2) + sh2
        x = x + gt2 * peer(h, w_pq[l], sub_keys[l], u_tab[l], v_tab[l])
        convs.append(cv); Cs.append(Cn); ns.append(nn_); ms.append(mn)
    return rmsnorm(x, g_final), jnp.stack(convs), jnp.stack(Cs), jnp.stack(ns), jnp.stack(ms)

def setup_inputs(seed: int = 0) -> dict:
    key = jax.random.key(seed)
    ks = jax.random.split(key, 32)
    nrm = jax.random.normal
    f32 = jnp.float32
    D = D_MODEL
    return {
        "x_prompt": nrm(ks[0], (BATCH, SEQ, D), f32),
        "x_sample": nrm(ks[1], (DEC_BATCH, DEC_SEQ, D), f32),
        "c_prompt": nrm(ks[2], (BATCH, D), f32),
        "c_sample": nrm(ks[3], (DEC_BATCH, D), f32),
        "state_conv": 0.5 * nrm(ks[4], (DEPTH, DEC_BATCH, CONV_W - 1, D_CONV), f32),
        "state_mlstm_C": 0.1 * nrm(ks[5], (DEPTH, DEC_BATCH, MLSTM_HEADS, MLSTM_DH, MLSTM_DH), f32),
        "state_mlstm_n": 0.1 * nrm(ks[6], (DEPTH, DEC_BATCH, MLSTM_HEADS, MLSTM_DH), f32),
        "state_mlstm_m": 0.5 * nrm(ks[7], (DEPTH, DEC_BATCH, MLSTM_HEADS), f32),
        "w_mod": 0.5 * D ** -0.5 * nrm(ks[8], (DEPTH, D, 6 * D), f32),
        "b_mod": 0.02 * nrm(ks[9], (DEPTH, 6 * D), f32),
        "g_mix": 1.0 + 0.02 * nrm(ks[10], (DEPTH, D), f32),
        "w_in": D ** -0.5 * nrm(ks[11], (DEPTH, D, D_IN), f32),
        "w_conv": CONV_W ** -0.5 * nrm(ks[12], (DEPTH, CONV_W, D_CONV), f32),
        "b_i": 0.1 * nrm(ks[13], (DEPTH, MLSTM_HEADS), f32),
        "b_f": jnp.linspace(3.0, 6.0, MLSTM_HEADS, dtype=f32)[None, :] + 0.1 * nrm(ks[14], (DEPTH, MLSTM_HEADS), f32),
        "g_conv": 1.0 + 0.02 * nrm(ks[15], (DEPTH, D_CONV), f32),
        "g_mlstm": 1.0 + 0.02 * nrm(ks[16], (DEPTH, D_MLSTM), f32),
        "w_out": D_MIX ** -0.5 * nrm(ks[17], (DEPTH, D_MIX, D), f32),
        "g_ffn": 1.0 + 0.02 * nrm(ks[18], (DEPTH, D), f32),
        "w_pq": D ** -0.5 * nrm(ks[19], (DEPTH, D, PEER_HEADS * PEER_DKEY), f32),
        "sub_keys": PEER_DHALF ** -0.5 * nrm(ks[20], (DEPTH, 2, PEER_HEADS, PEER_NKEYS, PEER_DHALF), f32),
        "u_tab": D ** -0.5 * nrm(ks[21], (DEPTH, PEER_NEXP, D), f32),
        "v_tab": nrm(ks[22], (DEPTH, PEER_NEXP, D), f32),
        "g_final": 1.0 + 0.02 * nrm(ks[23], (D,), f32),
    }

def reference(x_prompt, x_sample, c_prompt, c_sample, state_conv, state_mlstm_C, state_mlstm_n, state_mlstm_m,
              w_mod, b_mod, g_mix, w_in, w_conv, b_i, b_f, g_conv, g_mlstm, w_out, g_ffn, w_pq, sub_keys,
              u_tab, v_tab, g_final):
    weights = (w_mod, b_mod, g_mix, w_in, w_conv, b_i, b_f, g_conv, g_mlstm, w_out, g_ffn, w_pq, sub_keys,
               u_tab, v_tab, g_final)
    bp = x_prompt.shape[0]
    z_conv = jnp.zeros((DEPTH, bp, CONV_W - 1, D_CONV), x_prompt.dtype)
    z_C = jnp.zeros((DEPTH, bp, MLSTM_HEADS, MLSTM_DH, MLSTM_DH), jnp.float32)
    z_n = jnp.zeros((DEPTH, bp, MLSTM_HEADS, MLSTM_DH), jnp.float32)
    z_m = jnp.zeros((DEPTH, bp, MLSTM_HEADS), jnp.float32)
    y_prompt, conv_p, C_p, n_p, m_p = run_stack(x_prompt, c_prompt, z_conv, z_C, z_n, z_m, *weights)
    y_sample, conv_s, C_s, n_s, m_s = run_stack(x_sample, c_sample, state_conv, state_mlstm_C, state_mlstm_n,
                                                state_mlstm_m, *weights)
    return (y_prompt, y_sample, conv_p, C_p, n_p, m_p, conv_s, C_s, n_s, m_s)


_drawn_inputs = setup_inputs


def setup_inputs(seed=0):
    import zlib

    import numpy as np

    out = dict(_drawn_inputs(seed))
    spreads = {}
    factors = {'g_conv': 50.509, 'g_mlstm': 50.652, 'g_final': 25.113, 'g_ffn': 14.475}
    for name, (base, spread) in spreads.items():
        noise = np.random.default_rng([zlib.crc32(name.encode()), seed]).standard_normal(out[name].shape)
        drawn = base * np.exp(spread * noise) if base else spread * noise
        out[name] = __import__('jax').numpy.asarray(drawn.astype(out[name].dtype))
    for name, factor in factors.items():
        out[name] = (out[name] * factor).astype(out[name].dtype)
    return out
```

```python
from contextlib import ExitStack

import concourse.bass as bass
from concourse import mybir

F32 = mybir.dt.float32
F32R = mybir.dt.float32r
U32 = mybir.dt.uint32
ALU = mybir.AluOpType
ACT = mybir.ActivationFunctionType
AXX = mybir.AxisListType.X

P = 128
D = 1024
KT = D // P
TP = 512
NB, NL = 8, 4
TS = NB * NL
T = TP + TS
HF = T // 2
NH = 4
DH = 128
DC = 512
CT = DC // P
NSEQ = 1 + NB
PH, PK = 8, 16
NKEY = 128
HP = 2 * PH
GC = 256
NMOD = 6 * D // GC
NIN = 1 + 7 * 512 // GC
NOUT = D // GC
NPQ = HP * NKEY // GC
NW = NMOD + NIN + NOUT + NPQ
RAW = 4
LOWEST = -3.0e38
BIG = 1.0e30
VEC = {}
_at = 0
for _name, _n in (("g_mix", KT), ("g_ffn", KT), ("g_final", KT), ("g_conv", CT), ("g_mlstm", NH),
                  ("w_conv", 3 * CT), ("b_mod", 6 * KT)):
    VEC[_name] = (_at, _at + _n)
    _at += _n
NVEC = _at
EOFF = [0, 512, 896, 1152]
EW = 1280
NCH = NKEY
GRP = 8
NT = 2 * NCH
STILES = [0, 128, 256, 384, T - P]
NST = len(STILES)
TB = 32
NTB = T // TB
STEP_TOK = TB // 4
Q_EXP = 13
Q_GATE = Q_EXP + 1


def build(nc, a, o):
    with ExitStack() as ctx:
        base, top = 17408, 229344
        ctx.enter_context(nc.sbuf_tensor("arena", [P, (top - 16512) // 4 - 8], F32))

        def at(name, shape, offset, dt=F32):
            n = 4
            for s in shape[1:]:
                n *= s
            assert base <= offset and offset + n <= top and offset % 32 == 0, (name, offset, n)
            return nc.alloc_sbuf_tensor_at(name, shape, dt, offset=offset)

        pos = [base]

        def keep(name, shape, dt=F32):
            n = 4
            for s in shape[1:]:
                n *= s
            t = at(name, shape, pos[0], dt)
            pos[0] += -(-n // 32) * 32
            return t

        xT = keep("xT", [P, KT, T])
        mod = keep("mod", [P, 6 * KT, NSEQ])
        amod = keep("amod", [P, 2, KT, NSEQ])
        vec = keep("vec", [P, NVEC])
        ident = keep("ident", [P, P])
        ones = keep("ones", [P, P])
        blk = keep("blk", [P, P])
        iota = keep("iota", [P, P])
        cmask = keep("cmask", [P, P])
        smask = keep("smask", [TS, TS])
        bmask = keep("bmask", [TS, NB])
        sel = keep("sel", [NH, NH, P])
        eps = keep("eps", [P, 1])
        cT = keep("cT", [P, KT, NSEQ])
        sq = keep("sq", [P, 2, T])
        rs = keep("rs", [P, T])
        R0 = pos[0]
        RAW_AT = R0
        SPL_AT = RAW_AT + 32768
        H_AT = SPL_AT + 32768
        Z_AT = H_AT + 34816
        C_AT = Z_AT + 34816
        TAIL = C_AT + 17408 + 8224 + 768
        TAIL += -TAIL % 32

        raw = at("raw", [P, RAW, KT, GC], RAW_AT)
        wHi = at("wHi", [P, 2, KT, GC], SPL_AT, F32R)
        wLo = at("wLo", [P, 2, KT, GC], SPL_AT + 16384, F32R)
        hHi = at("hHi", [P, KT, T], H_AT, F32R)
        hLo = at("hLo", [P, KT, T], H_AT + 17408, F32R)
        zq = at("zq", [P, NH, T], Z_AT)
        zk = at("zk", [P, NH, T], Z_AT + 8704)
        zv = at("zv", [P, NH, T], Z_AT + 2 * 8704)
        zo = at("zo", [P, NH, T], Z_AT + 3 * 8704)
        hf = at("hf", [P, KT, T], C_AT)
        xc = at("xc", [P, CT, T], C_AT)
        bg = at("bg", [P, CT, T], C_AT + 8704)
        up = at("up", [P, CT, 2 + TP], C_AT + 17408)
        us = at("us", [P, CT, NB, 2 + NL], C_AT + 17408 + 8224)
        row_li = at("row_li", [P, T], TAIL)
        row_lf = at("row_lf", [NH, T], TAIL + 2176)
        row_t = at("row_t", [NH, T], TAIL + 2 * 2176)
        row_b = at("row_b", [NH, T], TAIL + 3 * 2176)
        row_r = at("row_r", [NH, T], TAIL + 4 * 2176)
        row_m = at("row_m", [NH, T], TAIL + 5 * 2176)
        row_z = at("row_z", [NH, T], TAIL + 6 * 2176)
        small = at("small", [NH, 64], TAIL + 7 * 2176)
        gbias, m0 = small[:, 0:2], small[:, 2:10]
        wi = small[:, 10:10 + TS]
        wold = small[:, 42:50]
        mout = small[:, 50:59]

        mp = [SPL_AT]

        def mix(name, shape, dt=F32):
            n = 4
            for s in shape[1:]:
                n *= s
            t = at(name, shape, mp[0], dt)
            mp[0] += -(-n // 32) * 32
            assert mp[0] <= SPL_AT + 32768, name
            return t

        ktok = mix("ktok", [P, NH + 1, DH])
        vtok = mix("vtok", [P, NH + 1, DH])
        vw = mix("vw", [P, NH, DH])
        er = mix("er", [P, EW + TS])
        vsw = mix("vsw", [TS, DH])
        vsm = mix("vsm", [TS, NB, DH])
        csb = mix("csb", [P, NB, DH])
        cst = mix("cst", [P, NH, DH])
        dn = mix("dn", [P, T])
        rcol = mix("rcol", [P, 2, NH + 1, NH])
        wsm = mix("wsm", [TS, NB])
        npo = mix("npo", [P, NH])
        nso = mix("nso", [P, NH, NB])
        n0 = mix("n0", [P, NH, NB])
        qwi = mix("qwi", [P, NH, TS])
        qn = mix("qn", [P, NH, TS])
        wib = mix("wib", [P, NH, TS + NB])
        gr = mix("gr", [P, 2, T])
        mb = at("mb", [P, NH, T], C_AT + 8704)
        emb = at("emb", [P, NH, T], C_AT + 17408)

        qT = at("qT", [P, HP, T], Z_AT)
        keys = at("keys", [P, HP, NKEY], C_AT + 17408)
        sc = at("sc", [P, NST, HP, NKEY], RAW_AT)
        tHi = at("tHi", [P, 2, KT, P], SPL_AT + 16384, F32R)
        tLo = at("tLo", [P, 2, KT, P], SPL_AT + 24576, F32R)
        ga = at("ga", [P, 2, T], SPL_AT + 8192)
        tab = at("tab", [P, RAW, KT, P], TAIL)
        zp = [Z_AT]

        def peer(name, shape, dt=F32):
            n = 4
            for q in shape[1:]:
                n *= q
            t = at(name, shape, zp[0], dt)
            zp[0] += -(-n // 32) * 32
            assert zp[0] <= Z_AT + 34816, name
            return t

        m16 = peer("m16", [P, HP, PK])
        ix = peer("ix", [P, HP, PK], U32)
        ixf = peer("ixf", [P, HP, PK])
        cand = peer("cand", [P, PH, PK, PK])
        pos16 = peer("pos16", [P, PH, PK], U32)
        pab = peer("pab", [P, 2, PH * PK], U32)
        pabf = peer("pabf", [P, 2, PH * PK])
        eqa = peer("eqa", [P, PH, PK, PK])
        scur = peer("scur", [P, HP, NKEY])
        tcur = peer("tcur", [P, PH, PK])
        eqb = at("eqb", [P, PH, PK, PK], C_AT)
        best = at("best", [P, 3, NST, PH * PK], C_AT + 8192)
        ssum = at("ssum", [P, NST * PH], C_AT + 8192 + 7680)
        idxT = at("idxT", [P, 4, T], C_AT + 17408)
        gHr = at("gHr", [P, T], C_AT, F32R)
        zp[0] = Z_AT
        oh2 = peer("oh2", [P, 2, STEP_TOK, P], F32R)
        w1h = peer("w1h", [P, 2, STEP_TOK, P], F32R)
        w1l = peer("w1l", [P, 2, STEP_TOK, P], F32R)
        cb = peer("cb", [P, 2, 4, STEP_TOK])
        stage = at("stage", [P, 2, NKEY, TB], RAW_AT)
        actHi = [at("actHi0", [P, GRP, T], Z_AT, F32R), at("actHi1", [P, GRP, T], H_AT, F32R)]
        actLo = [at("actLo0", [P, GRP, T], Z_AT + 17408, F32R), at("actLo1", [P, GRP, T], H_AT + 17408, F32R)]
        gt = at("gt", [P, 2, NTB, 4, TB], RAW_AT)
        gin = at("gin", [P, 4, T], RAW_AT + 17408)
        a32 = at("a32", [P, 2, T], RAW_AT + 17408 + 8704)
        acc = at("acc", [P, KT, T], C_AT)
        ga_dram = nc.dram_tensor("gelu_scratch", (NCH, P, T), F32, kind="Internal").ap()
        gt_dram = nc.dram_tensor("gate_scratch", (NCH // 4, P, NTB, 4 * TB), F32, kind="Internal").ap()

        ps = ctx.enter_context(nc.psum_tensor("ps", [P, 8, 512], F32))

        def pair(n):
            s = 2 * (n % 2)
            return ps[:, s:s + 2, 0:HF]

        def sem(name):
            return ctx.enter_context(nc.semaphore(name))

        s_vec = sem("small_inputs_landed")
        s_x = sem("x_landed")
        s_const = sem("constants_ready")
        s_raw = [sem(f"raw_landed{i}") for i in range(RAW)]
        s_rawfree = [sem(f"raw_free{i}") for i in range(RAW)]
        s_silu = sem("silu_ready")
        s_sq = sem("square_ready")
        s_squsd = sem("square_used")
        s_nrm = sem("square_sum_done")
        s_rms = sem("rms_ready")
        s_rsq = sem("inverse_rms_ready")
        s_xn = sem("x_normed")
        s_modp = sem("mod_product_done")
        s_mods = sem("mod_ready")
        s_aff = sem("prompt_affine_done")
        s_smp = sem("sample_affine_done")
        s_hhi = sem("h_hi_ready")
        s_hlo = sem("h_lo_ready")
        s_whi = sem("w_hi_ready")
        s_wlo = sem("w_lo_ready")
        s_wfree = sem("w_split_free")
        s_pj = sem("projection_done")
        s_ev = sem("projection_evacuated")
        s_conv = sem("conv_done")
        s_state = sem("conv_state_landed")
        s_convout = sem("conv_state_copied")
        s_rowa = sem("row_neg_abs_ready")
        s_rowe = sem("row_softplus_ready")
        s_rows = sem("rows_ready")
        s_rowx = sem("row_exps_ready")
        s_bc = sem("row_broadcast_done")
        s_bce = sem("row_broadcast_evacuated")
        s_col = sem("columns_transposed")
        s_colc = sem("columns_ready")
        s_n0 = sem("n0_landed")
        s_qn = sem("q_weighted")
        s_tok = sem("kv_transposed")
        s_tokc = sem("kv_tokens_ready")
        s_sp = sem("scores_done")
        s_er = sem("decay_exponents_ready")
        s_ex = sem("decay_weights_ready")
        s_p = sem("weighted_scores_ready")
        s_num = sem("numerator_done")
        s_hm = sem("head_output_ready")
        s_vw = sem("weighted_values_ready")
        s_stp = sem("state_product_done")
        s_stc = sem("state_ready")
        s_c0 = sem("c0_landed")
        s_gsq = sem("group_square_ready")
        s_gst = sem("group_sum_done")
        s_grms = sem("group_rms_ready")
        s_y = sem("mixer_normed")
        s_x1 = sem("residual_added")
        s_key = sem("keys_landed")
        s_scp = sem("retrieval_scores_done")
        s_sc = sem("retrieval_scores_ready")
        s_tk = sem("retrieval_chain")
        s_top = sem("retrieved_scores_ready")
        s_gexp = sem("retrieved_exps_ready")
        s_best = sem("retrieved_ready")
        s_bestT = sem("retrieved_transposed")
        s_idx = sem("expert_rows_ready")
        s_tab = [sem(f"table_landed{i}") for i in range(RAW)]
        s_thi = sem("table_hi_ready")
        s_tlo = sem("table_lo_ready")
        s_prod = sem("table_product_done")
        s_gelu = sem("gelu_ready")
        s_gfree = sem("a_banks_free")
        s_gas = [sem(f"gelu_stored{i}") for i in range(2)]
        s_oh = sem("one_hots_ready")
        s_cb = sem("token_columns_ready")
        s_gmm = sem("gate_product_done")
        s_ohfree = sem("one_hots_free")
        s_gev = sem("gate_evacuated")
        s_gevfree = sem("gate_banks_free")
        s_gst2 = sem("gate_block_stored")
        s_gin = [sem(f"gelu_landed{i}") for i in range(4)]
        s_gt = [sem(f"gates_landed{i}") for i in range(2)]
        s_a32 = sem("act_ready")
        s_ahi = sem("act_hi_ready")
        s_alo = sem("act_lo_ready")
        s_flush = sem("product_added")
        s_yo = sem("y_ready")
        s_dch = sem("vector_chain")
        s_pch = sem("pool_chain")
        s_ach = sem("scalar_chain")
        s_out = sem("outputs_stored")

        def linker(eng, s):
            n = [0]

            def link(ins):
                n[0] += 1
                ins.then_inc(s, 1)
                eng.wait_ge(s, n[0])
            return link

        def col(name, i=0):
            return vec[:, VEC[name][0] + i:VEC[name][0] + i + 1]

        def span(name):
            return vec[:, VEC[name][0]:VEC[name][1]]

        def smp(ap):
            return ap.rearrange("p k (b l) -> p k b l", l=NL)

        def over(ap, n):
            return ap.unsqueeze(len(ap.shape)).broadcast_to(list(ap.shape) + [n])

        block = ctx.enter_context(nc.Block())

        @block.sync
        def _(sp):
            sp.dma_start(vec[:], a["vecs"]).then_inc(s_vec, 16)
            sp.dma_start(cT[:], a["cT"]).then_inc(s_vec, 16)
            sp.dma_start(small[:, 0:10], a["rows"]).then_inc(s_vec, 16)
            sp.dma_start(xT[:], a["xT"]).then_inc(s_x, 16)

            def load(n):
                if n >= RAW:
                    sp.wait_ge(s_rawfree[n % RAW], n // RAW)
                sp.dma_start(raw[:, n % RAW], a["w"][n]).then_inc(s_raw[n % RAW], 16)

            for n in range(NMOD + NIN):
                load(n)
                if n == NMOD + 4:
                    sp.wait_ge(s_hlo, KT)
                    sp.dma_start(us[:, :, :, 0:2], a["sconv"]).then_inc(s_state, 16)
            sp.wait_ge(s_pj, 2 * NIN - 1)
            sp.dma_start(n0[:], a["n0"]).then_inc(s_n0, 16)
            sp.dma_start(csb[:], a["C0"][:, 0]).then_inc(s_c0, 16)
            sp.wait_ge(s_convout, 1)
            sp.dma_start(o["conv_p"], up[:, :, TP:TP + 2]).then_inc(s_out, 16)
            sp.dma_start(o["conv_s"], us[:, :, :, NL:NL + 2]).then_inc(s_out, 16)
            for n in range(NMOD + NIN, NMOD + NIN + 4):
                load(n)
            for h in range(NH):
                sp.wait_ge(s_stc, h + 1)
                sp.dma_start(o["C_s"][:, h], csb[:]).then_inc(s_out, 16)
                if h + 1 < NH:
                    sp.wait_ge(s_out, 16 * (3 + h))
                    sp.dma_start(csb[:], a["C0"][:, h + 1]).then_inc(s_c0, 16)
            sp.dma_start(o["C_p"], cst[:]).then_inc(s_out, 16)
            sp.dma_start(o["n_p"], npo[:]).then_inc(s_out, 16)
            sp.dma_start(o["n_s"], nso[:]).then_inc(s_out, 16)
            sp.dma_start(o["m"], mout).then_inc(s_out, 16)
            sp.dma_start(keys[:], a["keys"]).then_inc(s_key, 16)
            for n in range(NMOD + NIN + NOUT, NW):
                load(n)

            def table(n, j, wait=True):
                if wait:
                    sp.wait_ge(s_tlo, n - RAW + 1)
                sp.dma_start(tab[:, j], a["tab"][bass.ds(n, 1)].rearrange("a p (k e) -> p (a k) e", k=KT)).then_inc(s_tab[j], 16)

            def gelu_back(c, j, wait=True):
                if wait:
                    sp.wait_ge(s_a32, c - 3)
                sp.dma_start(gin[:, j], ga_dram[bass.ds(c, 1)].rearrange("a p t -> p (a t)")).then_inc(s_gin[j], 16)

            def gates_back(q, slot, wait=True):
                if wait:
                    sp.wait_ge(s_a32, 4 * q - 4)
                sp.dma_start(gt[:, slot], gt_dram[bass.ds(q, 1)].rearrange("a p b (c t) -> p (a b) c t", c=4)).then_inc(s_gt[slot], 16)

            sp.wait_ge(s_out, 160)
            for j in range(RAW):
                table(j, j, wait=False)
            with sp.Fori(1, NCH // 4) as i:
                for j in range(4):
                    table(4 * i + j, j)
            sp.wait_ge(s_gst2, 16 * (NTB + 1))
            for s in s_gas:
                sp.wait_ge(s, 16 * (1 + 60))
            gates_back(0, 0, wait=False)
            for j in range(4):
                gelu_back(j, j, wait=False)
            gates_back(1, 1, wait=False)
            for j in range(4):
                table(NCH + j, j)
                gelu_back(4 + j, j)
            for j in range(4):
                gelu_back(8 + j, j)
            gates_back(2, 0)
            for s in s_gas:
                sp.wait_ge(s, 16 * (1 + 64))
            with sp.Fori(0, 14) as i2:
                for p in range(2):
                    for j in range(4):
                        table(8 * i2 + (4 * p + j + NCH + 4), j)
                        gelu_back(8 * i2 + (4 * p + j + 12), j)
                    gates_back(2 * i2 + (p + 3), 1 - p)
            for n in range(NCH + 4 + 112, NT):
                table(n, n % 4)
                if n - NCH + 8 < NCH:
                    gelu_back(n - NCH + 8, n % 4)
                if n == NCH + 4 + 115:
                    gates_back(31, 1)
            for k in range(KT):
                sp.wait_ge(s_yo, k + 1)
                sp.dma_start(o["y"][:, k], acc[:, k]).then_inc(s_out, 16)
            sp.wait_ge(s_out, 16 * (10 + KT))

        @block.gpsimd
        def _(pool):
            link = linker(pool, s_pch)
            pool.memset(ident[:], 0.0)
            pool.memset(cmask[:], 1.0)
            pool.memset(smask[:], 1.0)
            pool.memset(bmask[:], 1.0)
            pool.iota(iota[:], [[1, P]], base=0, channel_multiplier=0, allow_small_or_imprecise_dtypes=True)
            link(pool.memset(sel[:], 0.0))
            pool.affine_select(out=ident[:], in_=ident[:], compare_op=ALU.not_equal, fill=1.0, base=0,
                               pattern=[[-1, P]], channel_multiplier=1)
            pool.affine_select(out=sel[:], in_=sel[:], compare_op=ALU.not_equal, fill=1.0, base=0,
                               pattern=[[-1, NH], [0, P]], channel_multiplier=1)
            pool.affine_select(out=cmask[:], in_=cmask[:], compare_op=ALU.is_ge, fill=0.0, base=0,
                               pattern=[[1, P]], channel_multiplier=-1)
            link(pool.affine_select(out=bmask[:], in_=bmask[:], compare_op=ALU.is_ge, fill=0.0, base=0,
                                    pattern=[[-NL, NB]], channel_multiplier=1))
            pool.affine_select(out=bmask[:], in_=bmask[:], compare_op=ALU.is_ge, fill=0.0, base=NL - 1,
                               pattern=[[NL, NB]], channel_multiplier=-1)
            link(pool.affine_select(out=smask[:], in_=smask[:], compare_op=ALU.is_ge, fill=0.0, base=0,
                                    pattern=[[-NL, NB], [0, NL]], channel_multiplier=1))
            pool.affine_select(out=smask[:], in_=smask[:], compare_op=ALU.is_ge, fill=0.0, base=0,
                               pattern=[[1, TS]], channel_multiplier=-1).then_inc(s_const, 1)
            for g in range(NIN + NOUT + NPQ):
                n = NMOD + g
                if g == NIN:
                    pool.wait_ge(s_out, 160)
                    pool.wait_ge(s_y, KT)
                pool.wait_ge(s_whi, g + 1)
                if g >= 2:
                    pool.wait_ge(s_wfree, g - 1)
                pool.tensor_tensor(wLo[:, g % 2], raw[:, n % RAW], wHi[:, g % 2].bitcast(F32),
                                   ALU.subtract).then_inc(s_wlo, 1)
                pool.wait_ge(s_wlo, g + 1)
                pool.sem_inc(s_rawfree[n % RAW], 1)

            def lo_part(n, j):
                pool.wait_ge(s_thi, n + 1)
                pool.tensor_tensor(tLo[:, j % 2], tab[:, j], tHi[:, j % 2].bitcast(F32), ALU.subtract).then_inc(s_tlo, 1)

            lo_part(0, 0)
            lo_part(1, 1)
            with pool.Fori(0, NCH // 4) as i:
                for j in range(4):
                    lo_part(4 * i + (j + 2), (j + 2) % 4)
            with pool.Fori(NCH // 4, NT // 4 - 1) as i:
                for j in range(4):
                    lo_part(4 * i + (j + 2), (j + 2) % 4)
            for n in range(NT - 2, NT):
                lo_part(n, n % 4)

        @block.tensor
        def _(pe):
            mm = nc.tensor.matmul

            def square_sum(r):
                for k in range(KT):
                    pe.wait_ge(s_sq, KT * r + k + 1)
                    for h in range(2):
                        last = mm(ps[:, 4 + h, 0:HF], ones[:], sq[:, k % 2, h * HF:(h + 1) * HF],
                                  start=(k == 0), stop=(k == KT - 1))
                    last.then_inc(s_squsd, 1)
                last_wait = KT * (r + 1)
                pe.wait_ge(s_squsd, last_wait)
                pe.sem_inc(s_nrm, 1)

            def project(g0, ng, one=False):
                def granule(g, slot, units, n, first_wait):
                    pe.wait_ge(s_whi, g + 1)
                    pe.wait_ge(s_wlo, g + 1)
                    for u in range(units):
                        if first_wait:
                            pe.wait_ge(s_ev, n + u)
                        s = 2 * ((1 + u) % 2) if units == 2 else 0
                        for k in range(KT):
                            hi = wHi[:, slot, k, u * P:(u + 1) * P]
                            lo = wLo[:, slot, k, u * P:(u + 1) * P]
                            for w, x, first, end in ((lo, hHi, k == 0, False), (hi, hHi, False, False),
                                                     (hi, hLo, False, k == KT - 1)):
                                for h in range(2):
                                    last = mm(ps[:, s + h, 0:HF], w, x[:, k, h * HF:(h + 1) * HF],
                                              start=first, stop=end)
                        last.then_inc(s_pj, 1)
                    pe.wait_ge(s_pj, n + units)
                    pe.sem_inc(s_wfree, 1)

                if one:
                    granule(g0, 0, 1, 0, False)
                else:
                    with pe.Fori(0, ng // 2) as i:
                        for q in range(2):
                            granule(2 * i + (g0 + q), (g0 + q) % 2, 2, 4 * i + (2 * (g0 + q) - 1), True)

            pe.sem_inc(s_ohfree, 2)
            pe.wait_ge(s_const, 2)
            square_sum(0)
            pe.wait_ge(s_silu, 1)
            for n in range(NMOD):
                pe.wait_ge(s_raw[n % RAW], 16 * (n // RAW + 1))
                for u in range(2):
                    c = (2 * n + u) * NSEQ
                    for k in range(KT):
                        last = mm(ps[:, 7, c:c + NSEQ], raw[:, n % RAW, k, u * P:(u + 1) * P], cT[:, k, :],
                                  start=(k == 0), stop=(k == KT - 1))
                last.then_inc(s_modp, 1)
                pe.wait_ge(s_modp, n + 1)
                pe.sem_inc(s_rawfree[n % RAW], 1)
            pe.wait_ge(s_hhi, KT)
            pe.wait_ge(s_hlo, KT)
            project(0, 1, one=True)
            project(1, NIN - 1)

            pe.wait_ge(s_rows, 1)
            pe.wait_ge(s_rowx, 1)
            for h in range(NH):
                if h:
                    pe.wait_ge(s_bce, 3 * h)
                for r, src in enumerate((row_m, row_t)):
                    for i in range(2):
                        last = mm(ps[:, 4 + 2 * r + i, 0:HF], sel[:, h, :], src[:, i * HF:(i + 1) * HF],
                                  start=True, stop=True)
                    last.then_inc(s_bc, 1)
                pe.wait_ge(s_bce, 3 * h + 1)
                mm(ps[:, 4, 0:TS], sel[:, h, :], wi, start=True, stop=True)
                mm(ps[:, 4, TS:TS + NB], sel[:, h, :], wold, start=True, stop=True).then_inc(s_bc, 1)
            pe.wait_ge(s_ev, 2 * NIN - 1 + 1)
            for w, src in enumerate((row_r, row_li)):
                for i in range(NH + 1):
                    n = P if i < NH else TS
                    c = (w * (NH + 1) + i) * NH
                    last = nc.tensor.transpose(ps[0:n, 0, c:c + NH], src[0:NH, i * P:i * P + n], ident[0:NH, 0:NH])
            last.then_inc(s_col, 1)

            for h in range(NH):
                if h == 0:
                    pe.wait_ge(s_colc, 1)
                else:
                    pe.wait_ge(s_stc, h)
                    pe.wait_ge(s_hm, h)
                for i in range(NH):
                    nc.tensor.transpose(ps[:, 0, i * P:(i + 1) * P], zk[:, h, i * P:(i + 1) * P], ident[:])
                    nc.tensor.transpose(ps[:, 1, i * P:(i + 1) * P], zv[:, h, i * P:(i + 1) * P], ident[:])
                nc.tensor.transpose(ps[0:TS, 2, 0:P], zk[:, h, TP:T], ident[:])
                nc.tensor.transpose(ps[0:TS, 2, P:2 * P], zv[:, h, TP:T], ident[:]).then_inc(s_tok, 1)
                if h == 0:
                    pe.wait_ge(s_bce, 3 * NH)
                for i, (b, c) in enumerate(((3, 0), (4, 0), (5, 0), (4, 384))):
                    mm(ps[:, b, c:c + TP - i * P], zk[:, h, i * P:(i + 1) * P], zq[:, h, i * P:TP], start=True, stop=True)
                mm(ps[0:TS, 5, 256:256 + TS], zk[:, h, TP:T], zq[:, h, TP:T], start=True, stop=True).then_inc(s_sp, 1)
                pe.wait_ge(s_tokc, h + 1)
                pe.wait_ge(s_p, h + 1)
                for bank, lhs in ((6, vtok), (7, None)):
                    for i in range(NH):
                        mm(ps[:, bank, i * P:TP], vtok[:, i, :] if lhs else ones[:],
                           er[:, EOFF[i]:EOFF[i] + TP - i * P], start=(i == 0), stop=(i == NH - 1))
                pe.wait_ge(s_c0, 16 * (h + 1))
                pe.wait_ge(s_qn, 1)
                for b in range(NB):
                    mm(ps[:, 2, 256 + b * NL:256 + (b + 1) * NL], csb[:, b, :], qwi[:, h, b * NL:(b + 1) * NL],
                       start=(b == 0), stop=False)
                mm(ps[:, 2, 256:256 + TS], vtok[0:TS, NH, :], er[0:TS, EW:EW + TS], start=False, stop=True)
                mm(ps[:, 2, 288:288 + TS], ones[:], qn[:, h, :], start=True, stop=False)
                mm(ps[:, 2, 288:288 + TS], ones[0:TS, :], er[0:TS, EW:EW + TS], start=False, stop=True).then_inc(s_num, 1)
                pe.wait_ge(s_vw, h + 1)
                for i in range(NH):
                    mm(ps[:, 0, 0:DH], ktok[:, i, :], vw[:, i, :], start=(i == 0), stop=(i == NH - 1))
                for i in range(NH):
                    mm(ps[:, 0, DH:DH + 1], ktok[:, i, :], rcol[:, 1, i, h:h + 1], start=(i == 0), stop=(i == NH - 1))
                mm(ps[:, 0, 136:136 + NB], ktok[0:TS, NH, :], wsm[:], start=True, stop=True)
                for i, b in enumerate((1, 3)):
                    last = mm(ps[:, b, :], ktok[0:TS, NH, :], vsm[:, 4 * i:4 * i + 4, :], start=True, stop=True)
                last.then_inc(s_stp, 1)

            pe.wait_ge(s_stc, NH)
            pe.wait_ge(s_hm, NH)
            for i in range(CT + NH):
                pe.wait_ge(s_gsq, i + 1)
                if i >= 2:
                    pe.wait_ge(s_grms, i - 1)
                for h in range(2):
                    last = mm(ps[:, 2 * (i % 2) + h, 0:HF], blk[:] if i < CT else ones[:], sq[:, i % 2, h * HF:(h + 1) * HF],
                              start=True, stop=True)
                last.then_inc(s_gst, 1)
            pe.wait_ge(s_grms, CT + NH)
            pe.wait_ge(s_hhi, 2 * KT)
            pe.wait_ge(s_hlo, 2 * KT)
            project(NIN, NOUT)
            square_sum(1)
            pe.wait_ge(s_hhi, 3 * KT)
            pe.wait_ge(s_hlo, 3 * KT)
            project(NIN + NOUT, NPQ)
            pe.wait_ge(s_key, 16)
            pe.wait_ge(s_ev, 1 + 2 * (NIN + NOUT + NPQ) - 1)
            for i, t0 in enumerate(STILES):
                if i >= 2:
                    pe.wait_ge(s_sc, i - 1)
                for j in range(HP):
                    last = mm(ps[:, 4 * (i % 2) + j // 4, (j % 4) * NKEY:(j % 4 + 1) * NKEY], qT[:, j, t0:t0 + P],
                              keys[:, j, :], start=True, stop=True)
                last.then_inc(s_scp, 1)
            pe.wait_ge(s_sc, NST)

            def product(n, j, hi_in, lo_in):
                pe.wait_ge(s_thi, n + 1)
                pe.wait_ge(s_tlo, n + 1)
                pe.wait_ge(s_gfree, n + 1)
                s = 2 * (j % 2)
                for k in range(KT):
                    hi, lo = tHi[:, j % 2, k, :], tLo[:, j % 2, k, :]
                    for w, x, first, end in ((lo, hi_in, k == 0, False), (hi, hi_in, False, False),
                                             (hi, lo_in, False, k == KT - 1)):
                        for h in range(2):
                            last = mm(ps[:, s + h, 0:HF], w, x[:, k, h * HF:(h + 1) * HF], start=first, stop=end)
                last.then_inc(s_prod, 1)

            def gate_product(st, j):
                pe.wait_ge(s_oh, st + 1)
                pe.wait_ge(s_gevfree, st + 1)
                for t in range(STEP_TOK):
                    out = ps[:, 4 + 2 * (j % 2) + t // 4, (t % 4) * P:(t % 4 + 1) * P]
                    mm(out, oh2[:, j % 2, t, :], w1l[:, j % 2, t, :], start=True, stop=False)
                    last = mm(out, oh2[:, j % 2, t, :], w1h[:, j % 2, t, :], start=False, stop=True)
                last.then_inc(s_gmm, 1)
                pe.wait_ge(s_gmm, st + 1)
                pe.sem_inc(s_ohfree, 1)

            with pe.Fori(0, Q_GATE) as i:
                for j in range(4):
                    product(4 * i + j, j, hHi, hLo)
            pe.wait_ge(s_best, 1)
            for q in range(3):
                for i in range(NST):
                    out = ps[:, 4 + q, i * P:(i + 1) * P] if i < 4 else ps[:, 7, q * P:(q + 1) * P]
                    last = nc.tensor.transpose(out, best[:, q, i, :], ident[:])
            last.then_inc(s_bestT, 1)
            pe.wait_ge(s_idx, 1)
            with pe.Fori(0, NTB) as i:
                for j in range(4):
                    product(4 * i + (4 * Q_GATE + j), j, hHi, hLo)
                    gate_product(4 * i + j, j)
            for n in range(4 * (Q_GATE + NTB), NCH):
                product(n, n % 4, hHi, hLo)
            with pe.Fori(0, NCH // GRP // 2) as i:
                for g in range(2):
                    pe.wait_ge(s_alo, 2 * GRP * i + GRP * (g + 1))
                    for j in range(KT):
                        product(2 * GRP * i + (NCH + GRP * g + j), j, actHi[g], actLo[g])
            square_sum(2)

        @block.scalar
        def _(act):
            link = linker(act, s_ach)
            f = nc.scalar.activation

            def squares(r):
                for k in range(KT):
                    if r:
                        act.wait_ge(s_x1, KT * (r - 1) + k + 1)
                    if k >= 2 or r:
                        act.wait_ge(s_squsd, KT * r + k - 1)
                    f(sq[:, k % 2], xT[:, k], ACT.Square).then_inc(s_sq, 1)

            def rms(r):
                act.wait_ge(s_nrm, r + 1)
                f(rs[:].rearrange("p (h t) -> p h t", h=2), ps[:, 4:6, 0:HF], ACT.Sqrt, bias=eps[:], scale=1.0 / D).then_inc(s_rms, 1)

            def hi_part(g):
                n = NMOD + g
                act.wait_ge(s_raw[n % RAW], 16 * (n // RAW + 1))
                if g >= 2:
                    act.wait_ge(s_wfree, g - 1)
                nc.scalar.copy(wHi[:, g % 2], raw[:, n % RAW]).then_inc(s_whi, 1)

            def make_h(r):
                act.wait_ge(s_mods, 1)
                for k in range(KT):
                    act.wait_ge(s_xn, KT * r + k + 1)
                    f(hf[:, k, 0:TP], hf[:, k, 0:TP], ACT.Identity, bias=mod[:, 3 * r * KT + k, 0:1],
                      scale=amod[:, r, k, 0:1]).then_inc(s_aff, 1)
                act.wait_ge(s_smp, r + 1)
                for k in range(KT):
                    act.wait_ge(s_aff, KT * r + k + 1)
                    nc.scalar.copy(hHi[:, k], hf[:, k]).then_inc(s_hhi, 1)

            def evacuate(n, out, func=ACT.Identity, scale=1.0):
                act.wait_ge(s_pj, n + 1)
                f(out.rearrange("p (h t) -> p h t", h=2), pair(n), func, scale=scale).then_inc(s_ev, 1)

            act.sem_inc(s_ev, 1)
            act.sem_inc(s_gfree, 2)
            act.sem_inc(s_gevfree, 2)
            act.wait_ge(s_vec, 48)
            f(cT[:], cT[:], ACT.Silu).then_inc(s_silu, 1)
            act.wait_ge(s_x, 16)
            squares(0)
            act.wait_ge(s_const, 2)
            rms(0)
            hi_part(0)
            hi_part(1)
            make_h(0)

            dest = {0: xc, 1: bg, 3: zq, 4: zk, 5: zv, 6: zo}
            for g in range(NIN):
                if g == 0:
                    evacuate(0, row_li[:])
                else:
                    for u in range(2):
                        n = 2 * g - 1 + u
                        kind, i = (n - 1) // 4, (n - 1) % 4
                        if kind == 2:
                            act.wait_ge(s_pj, n + 1)
                            s = 2 * (n % 2)
                            f(up[:, i, 2:2 + HF], ps[:, s, 0:HF], ACT.Identity)
                            f(up[:, i, 2 + HF:2 + TP], ps[:, s + 1, 0:TP - HF], ACT.Identity)
                            f(us[:, i, :, 2:2 + NL], ps[:, s + 1, TP - HF:HF].rearrange("p (b l) -> p b l", l=NL),
                              ACT.Identity).then_inc(s_ev, 1)
                        elif kind == 6:
                            evacuate(n, zo[:, i], ACT.Sigmoid)
                        else:
                            evacuate(n, dest[kind][:, i], scale=DH ** -0.5 if kind == 4 else 1.0)
                if g + 2 < NIN:
                    hi_part(g + 2)
                if g == 3:
                    act.wait_ge(s_rowa, 1)
                    link(f(row_t[:], row_t[:], ACT.Exp))
                    f(row_t[:], row_t[:], ACT.Ln, bias=1.0).then_inc(s_rowe, 1)
                if g == 5:
                    act.wait_ge(s_rows, 1)
                    f(row_t[:], row_t[:], ACT.Exp, scale=-1.0)
                    f(row_li[0:NH], row_li[0:NH], ACT.Exp)
                    f(small[:, 10:50], small[:, 10:50], ACT.Exp).then_inc(s_rowx, 1)

            act.wait_ge(s_conv, 1)
            act.wait_ge(s_out, 32)
            for h in range(NH):
                act.wait_ge(s_bc, 3 * h + 1)
                f(mb[:, h].rearrange("p (h t) -> p h t", h=2), ps[:, 4:6, 0:HF], ACT.Identity).then_inc(s_bce, 1)
                act.wait_ge(s_bc, 3 * h + 2)
                f(emb[:, h].rearrange("p (h t) -> p h t", h=2), ps[:, 6:8, 0:HF], ACT.Identity).then_inc(s_bce, 1)
                act.wait_ge(s_bc, 3 * h + 3)
                f(wib[:, h], ps[:, 4, 0:TS + NB], ACT.Identity).then_inc(s_bce, 1)
            act.wait_ge(s_col, 1)
            f(rcol[:, :, 0:NH, :], ps[:, 0, 0:40].rearrange("p (w i h) -> p w i h", w=2, h=NH)[:, :, 0:NH, :], ACT.Identity)
            f(rcol[0:TS, :, NH, :], ps[0:TS, 0, 0:40].rearrange("p (w i h) -> p w i h", w=2, h=NH)[:, :, NH, :],
              ACT.Identity).then_inc(s_colc, 1)
            for h in range(NH):
                act.wait_ge(s_tok, h + 1)
                if h:
                    act.wait_ge(s_stp, h)
                f(ktok[:, 0:NH, :], ps[:, 0, :].rearrange("p (i d) -> p i d", i=NH), ACT.Identity)
                f(vtok[:, 0:NH, :], ps[:, 1, :].rearrange("p (i d) -> p i d", i=NH), ACT.Identity)
                f(ktok[0:TS, NH, :], ps[0:TS, 2, 0:P], ACT.Identity)
                f(vtok[0:TS, NH, :], ps[0:TS, 2, P:2 * P], ACT.Identity).then_inc(s_tokc, 1)
                act.wait_ge(s_er, h + 1)
                f(er[:, 0:EW], er[:, 0:EW], ACT.Exp, scale=-1.0)
                f(er[0:TS, EW:EW + TS], er[0:TS, EW:EW + TS], ACT.Exp, scale=-1.0).then_inc(s_ex, 1)
            for i in range(CT + NH + 1):
                if i < CT + NH:
                    if i == CT:
                        act.wait_ge(s_hm, NH)
                    if i >= 2:
                        act.wait_ge(s_gst, i - 1)
                    f(sq[:, i % 2], (xc if i < CT else zq)[:, i % 4], ACT.Square).then_inc(s_gsq, 1)
                if i >= 1:
                    j = i - 1
                    act.wait_ge(s_gst, j + 1)
                    if j >= 2:
                        act.wait_ge(s_y, j - 1)
                    f(gr[:, j % 2].rearrange("p (h t) -> p h t", h=2), pair(j), ACT.Sqrt, bias=eps[:],
                      scale=1.0 / 64 if j < CT else 1.0 / DH).then_inc(s_grms, 1)
            for k in range(KT):
                act.wait_ge(s_y, k + 1)
                nc.scalar.copy(hHi[:, k], (xc if k < CT else zq)[:, k % 4]).then_inc(s_hhi, 1)
            act.wait_ge(s_out, 160)
            act.wait_ge(s_y, KT)
            hi_part(NIN)
            hi_part(NIN + 1)
            for g in range(NIN, NIN + NOUT):
                for u in range(2):
                    n = 2 * g - 1 + u
                    evacuate(n, hf[:, 2 * (g - NIN) + u])
                if g + 2 < NIN + NOUT:
                    hi_part(g + 2)
            hi_part(NIN + NOUT)
            hi_part(NIN + NOUT + 1)
            squares(1)
            rms(1)
            make_h(1)
            for g in range(NIN + NOUT, NIN + NOUT + NPQ):
                for u in range(2):
                    evacuate(2 * g - 1 + u, qT[:, 2 * (g - NIN - NOUT) + u])
                if g + 2 < NIN + NOUT + NPQ:
                    hi_part(g + 2)
            for i in range(NST):
                act.wait_ge(s_scp, i + 1)
                f(sc[:, i].rearrange("p (b j) n -> p b (j n)", b=4), ps[:, 4 * (i % 2):4 * (i % 2) + 4, :], ACT.Identity).then_inc(s_sc, 1)

            def a_step(i, j):
                act.wait_ge(s_prod, 4 * i + (j + 1))
                act.wait_ge(s_gas[j % 2], 32 * i + 16 * (j // 2 + 1))
                f(ga[:, j % 2].rearrange("p (h t) -> p h t", h=2), pair(j), ACT.Gelu_apprx_tanh).then_inc(s_gelu, 1)
                act.wait_ge(s_gelu, 4 * i + (j + 1))
                act.sem_inc(s_gfree, 1)
                act.wait_ge(s_tab[(j + 2) % 4], 16 * i + 16 * ((j + 2) // 4 + 1))
                nc.scalar.copy(tHi[:, j % 2], tab[:, (j + 2) % 4]).then_inc(s_thi, 1)
                c = 4 * i + j
                act.dma_start(ga_dram[c] if isinstance(c, int) else ga_dram[bass.ds(c, 1)].rearrange("a p t -> p (a t)"),
                              ga[:, j % 2]).then_inc(s_gas[j % 2], 16)

            act.sem_inc(s_gas[0], 16)
            act.sem_inc(s_gas[1], 16)
            for n in range(2):
                act.wait_ge(s_tab[n], 16)
                nc.scalar.copy(tHi[:, n], tab[:, n]).then_inc(s_thi, 1)
            with act.Fori(0, Q_EXP) as i:
                for j in range(4):
                    a_step(i, j)
            act.wait_ge(s_top, 1)
            f(best[:, 0], best[:, 0], ACT.Exp).then_inc(s_gexp, 1)
            for j in range(4):
                a_step(Q_EXP, j)
            act.wait_ge(s_idx, 1)
            act.sem_inc(s_gst2, 16)
            with act.Fori(0, NTB) as i:
                for j in range(4):
                    a_step(i + Q_GATE, j)
                    act.wait_ge(s_gmm, 4 * i + (j + 1))
                    f(stage[:, bass.ds(i % 2, 1), :, STEP_TOK * j:STEP_TOK * (j + 1)].rearrange("p s c t -> p t (s c)"),
                      ps[:, 4 + 2 * (j % 2):6 + 2 * (j % 2), :].rearrange("p b (t c) -> p (b t) c", c=P), ACT.Identity).then_inc(s_gev, 1)
                    act.wait_ge(s_gev, 4 * i + (j + 1))
                    act.sem_inc(s_gevfree, 1)
                act.wait_ge(s_gst2, 16 * i + 16)
                act.dma_start(gt_dram[:, :, bass.ds(i, 1), :].rearrange("q p a (c t) -> p (a q) c t", c=4),
                              stage[:, bass.ds(i % 2, 1)].rearrange("p s (q c) t -> p (s q) c t", c=4)).then_inc(s_gst2, 16)

            def act_hi(c, g, k):
                act.wait_ge(s_a32, c + 1)
                nc.scalar.copy(actHi[g][:, k], a32[:, k % 2]).then_inc(s_ahi, 1)

            for i in range(Q_GATE + NTB, NCH // 4):
                for j in range(4):
                    a_step(i, j)
                    act_hi(2 * j, 0, 2 * j)
                    act_hi(2 * j + 1, 0, 2 * j + 1)

            def out_step(i, s, prep=True, split=True):
                if prep:
                    act_hi(16 * i + (s + GRP), (s // GRP + 1) % 2, s % GRP)
                if split:
                    act.wait_ge(s_prod, 16 * i + (NCH + s + 1))
                    act.wait_ge(s_tab[(s + 2) % 4], 64 * i + 16 * (NCH // 4 + (s + 2) // 4 + 1))
                    nc.scalar.copy(tHi[:, s % 2], tab[:, (s + 2) % 4]).then_inc(s_thi, 1)

            with act.Fori(0, NCH // 16 - 1) as i:
                for s in range(16):
                    out_step(i, s)
            for s in range(16):
                out_step(NCH // 16 - 1, s, prep=s < 8, split=s < 14)
            squares(2)
            rms(2)

        @block.vector
        def _(v):
            link = linker(v, s_dch)
            tt, tsc, stt = nc.vector.tensor_tensor, nc.vector.tensor_scalar, nc.vector.scalar_tensor_tensor

            def make_h(r):
                v.wait_ge(s_rms, r + 1)
                link(nc.vector.reciprocal(rs[:], rs[:]))
                for k in range(KT):
                    tt(hf[:, k], xT[:, k], rs[:], ALU.mult).then_inc(s_xn, 1)
                if r == 0:
                    v.wait_ge(s_modp, NMOD)
                    link(tt(mod[:], ps[:, 7, 0:6 * KT * NSEQ].rearrange("p (k s) -> p k s", s=NSEQ), over(span("b_mod"), NSEQ), ALU.add))
                    stt(amod[:, 0], mod[:, KT:2 * KT], 1.0, over(span("g_mix"), NSEQ), ALU.add, ALU.mult)
                    link(stt(amod[:, 1], mod[:, 4 * KT:5 * KT], 1.0, over(span("g_ffn"), NSEQ), ALU.add, ALU.mult))
                    v.sem_inc(s_mods, 1)
                v.wait_ge(s_xn, KT * (r + 1))
                link(tt(smp(hf[:, :, TP:T]), smp(hf[:, :, TP:T]), over(amod[:, r, :, 1:NSEQ], NL), ALU.mult))
                tt(smp(hf[:, :, TP:T]), smp(hf[:, :, TP:T]), over(mod[:, 3 * r * KT:(3 * r + 1) * KT, 1:NSEQ], NL),
                   ALU.add).then_inc(s_smp, 1)
                for k in range(KT):
                    v.wait_ge(s_hhi, (2 * KT if r else 0) + k + 1)
                    tt(hLo[:, k], hf[:, k], hHi[:, k].bitcast(F32), ALU.subtract).then_inc(s_hlo, 1)

            nc.vector.memset(ones[:], 1.0)
            nc.vector.memset(eps[:], 1e-6)
            nc.vector.memset(row_z[:], 1.0)
            link(nc.vector.memset(blk[:], 0.0))
            nc.vector.memset(blk[0:64, 0:64], 1.0)
            nc.vector.memset(row_z[:, TP:T].rearrange("p (b l) -> p b l", l=NL)[:, :, 0:1], 0.0)
            nc.vector.memset(blk[64:P, 64:P], 1.0).then_inc(s_const, 1)
            v.wait_ge(s_x, 16)
            v.wait_ge(s_vec, 48)
            make_h(0)

            v.wait_ge(s_ev, 1 + 1)
            link(nc.vector.tensor_copy(row_lf[:], row_li[32:32 + NH, :]))
            tsc(row_li[0:NH], row_li[0:NH], gbias[:, 0:1], None, ALU.add)
            link(tsc(row_lf[:], row_lf[:], gbias[:, 1:2], None, ALU.add))
            stt(row_t[:], row_lf[:], -1.0, row_lf[:], ALU.mult, ALU.min).then_inc(s_rowa, 1)
            v.wait_ge(s_rowe, 1)
            link(stt(row_lf[:], row_lf[:], 0.0, row_t[:], ALU.min, ALU.subtract))
            link(nc.vector.tensor_tensor_scan(row_b[:], row_z[:], row_lf[:], 0.0, ALU.mult, ALU.add))
            tsc(row_z[:], row_z[:], 1.0, BIG, ALU.subtract, ALU.mult)
            link(tt(row_r[:], row_li[0:NH], row_b[:], ALU.subtract))
            link(nc.vector.tensor_copy(row_t[:], row_r[:]))
            tsc(row_t[:, 0:1], row_r[:, 0:1], 0.0, None, ALU.max)
            first = row_t[:, TP:T].rearrange("p (b l) -> p b l", l=NL)[:, :, 0]
            link(tt(first, first, m0, ALU.max))
            link(nc.vector.tensor_tensor_scan(row_m[:], row_z[:], row_t[:], 0.0, ALU.add, ALU.max))
            ms = row_m[:, TP:T].rearrange("p (b l) -> p b l", l=NL)
            ml = ms[:, :, NL - 1]
            rsm = row_r[:, TP:T].rearrange("p (b l) -> p b l", l=NL)
            link(tt(row_t[:], row_b[:], row_m[:], ALU.add))
            nc.vector.tensor_copy(mout[:, 0:1], row_t[:, TP - 1:TP])
            nc.vector.tensor_copy(mout[:, 1:NSEQ], row_t[:, TP:T].rearrange("p (b l) -> p b l", l=NL)[:, :, NL - 1])
            tsc(row_li[0:NH, 0:TP], row_r[:, 0:TP], row_m[:, TP - 1:TP], None, ALU.subtract)
            tt(row_li[0:NH, TP:T].rearrange("p (b l) -> p b l", l=NL), rsm, over(ml, NL), ALU.subtract)
            tt(wold, m0, ml, ALU.subtract)
            tt(wi.rearrange("p (b l) -> p b l", l=NL), over(m0, NL), ms, ALU.subtract).then_inc(s_rows, 1)

            v.wait_ge(s_ev, 13 + 1)
            v.wait_ge(s_state, 16)
            nc.vector.memset(up[:, :, 0:2], 0.0)
            tt(up[:, :, 2:2 + TP], up[:, :, 2:2 + TP], xc[:, :, 0:TP], ALU.mult)
            link(tt(us[:, :, :, 2:2 + NL], us[:, :, :, 2:2 + NL], smp(xc[:, :, TP:T]), ALU.mult))
            v.sem_inc(s_convout, 1)
            for j in range(3):
                for i in range(CT):
                    w = col("w_conv", j * CT + i)
                    yp, ys = xc[:, i, 0:TP], xc[:, i, TP:T].rearrange("p (b l) -> p b l", l=NL)
                    if j == 0:
                        tsc(yp, up[:, i, j:j + TP], w, None, ALU.mult)
                        last = tsc(ys, us[:, i, :, j:j + NL], w, None, ALU.mult)
                    else:
                        stt(yp, up[:, i, j:j + TP], w, yp, ALU.mult, ALU.add)
                        last = stt(ys, us[:, i, :, j:j + NL], w, ys, ALU.mult, ALU.add)
                link(last)
            tt(xc[:], xc[:], bg[:], ALU.mult).then_inc(s_conv, 1)

            v.wait_ge(s_bce, 3 * NH)
            v.wait_ge(s_n0, 16)
            v.wait_ge(s_colc, 1)
            link(tt(qwi[:], zq[:, :, TP:T], wib[:, :, 0:TS], ALU.mult))
            tt(smp(qn[:]), smp(qwi[:]), over(n0[:], NL), ALU.mult).then_inc(s_qn, 1)
            for h in range(NH):
                if h:
                    v.wait_ge(s_num, h)
                for i in range(NH):
                    tsc(er[:, EOFF[i]:EOFF[i] + TP - i * P], mb[:, h, i * P:TP], rcol[:, 0, i, h:h + 1], 0.0,
                        ALU.subtract, ALU.max)
                tsc(er[0:TS, EW:EW + TS], mb[0:TS, h, TP:T], rcol[0:TS, 0, NH, h:h + 1], 0.0,
                    ALU.subtract, ALU.max).then_inc(s_er, 1)
                v.wait_ge(s_tokc, h + 1)
                if h:
                    v.wait_ge(s_stp, h)
                tt(vw[:], vtok[:, 0:NH, :], over(rcol[:, 1, 0:NH, h], DH), ALU.mult)
                tsc(wsm[:], bmask[:], rcol[0:TS, 1, NH, h:h + 1], None, ALU.mult)
                link(tsc(vsw[:], vtok[0:TS, NH, :], rcol[0:TS, 1, NH, h:h + 1], None, ALU.mult))
                tt(vsm[:], vsw[:].unsqueeze(1).broadcast_to([TS, NB, DH]), over(bmask[:], DH), ALU.mult).then_inc(s_vw, 1)
                v.wait_ge(s_ex, h + 1)
                v.wait_ge(s_sp, h + 1)
                for i in range(NH):
                    c = EOFF[i]
                    last = tt(er[:, c:c + P], er[:, c:c + P], cmask[:], ALU.mult)
                link(tt(er[0:TS, EW:EW + TS], er[0:TS, EW:EW + TS], smask[:], ALU.mult))
                for i, (b, c) in enumerate(((3, 0), (4, 0), (5, 0), (4, 384))):
                    e = er[:, EOFF[i]:EOFF[i] + TP - i * P]
                    tt(e, e, ps[:, b, c:c + TP - i * P], ALU.mult)
                tt(er[0:TS, EW:EW + TS], er[0:TS, EW:EW + TS], ps[0:TS, 5, 256:256 + TS], ALU.mult).then_inc(s_p, 1)
                v.wait_ge(s_num, h + 1)
                tt(dn[:, 0:TP], ps[:, 7, :], emb[:, h, 0:TP], ALU.max)
                link(tt(dn[:, TP:T], ps[:, 2, 288:288 + TS], emb[:, h, TP:T], ALU.max))
                stt(dn[:, 0:TP], ps[:, 7, :], -1.0, dn[:, 0:TP], ALU.mult, ALU.max)
                link(stt(dn[:, TP:T], ps[:, 2, 288:288 + TS], -1.0, dn[:, TP:T], ALU.mult, ALU.max))
                link(nc.vector.reciprocal(dn[:], dn[:]))
                link(tt(dn[:], dn[:], zo[:, h], ALU.mult))
                tt(zq[:, h, 0:TP], ps[:, 6, :], dn[:, 0:TP], ALU.mult)
                tt(zq[:, h, TP:T], ps[:, 2, 256:256 + TS], dn[:, TP:T], ALU.mult).then_inc(s_hm, 1)
                v.wait_ge(s_stp, h + 1)
                nc.vector.tensor_copy(cst[:, h], ps[:, 0, 0:DH])
                nc.vector.tensor_copy(npo[:, h:h + 1], ps[:, 0, DH:DH + 1])
                tt(nso[:, h], n0[:, h], wib[:, h, TS:TS + NB], ALU.mult)
                link(tt(csb[:], csb[:], over(wib[:, h, TS:TS + NB], DH), ALU.mult))
                tt(nso[:, h], nso[:, h], ps[:, 0, 136:136 + NB], ALU.add)
                tt(csb[:, 0:4], csb[:, 0:4], ps[:, 1, :].rearrange("p (b d) -> p b d", b=4), ALU.add)
                tt(csb[:, 4:8], csb[:, 4:8], ps[:, 3, :].rearrange("p (b d) -> p b d", b=4), ALU.add).then_inc(s_stc, 1)

            for i in range(CT + NH):
                v.wait_ge(s_grms, i + 1)
                link(nc.vector.reciprocal(gr[:, i % 2], gr[:, i % 2]))
                y = (xc if i < CT else zq)[:, i % 4]
                stt(y, y, col("g_conv", i) if i < CT else col("g_mlstm", i - CT), gr[:, i % 2],
                    ALU.mult, ALU.mult).then_inc(s_y, 1)
            for k in range(KT):
                v.wait_ge(s_hhi, KT + k + 1)
                tt(hLo[:, k], (xc if k < CT else zq)[:, k % 4], hHi[:, k].bitcast(F32), ALU.subtract).then_inc(s_hlo, 1)
            for k in range(KT):
                v.wait_ge(s_ev, 1 + 2 * NIN - 1 + k + 1)
                xs = xT[:, k, TP:T].rearrange("p (b l) -> p b l", l=NL)
                ms_ = hf[:, k, TP:T].rearrange("p (b l) -> p b l", l=NL)
                stt(xT[:, k, 0:TP], hf[:, k, 0:TP], mod[:, 2 * KT + k, 0:1], xT[:, k, 0:TP], ALU.mult, ALU.add)
                link(tt(ms_, ms_, over(mod[:, 2 * KT + k, 1:NSEQ], NL), ALU.mult))
                tt(xs, xs, ms_, ALU.add).then_inc(s_x1, 1)
            v.wait_ge(s_x1, KT)
            make_h(1)

            CHAIN = 15

            def chain(i, n):
                v.wait_ge(s_tk, CHAIN * i + n)
                v.nop(nofuse=True)

            v.wait_ge(s_scp, NST)
            with v.Fori(0, NST) as i:
                def row(j):
                    return scur[:, j]
                v.wait_ge(s_sc, i + 1)
                nc.vector.tensor_copy(scur[:], sc[:, bass.ds(i, 1)].rearrange("p a j n -> p (a j) n")).then_inc(s_tk, 1)
                chain(i, 1)
                for j in range(HP):
                    last = nc.vector.max(m16[:, j, 0:8], row(j))
                last.then_inc(s_tk, 1)
                chain(i, 2)
                for j in range(HP):
                    nc.vector.max_index(ix[:, j, 0:8], m16[:, j, 0:8], row(j))
                    last = nc.vector.match_replace(row(j), m16[:, j, 0:8], row(j), LOWEST)
                last.then_inc(s_tk, 1)
                chain(i, 3)
                for j in range(HP):
                    last = nc.vector.max(m16[:, j, 8:16], row(j))
                last.then_inc(s_tk, 1)
                chain(i, 4)
                for j in range(HP):
                    last = nc.vector.max_index(ix[:, j, 8:16], m16[:, j, 8:16], row(j))
                last.then_inc(s_tk, 1)
                halves = m16[:].rearrange("p (h two) k -> p h two k", two=2)
                chain(i, 5)
                nc.vector.tensor_copy(ixf[:], ix[:])
                tt(cand[:], over(halves[:, :, 0, :], PK),
                   halves[:, :, 1, :].unsqueeze(2).broadcast_to([P, PH, PK, PK]), ALU.add).then_inc(s_tk, 1)
                chain(i, 6)

                def sums(h):
                    return cand[:, h].rearrange("p a b -> p (a b)")

                def top(h, r):
                    return tcur[:, h, r:r + 8]
                for h in range(PH):
                    last = nc.vector.max(top(h, 0), sums(h))
                last.then_inc(s_tk, 1)
                chain(i, 7)
                for h in range(PH):
                    nc.vector.max_index(pos16[:, h, 0:8], top(h, 0), sums(h))
                    last = nc.vector.match_replace(sums(h), top(h, 0), sums(h), LOWEST)
                last.then_inc(s_tk, 1)
                chain(i, 8)
                for h in range(PH):
                    last = nc.vector.max(top(h, 8), sums(h))
                last.then_inc(s_tk, 1)
                chain(i, 9)
                for h in range(PH):
                    last = nc.vector.max_index(pos16[:, h, 8:16], top(h, 8), sums(h))
                last.then_inc(s_tk, 1)
                chain(i, 10)
                flat = pos16[:].rearrange("p h k -> p (h k)")
                tsc(pab[:, 0], flat, 4, None, ALU.logical_shift_right)
                tsc(pab[:, 1], flat, PK - 1, None, ALU.bitwise_and).then_inc(s_tk, 1)
                tt(best[:, 0, bass.ds(i, 1), :].rearrange("p a (h k) -> p (a h) k", k=PK), tcur[:], over(tcur[:, :, 0], PK),
                   ALU.subtract)
                v.wait_ge(s_tk, CHAIN * i + 11)
                nc.vector.tensor_copy(pabf[:], pab[:]).then_inc(s_tk, 1)
                v.wait_ge(s_tk, CHAIN * i + 12)
                rank = iota[:, 0:PK].unsqueeze(1).broadcast_to([P, PH * PK, PK])
                half = ixf[:].rearrange("p (h two) k -> p h two k", two=2)
                e = (eqa, eqb)
                for w in range(2):
                    last = tt(e[w][:].rearrange("p h k a -> p (h k) a"), rank, over(pabf[:, w], PK), ALU.is_equal)
                last.then_inc(s_tk, 1)
                v.wait_ge(s_tk, CHAIN * i + 13)
                for w in range(2):
                    last = tt(e[w][:], e[w][:], half[:, :, w, :].unsqueeze(2).broadcast_to([P, PH, PK, PK]), ALU.mult)
                last.then_inc(s_tk, 1)
                v.wait_ge(s_tk, CHAIN * i + 14)
                for w in range(2):
                    last = nc.vector.tensor_reduce(best[:, 1 + w, bass.ds(i, 1), :].rearrange("p a n -> p (a n)"),
                                                   e[w][:].rearrange("p h k a -> p (h k) a"), AXX, ALU.add)
                last.then_inc(s_tk, 1)
                v.wait_ge(s_tk, CHAIN * i + 15)
            v.sem_inc(s_top, 1)
            v.wait_ge(s_gexp, 1)
            w_ = best[:, 0].rearrange("p i (h k) -> p (i h) k", k=PK)
            link(nc.vector.tensor_reduce(ssum[:], w_, AXX, ALU.add))
            link(nc.vector.reciprocal(ssum[:], ssum[:]))
            tt(w_, w_, over(ssum[:], PK), ALU.mult).then_inc(s_best, 1)
            v.wait_ge(s_bestT, 1)
            nc.vector.tensor_copy(idxT[:, 2, 0:TP], ps[:, 4, :])
            nc.vector.tensor_copy(idxT[:, 2, TP:T], ps[:, 7, P - TS:P])
            for q in range(2):
                nc.vector.tensor_copy(idxT[:, q, 0:TP], ps[:, 5 + q, :])
                last = nc.vector.tensor_copy(idxT[:, q, TP:T], ps[:, 7, (q + 2) * P - TS:(q + 2) * P])
            link(last)
            link(nc.vector.tensor_copy(gHr[:], idxT[:, 2, :]))
            link(tt(idxT[:, 3], idxT[:, 2], gHr[:].bitcast(F32), ALU.subtract))
            link(nc.vector.tensor_copy(idxT[:, 2], gHr[:].bitcast(F32)))
            v.sem_inc(s_idx, 1)

            with v.Fori(0, NTB) as i:
                for j in range(4):
                    v.wait_ge(s_ohfree, 4 * i + (j + 1))
                    nc.vector.tensor_copy(cb[:, j % 2], idxT[:, :, bass.ds(TB * i + STEP_TOK * j, STEP_TOK)]).then_inc(s_cb, 1)
                    v.wait_ge(s_cb, 4 * i + (j + 1))
                    for t in range(STEP_TOK):
                        c = cb[:, j % 2, :, t:t + 1]
                        tsc(oh2[:, j % 2, t], iota[:], c[:, 1], None, ALU.is_equal)
                        tsc(w1l[:, j % 2, t], iota[:], c[:, 0], c[:, 3], ALU.is_equal, ALU.mult)
                        last = tsc(w1h[:, j % 2, t], iota[:], c[:, 0], c[:, 2], ALU.is_equal, ALU.mult)
                    last.then_inc(s_oh, 1)

            def act_lo(g, k, count):
                v.wait_ge(s_ahi, count)
                tt(actLo[g][:, k], a32[:, k % 2], actHi[g][:, k].bitcast(F32), ALU.subtract).then_inc(s_alo, 1)

            v.wait_ge(s_gmm, 4 * NTB)
            link(nc.vector.memset(acc[:], 0.0))
            for c in range(GRP):
                v.wait_ge(s_gin[c % 4], 16 * (c // 4 + 1))
                v.wait_ge(s_gt[c // 4 % 2], 16)
                tt(a32[:, c % 2].rearrange("p (b t) -> p b t", t=TB), gin[:, c % 4].rearrange("p (b t) -> p b t", t=TB),
                   gt[:, c // 4 % 2, :, c % 4, :], ALU.mult).then_inc(s_a32, 1)
                act_lo(0, c, c + 1)

            def out_step(i, s, prep=True):
                if prep:
                    c = s + GRP
                    v.wait_ge(s_gin[c % 4], 64 * i + 16 * (c // 4 + 1))
                    v.wait_ge(s_gt[c // 4 % 2], 32 * i + 16 * (c // 8 + 1))
                    tt(a32[:, c % 2].rearrange("p (b t) -> p b t", t=TB), gin[:, c % 4].rearrange("p (b t) -> p b t", t=TB),
                       gt[:, c // 4 % 2, :, c % 4, :], ALU.mult).then_inc(s_a32, 1)
                    act_lo((s // GRP + 1) % 2, s % GRP, 16 * i + (c + 1))
                v.wait_ge(s_prod, 16 * i + (NCH + s + 1))
                k = s % KT
                av = acc[:, k].rearrange("p (h t) -> p h t", h=2)
                tt(av, av, pair(s), ALU.add).then_inc(s_flush, 1)
                v.wait_ge(s_flush, 16 * i + (s + 1))
                v.sem_inc(s_gfree, 1)

            with v.Fori(0, NCH // 16 - 1) as i:
                for s in range(16):
                    out_step(i, s)
            for s in range(16):
                out_step(NCH // 16 - 1, s, prep=s < 8)
            for k in range(KT):
                xs = xT[:, k, TP:T].rearrange("p (b l) -> p b l", l=NL)
                ms_ = acc[:, k, TP:T].rearrange("p (b l) -> p b l", l=NL)
                stt(xT[:, k, 0:TP], acc[:, k, 0:TP], mod[:, 5 * KT + k, 0:1], xT[:, k, 0:TP], ALU.mult, ALU.add)
                link(tt(ms_, ms_, over(mod[:, 5 * KT + k, 1:NSEQ], NL), ALU.mult))
                tt(xs, xs, ms_, ALU.add).then_inc(s_x1, 1)
            v.wait_ge(s_rms, 3)
            link(nc.vector.reciprocal(rs[:], rs[:]))
            for k in range(KT):
                stt(acc[:, k], xT[:, k], col("g_final", k), rs[:], ALU.mult, ALU.mult).then_inc(s_yo, 1)


def kernel(**inputs):
    import numpy as np
    import concourse.bacc as bacc
    from concourse.bass_utils import run_bass_kernel_spmd

    i = {k: np.asarray(v) for k, v in inputs.items()}

    def tiles(v):
        return v.reshape(-1, P).T

    def granules(w):
        return w.reshape(KT, P, -1, GC).transpose(2, 1, 0, 3)

    w_in = i["w_in"][0]
    gates = np.zeros((D, GC), w_in.dtype)
    gates[:, 0:NH] = w_in[:, 3584:3588]
    gates[:, 32:32 + NH] = w_in[:, 3588:3592]
    arrays = {
        "xT": np.concatenate([i["x_prompt"].reshape(TP, D), i["x_sample"].reshape(TS, D)]).reshape(T, KT, P).transpose(2, 1, 0),
        "cT": np.concatenate([i["c_prompt"], i["c_sample"]]).reshape(NSEQ, KT, P).transpose(2, 1, 0),
        "vecs": np.concatenate([tiles(i["g_mix"][0]), tiles(i["g_ffn"][0]), tiles(i["g_final"]), tiles(i["g_conv"][0]),
                                tiles(i["g_mlstm"][0]), tiles(i["w_conv"][0].reshape(-1)), tiles(i["b_mod"][0])], axis=1),
        "rows": np.concatenate([i["b_i"].T, i["b_f"].T, i["state_mlstm_m"][0].T], axis=1),
        "sconv": i["state_conv"][0].reshape(NB, 2, CT, P).transpose(3, 2, 0, 1),
        "C0": i["state_mlstm_C"][0].transpose(2, 1, 0, 3),
        "n0": i["state_mlstm_n"][0].transpose(2, 1, 0),
        "w": np.concatenate([granules(i["w_mod"][0]), granules(gates), granules(w_in[:, 0:3584]),
                             granules(i["w_out"][0]), granules(i["w_pq"][0])]),
        "keys": i["sub_keys"][0].transpose(3, 1, 0, 2).reshape(P, HP, NKEY),
        "tab": np.concatenate([i["u_tab"][0].reshape(NCH, P, KT, P).transpose(0, 3, 2, 1).reshape(NCH, P, D),
                               i["v_tab"][0].reshape(NCH // GRP, GRP, P, KT, P).transpose(0, 3, 2, 1, 4).reshape(NCH, P, D)]),
    }
    outs = {"y": (P, KT, T), "conv_p": (P, CT, 2), "conv_s": (P, CT, NB, 2), "C_p": (P, NH, DH), "n_p": (P, NH),
            "C_s": (P, NH, NB, DH), "n_s": (P, NH, NB), "m": (NH, NSEQ)}
    nc = bacc.Bacc("TRN2", target_bir_lowering=False, num_devices=1)
    arrays = {k: np.ascontiguousarray(v) for k, v in arrays.items()}
    a = {k: nc.dram_tensor("in_" + k, v.shape, mybir.dt.from_np(v.dtype), kind="ExternalInput").ap() for k, v in arrays.items()}
    o = {k: nc.dram_tensor("out_" + k, s, F32, kind="ExternalOutput").ap() for k, s in outs.items()}
    build(nc, a, o)
    r = run_bass_kernel_spmd(nc, [{"in_" + k: v for k, v in arrays.items()}], core_ids=[0]).results[0]
    r = {k: np.asarray(r["out_" + k]) for k in outs}
    y = r["y"].transpose(2, 1, 0).reshape(T, D)
    return (y[:TP].reshape(1, TP, D), y[TP:].reshape(NB, NL, D),
            r["conv_p"].transpose(2, 1, 0).reshape(1, 1, 2, DC),
            r["C_p"].transpose(1, 0, 2).reshape(1, 1, NH, DH, DH),
            r["n_p"].T.reshape(1, 1, NH, DH), r["m"][:, 0].reshape(1, 1, NH),
            r["conv_s"].transpose(2, 3, 1, 0).reshape(1, NB, 2, DC),
            r["C_s"].transpose(2, 1, 0, 3).reshape(1, NB, NH, DH, DH),
            r["n_s"].transpose(2, 1, 0).reshape(1, NB, NH, DH), r["m"][:, 1:].T.reshape(1, NB, NH))
```

```python
from contextlib import ExitStack

import concourse.bass as bass
from concourse import mybir

F32 = mybir.dt.float32
F32R = mybir.dt.float32r
U32 = mybir.dt.uint32
ALU = mybir.AluOpType
ACT = mybir.ActivationFunctionType
AXX = mybir.AxisListType.X

P = 128
D = 1024
KT = D // P
TP = 512
NB, NL = 8, 4
TS = NB * NL
T = TP + TS
HF = T // 2
NH = 4
DH = 128
DC = 512
CT = DC // P
NSEQ = 1 + NB
PH, PK = 8, 16
NKEY = 128
HP = 2 * PH
GC = 256
NMOD = 6 * D // GC
NIN = 1 + 7 * 512 // GC
NOUT = D // GC
NPQ = HP * NKEY // GC
NW = NMOD + NIN + NOUT + NPQ
RAW = 4
GR = 32 + NH
LOWEST = -3.0e38
BIG = 1.0e30
VEC = {}
_at = 0
for _name, _n in (("g_mix", KT), ("g_ffn", KT), ("g_final", KT), ("g_conv", CT), ("g_mlstm", NH),
                  ("w_conv", 3 * CT), ("b_mod", 6 * KT)):
    VEC[_name] = (_at, _at + _n)
    _at += _n
NVEC = _at
EOFF = [0, 512, 896, 1152]
EW = 1280
NCH = NKEY
GRP = 8
NT = 2 * NCH
STILES = [0, 128, 256, 384, T - P]
NST = len(STILES)
TB = 32
NTB = T // TB
STEP_TOK = TB // 4
Q_EXP = 12
Q_GATE = Q_EXP + 1


def build(nc, a, o):
    with ExitStack() as ctx:
        base, top = 17408, 229344
        ctx.enter_context(nc.sbuf_tensor("arena", [P, (top - 16512) // 4 - 8], F32))

        def at(name, shape, offset, dt=F32):
            n = 4
            for s in shape[1:]:
                n *= s
            assert base <= offset and offset + n <= top and offset % 32 == 0, (name, offset, n)
            return nc.alloc_sbuf_tensor_at(name, shape, dt, offset=offset)

        pos = [base]

        def keep(name, shape, dt=F32):
            n = 4
            for s in shape[1:]:
                n *= s
            t = at(name, shape, pos[0], dt)
            pos[0] += -(-n // 32) * 32
            return t

        xT = keep("xT", [P, KT, T])
        mod = keep("mod", [P, 6 * KT, NSEQ])
        amod = keep("amod", [P, 2, KT, NSEQ])
        vec = keep("vec", [P, NVEC])
        ident = keep("ident", [P, P])
        ones = keep("ones", [P, P])
        iota = keep("iota", [P, P])
        cmask = keep("cmask", [P, P])
        smask = keep("smask", [TS, TS])
        bmask = keep("bmask", [TS, NB])
        sel = keep("sel", [NH, NH, P])
        eps = keep("eps", [P, 1])
        cT = keep("cT", [P, KT, NSEQ])
        sq = keep("sq", [P, 2, T])
        rs = keep("rs", [P, T])
        fsel = keep("fsel", [P, CT + NH, GR])
        dsel = keep("dsel", [P, NH, GR])
        R0 = pos[0]
        RAW_AT = R0
        SPL_AT = RAW_AT + 32768
        H_AT = SPL_AT + 32768
        Z_AT = H_AT + 34816
        C_AT = Z_AT + 34816
        TAIL = C_AT + 17408 + 8224 + 768
        TAIL += -TAIL % 32

        raw = at("raw", [P, RAW, KT, GC], RAW_AT)
        wHi = at("wHi", [P, 2, KT, GC], SPL_AT, F32R)
        wLo = at("wLo", [P, 2, KT, GC], SPL_AT + 16384, F32R)
        hHi = at("hHi", [P, KT, T], H_AT, F32R)
        hLo = at("hLo", [P, KT, T], H_AT + 17408, F32R)
        zq = at("zq", [P, NH, T], Z_AT)
        zk = at("zk", [P, NH, T], Z_AT + 8704)
        zv = at("zv", [P, NH, T], Z_AT + 2 * 8704)
        zo = at("zo", [P, NH, T], Z_AT + 3 * 8704)
        hf = at("hf", [P, KT, T], C_AT)
        xc = at("xc", [P, CT, T], C_AT)
        bg = at("bg", [P, CT, T], C_AT + 8704)
        up = at("up", [P, CT, 2 + TP], C_AT + 17408)
        us = at("us", [P, CT, NB, 2 + NL], C_AT + 17408 + 8224)
        row_li = at("row_li", [P, T], TAIL)
        row_lf = at("row_lf", [NH, T], TAIL + 2176)
        row_t = at("row_t", [NH, T], TAIL + 2 * 2176)
        row_b = at("row_b", [NH, T], TAIL + 3 * 2176)
        row_r = at("row_r", [NH, T], TAIL + 4 * 2176)
        row_m = at("row_m", [NH, T], TAIL + 5 * 2176)
        row_z = rs[0:NH]
        small = at("small", [NH, 64], TAIL + 6 * 2176)
        gbias, m0 = small[:, 0:2], small[:, 2:10]
        wi = small[:, 10:10 + TS]
        wold = small[:, 42:50]
        mout = small[:, 50:59]

        bsel = at("bsel", [GR, NH, P], TAIL + 6 * 2176 + 256)
        mrow = at("mrow", [NSEQ, 2, GC], Z_AT)
        mp = [SPL_AT]

        def mix(name, shape, dt=F32):
            n = 4
            for s in shape[1:]:
                n *= s
            t = at(name, shape, mp[0], dt)
            mp[0] += -(-n // 32) * 32
            assert mp[0] <= SPL_AT + 32768, name
            return t

        ktok = mix("ktok", [P, NH + 1, DH])
        vtok = mix("vtok", [P, NH + 1, DH])
        vw = mix("vw", [P, NH, DH])
        er = mix("er", [P, EW + TS])
        vsw = mix("vsw", [TS, DH])
        vsm = mix("vsm", [TS, NB, DH])
        csb = mix("csb", [P, NB, DH])
        cst = mix("cst", [P, NH, DH])
        grp = mix("grp", [GR, T])
        drow = mix("drow", [GR, T])
        rcol = mix("rcol", [P, 2, NH + 1, NH])
        wsm = mix("wsm", [TS, NB])
        npo = mix("npo", [P, NH])
        nso = mix("nso", [P, NH, NB])
        n0 = mix("n0", [P, NH, NB])
        qwi = mix("qwi", [P, NH, TS])
        qn = mix("qn", [P, NH, TS])
        wib = mix("wib", [P, NH, TS + NB])
        mb = at("mb", [P, NH, T], C_AT + 8704)

        qT = at("qT", [P, HP, T], Z_AT)
        keys = at("keys", [P, HP, NKEY], C_AT + 17408)
        sc = at("sc", [P, NST, HP, NKEY], RAW_AT)
        tHi = at("tHi", [P, 2, KT, P], SPL_AT + 16384, F32R)
        tLo = at("tLo", [P, 2, KT, P], SPL_AT + 24576, F32R)
        ga = at("ga", [P, 2, T], SPL_AT + 8192)
        tab = at("tab", [P, RAW, KT, P], TAIL)
        zp = [Z_AT]

        def peer(name, shape, dt=F32):
            n = 4
            for q in shape[1:]:
                n *= q
            t = at(name, shape, zp[0], dt)
            zp[0] += -(-n // 32) * 32
            assert zp[0] <= Z_AT + 34816, name
            return t

        m16 = peer("m16", [P, HP, PK])
        ix = peer("ix", [P, HP, PK], U32)
        ixf = peer("ixf", [P, HP, PK])
        cand = peer("cand", [P, PH, PK, PK])
        pos16 = peer("pos16", [P, PH, PK], U32)
        pab = peer("pab", [P, 2, PH * PK], U32)
        pabf = peer("pabf", [P, 2, PH * PK])
        eqa = peer("eqa", [P, PH, PK, PK])
        scur = peer("scur", [P, HP, NKEY])
        tcur = peer("tcur", [P, PH, PK])
        eqb = at("eqb", [P, PH, PK, PK], C_AT)
        best = at("best", [P, 3, NST, PH * PK], C_AT + 8192)
        ssum = at("ssum", [P, NST * PH], C_AT + 8192 + 7680)
        idxT = at("idxT", [P, 4, T], C_AT + 17408)
        gHr = at("gHr", [P, T], C_AT, F32R)
        zp[0] = Z_AT
        oh2 = peer("oh2", [P, 2, STEP_TOK, P], F32R)
        w1 = peer("w1", [P, 2, STEP_TOK, 2, P], F32R)
        oh1 = peer("oh1", [P, STEP_TOK, P])
        stage = at("stage", [P, 2, NKEY, TB], RAW_AT)
        actHi = [at("actHi0", [P, GRP, T], Z_AT, F32R), at("actHi1", [P, GRP, T], H_AT, F32R)]
        actLo = [at("actLo0", [P, GRP, T], Z_AT + 17408, F32R), at("actLo1", [P, GRP, T], H_AT + 17408, F32R)]
        gt = at("gt", [P, 2, NTB, 4, TB], RAW_AT)
        gin = at("gin", [P, 4, T], RAW_AT + 17408)
        a32 = at("a32", [P, 2, T], RAW_AT + 17408 + 8704)
        acc = at("acc", [P, KT, T], C_AT)
        ga_dram = nc.dram_tensor("gelu_scratch", (NCH, P, T), F32, kind="Internal").ap()
        gt_dram = nc.dram_tensor("gate_scratch", (NCH // 4, P, NTB, 4 * TB), F32, kind="Internal").ap()

        ps = ctx.enter_context(nc.psum_tensor("ps", [P, 8, 512], F32))

        def pair(n):
            s = 2 * (n % 2)
            return ps[:, s:s + 2, 0:HF]

        def sem(name):
            return ctx.enter_context(nc.semaphore(name))

        s_vec = sem("small_inputs_landed")
        s_x = sem("x_landed")
        s_const = sem("constants_ready")
        s_raw = [sem(f"raw_landed{i}") for i in range(RAW)]
        s_silu = sem("silu_ready")
        s_sq = sem("square_ready")
        s_squsd = sem("square_used")
        s_nrm = sem("square_sum_done")
        s_rms = sem("rms_ready")
        s_rsq = sem("inverse_rms_ready")
        s_xn = sem("x_normed")
        s_modp = sem("mod_product_done")
        s_modr = sem("mod_rows_ready")
        s_modt = sem("mod_rows_transposed")
        s_mods = sem("mod_ready")
        s_aff = sem("prompt_affine_done")
        s_smp = sem("sample_affine_done")
        s_hhi = sem("h_hi_ready")
        s_hlo = sem("h_lo_ready")
        s_whi = sem("w_hi_ready")
        s_wlo = sem("w_lo_ready")
        s_wfree = sem("w_split_free")
        s_pj = sem("projection_done")
        s_ev = sem("projection_evacuated")
        s_conv = sem("conv_done")
        s_state = sem("conv_state_landed")
        s_convout = sem("conv_state_copied")
        s_rowa = sem("row_neg_abs_ready")
        s_rowe = sem("row_softplus_ready")
        s_rows = sem("rows_ready")
        s_rowx = sem("row_exps_ready")
        s_bc = sem("row_broadcast_done")
        s_bce = sem("row_broadcast_evacuated")
        s_col = sem("columns_transposed")
        s_colc = sem("columns_ready")
        s_n0 = sem("n0_landed")
        s_qn = sem("q_weighted")
        s_tok = sem("kv_transposed")
        s_tokc = sem("kv_tokens_ready")
        s_sp = sem("scores_done")
        s_er = sem("decay_exponents_ready")
        s_ex = sem("decay_weights_ready")
        s_p = sem("weighted_scores_ready")
        s_num = sem("numerator_done")
        s_den = sem("denominator_done")
        s_drow = sem("denominator_rows_ready")
        s_dsq = sem("denominator_term_ready")
        s_gsum = sem("group_mean_squares_ready")
        s_grow = sem("group_rows_ready")
        s_gbc = sem("group_rows_broadcast")
        s_hm = sem("head_output_ready")
        s_vw = sem("weighted_values_ready")
        s_stp = sem("state_product_done")
        s_stc = sem("state_ready")
        s_c0 = sem("c0_landed")
        s_gsq = sem("group_square_ready")
        s_gst = sem("group_sum_done")
        s_grms = sem("group_rms_ready")
        s_y = sem("mixer_normed")
        s_x1 = sem("residual_added")
        s_key = sem("keys_landed")
        s_scp = sem("retrieval_scores_done")
        s_sc = sem("retrieval_scores_ready")
        s_tk = sem("retrieval_chain")
        s_top = sem("retrieved_scores_ready")
        s_gexp = sem("retrieved_exps_ready")
        s_best = sem("retrieved_ready")
        s_bestT = sem("retrieved_transposed")
        s_idx = sem("expert_rows_ready")
        s_tab = [sem(f"table_landed{i}") for i in range(RAW)]
        s_thi = sem("table_hi_ready")
        s_tlo = sem("table_lo_ready")
        s_prod = sem("table_product_done")
        s_gelu = sem("gelu_ready")
        s_gas = [sem(f"gelu_stored{i}") for i in range(2)]
        s_oh = sem("one_hots_ready")
        s_oh1 = sem("first_one_hots_ready")
        s_gmm = sem("gate_product_done")
        s_gev = sem("gate_hi_evacuated")
        s_gadd = sem("gate_lo_added")
        s_gst2 = sem("gate_block_stored")
        s_gin = [sem(f"gelu_landed{i}") for i in range(4)]
        s_gt = [sem(f"gates_landed{i}") for i in range(2)]
        s_a32 = sem("act_ready")
        s_ahi = sem("act_hi_ready")
        s_alo = sem("act_lo_ready")
        s_flush = sem("product_added")
        s_yo = sem("y_ready")
        s_dch = sem("vector_chain")
        s_pch = sem("pool_chain")
        s_ach = sem("scalar_chain")
        s_out = sem("outputs_stored")

        def linker(eng, s):
            n = [0]

            def link(ins):
                n[0] += 1
                ins.then_inc(s, 1)
                eng.wait_ge(s, n[0])
            return link

        def col(name, i=0):
            return vec[:, VEC[name][0] + i:VEC[name][0] + i + 1]

        def span(name):
            return vec[:, VEC[name][0]:VEC[name][1]]

        def smp(ap):
            return ap.rearrange("p k (b l) -> p k b l", l=NL)

        def over(ap, n):
            return ap.unsqueeze(len(ap.shape)).broadcast_to(list(ap.shape) + [n])

        block = ctx.enter_context(nc.Block())

        @block.sync
        def _(sp):
            sp.dma_start(vec[:], a["vecs"]).then_inc(s_vec, 16)
            sp.dma_start(cT[:], a["cT"]).then_inc(s_vec, 16)
            sp.dma_start(small[:, 0:10], a["rows"]).then_inc(s_vec, 16)
            sp.dma_start(xT[:], a["xT"]).then_inc(s_x, 16)

            def load(n):
                if n >= NMOD + RAW:
                    sp.wait_ge(s_wlo, n - RAW - NMOD + 1)
                elif n >= RAW:
                    sp.wait_ge(s_modp, n - RAW + 1)
                sp.dma_start(raw[:, n % RAW], a["w"][n]).then_inc(s_raw[n % RAW], 16)

            for n in range(RAW):
                load(n)
            with sp.Fori(1, NMOD // RAW) as i:
                for j in range(RAW):
                    sp.wait_ge(s_modp, RAW * i + (j - RAW + 1))
                    sp.dma_start(raw[:, j], a["w"][bass.ds(RAW * i + j, 1)].rearrange("a p k e -> p (a k) e")).then_inc(s_raw[j], 16)
            for n in range(NMOD, NMOD + NIN):
                load(n)
                if n == NMOD + 4:
                    sp.wait_ge(s_hlo, KT)
                    sp.dma_start(us[:, :, :, 0:2], a["sconv"]).then_inc(s_state, 16)
            sp.wait_ge(s_pj, 2 * NIN - 1)
            sp.dma_start(n0[:], a["n0"]).then_inc(s_n0, 16)
            sp.dma_start(csb[:], a["C0"][:, 0]).then_inc(s_c0, 16)
            sp.wait_ge(s_convout, 1)
            sp.dma_start(o["conv_p"], up[:, :, TP:TP + 2]).then_inc(s_out, 16)
            sp.dma_start(o["conv_s"], us[:, :, :, NL:NL + 2]).then_inc(s_out, 16)
            for n in range(NMOD + NIN, NMOD + NIN + 4):
                load(n)
            for h in range(NH):
                sp.wait_ge(s_stc, h + 1)
                sp.dma_start(o["C_s"][:, h], csb[:]).then_inc(s_out, 16)
                if h + 1 < NH:
                    sp.wait_ge(s_out, 16 * (3 + h))
                    sp.dma_start(csb[:], a["C0"][:, h + 1]).then_inc(s_c0, 16)
            sp.dma_start(o["C_p"], cst[:]).then_inc(s_out, 16)
            sp.dma_start(o["n_p"], npo[:]).then_inc(s_out, 16)
            sp.dma_start(o["n_s"], nso[:]).then_inc(s_out, 16)
            sp.dma_start(o["m"], mout).then_inc(s_out, 16)
            sp.dma_start(keys[:], a["keys"]).then_inc(s_key, 16)
            for n in range(NMOD + NIN + NOUT, NW):
                load(n)

            def table(n, j, wait=True):
                if wait:
                    sp.wait_ge(s_tlo, n - RAW + 1)
                sp.dma_start(tab[:, j], a["tab"][bass.ds(n, 1)].rearrange("a p (k e) -> p (a k) e", k=KT)).then_inc(s_tab[j], 16)

            def gelu_back(c, j, wait=True):
                if wait:
                    sp.wait_ge(s_a32, c - 3)
                sp.dma_start(gin[:, j], ga_dram[bass.ds(c, 1)].rearrange("a p t -> p (a t)")).then_inc(s_gin[j], 16)

            def gates_back(q, slot, wait=True):
                if wait:
                    sp.wait_ge(s_a32, 4 * q - 4)
                sp.dma_start(gt[:, slot], gt_dram[bass.ds(q, 1)].rearrange("a p b (c t) -> p (a b) c t", c=4)).then_inc(s_gt[slot], 16)

            sp.wait_ge(s_out, 160)
            for j in range(RAW):
                table(j, j, wait=False)
            QD = Q_GATE + NTB
            with sp.Fori(1, QD) as i:
                for j in range(4):
                    table(4 * i + j, j)
            for j in range(4):
                table(4 * QD + j, j)
            sp.wait_ge(s_gst2, 16 * (NTB + 1))
            for s in s_gas:
                sp.wait_ge(s, 16 * (1 + 2 * QD - 2))
            gates_back(0, 0, wait=False)
            for j in range(4):
                gelu_back(j, j, wait=False)
            gates_back(1, 1, wait=False)
            for n in range(4 * QD + 4, NCH + 4):
                table(n, n % 4)
                gelu_back(n - 4 * QD, n % 4)
            gates_back(2, 0)
            for s in s_gas:
                sp.wait_ge(s, 16 * (1 + 64))
            with sp.Fori(0, 14) as i2:
                for p in range(2):
                    for j in range(4):
                        table(8 * i2 + (4 * p + j + NCH + 4), j)
                        gelu_back(8 * i2 + (4 * p + j + 12), j)
                    gates_back(2 * i2 + (p + 3), 1 - p)
            for n in range(NCH + 4 + 112, NT):
                table(n, n % 4)
                if n - NCH + 8 < NCH:
                    gelu_back(n - NCH + 8, n % 4)
                if n == NCH + 4 + 115:
                    gates_back(31, 1)
            for k in range(KT):
                sp.wait_ge(s_yo, k + 1)
                sp.dma_start(o["y"][:, k], acc[:, k]).then_inc(s_out, 16)
            sp.wait_ge(s_out, 16 * (10 + KT))

        @block.gpsimd
        def _(pool):
            link = linker(pool, s_pch)
            pool.memset(ident[:], 0.0)
            pool.memset(cmask[:], 1.0)
            pool.memset(smask[:], 1.0)
            pool.memset(bmask[:], 1.0)
            pool.iota(iota[:], [[1, P]], base=0, channel_multiplier=0, allow_small_or_imprecise_dtypes=True)
            pool.memset(bsel[0:8], 1.0)
            link(pool.memset(sel[:], 0.0))
            link(pool.affine_select(out=bsel[0:8], in_=bsel[0:8], compare_op=ALU.is_ge, fill=0.0, base=0,
                                    pattern=[[P, CT], [1, P]], channel_multiplier=-64))
            pool.affine_select(out=bsel[0:8], in_=bsel[0:8], compare_op=ALU.is_ge, fill=0.0, base=63,
                               pattern=[[-P, CT], [-1, P]], channel_multiplier=64)
            pool.affine_select(out=ident[:], in_=ident[:], compare_op=ALU.not_equal, fill=1.0, base=0,
                               pattern=[[-1, P]], channel_multiplier=1)
            pool.affine_select(out=sel[:], in_=sel[:], compare_op=ALU.not_equal, fill=1.0, base=0,
                               pattern=[[-1, NH], [0, P]], channel_multiplier=1)
            pool.affine_select(out=cmask[:], in_=cmask[:], compare_op=ALU.is_ge, fill=0.0, base=0,
                               pattern=[[1, P]], channel_multiplier=-1)
            link(pool.affine_select(out=bmask[:], in_=bmask[:], compare_op=ALU.is_ge, fill=0.0, base=0,
                                    pattern=[[-NL, NB]], channel_multiplier=1))
            pool.affine_select(out=bmask[:], in_=bmask[:], compare_op=ALU.is_ge, fill=0.0, base=NL - 1,
                               pattern=[[NL, NB]], channel_multiplier=-1)
            link(pool.affine_select(out=smask[:], in_=smask[:], compare_op=ALU.is_ge, fill=0.0, base=0,
                                    pattern=[[-NL, NB], [0, NL]], channel_multiplier=1))
            pool.affine_select(out=smask[:], in_=smask[:], compare_op=ALU.is_ge, fill=0.0, base=0,
                               pattern=[[1, TS]], channel_multiplier=-1).then_inc(s_const, 1)
            for g in range(NIN + NOUT + NPQ):
                n = NMOD + g
                if g == NIN:
                    pool.wait_ge(s_out, 160)
                    pool.wait_ge(s_y, KT)
                pool.wait_ge(s_whi, g + 1)
                if g >= 2:
                    pool.wait_ge(s_wfree, g - 1)
                pool.tensor_tensor(wLo[:, g % 2], raw[:, n % RAW], wHi[:, g % 2].bitcast(F32),
                                   ALU.subtract).then_inc(s_wlo, 1)

            def lo_part(n, j):
                pool.wait_ge(s_thi, n + 1)
                pool.tensor_tensor(tLo[:, j % 2], tab[:, j], tHi[:, j % 2].bitcast(F32), ALU.subtract).then_inc(s_tlo, 1)

            lo_part(0, 0)
            lo_part(1, 1)
            with pool.Fori(0, NCH // 4) as i:
                for j in range(4):
                    lo_part(4 * i + (j + 2), (j + 2) % 4)
            with pool.Fori(NCH // 4, NT // 4 - 1) as i:
                for j in range(4):
                    lo_part(4 * i + (j + 2), (j + 2) % 4)
            for n in range(NT - 2, NT):
                lo_part(n, n % 4)

        @block.tensor
        def _(pe):
            mm = nc.tensor.matmul

            def square_sum(r):
                for k in range(KT):
                    pe.wait_ge(s_sq, KT * r + k + 1)
                    for h in range(2):
                        last = mm(ps[:, 4 + h, 0:HF], ones[:], sq[:, k % 2, h * HF:(h + 1) * HF],
                                  start=(k == 0), stop=(k == KT - 1))
                    last.then_inc(s_squsd, 1)
                last_wait = KT * (r + 1)
                pe.wait_ge(s_squsd, last_wait)
                pe.sem_inc(s_nrm, 1)

            def project(g0, ng, one=False):
                def granule(g, slot, units, n, first_wait):
                    pe.wait_ge(s_whi, g + 1)
                    pe.wait_ge(s_wlo, g + 1)
                    for u in range(units):
                        if first_wait:
                            pe.wait_ge(s_ev, n + u)
                        s = 2 * ((1 + u) % 2) if units == 2 else 0
                        for k in range(KT):
                            hi = wHi[:, slot, k, u * P:(u + 1) * P]
                            lo = wLo[:, slot, k, u * P:(u + 1) * P]
                            for w, x, first, end in ((lo, hHi, k == 0, False), (hi, hHi, False, False),
                                                     (hi, hLo, False, k == KT - 1)):
                                for h in range(2):
                                    last = mm(ps[:, s + h, 0:HF], w, x[:, k, h * HF:(h + 1) * HF],
                                              start=first, stop=end)
                        last.then_inc(s_pj, 1)
                    pe.wait_ge(s_pj, n + units)
                    pe.sem_inc(s_wfree, 1)

                if one:
                    granule(g0, 0, 1, 0, False)
                else:
                    with pe.Fori(0, ng // 2) as i:
                        for q in range(2):
                            granule(2 * i + (g0 + q), (g0 + q) % 2, 2, 4 * i + (2 * (g0 + q) - 1), True)

            pe.sem_inc(s_gmm, 2)
            pe.sem_inc(s_modt, 2)
            pe.wait_ge(s_const, 2)
            square_sum(0)
            pe.wait_ge(s_silu, 1)

            def mod_rows(n, j, landed):
                pe.wait_ge(s_raw[j], 16 * landed)
                pe.wait_ge(s_modr, n + 1)
                for k in range(KT):
                    last = mm(ps[0:NSEQ, j % 2, 0:GC], cT[:, k, :], raw[:, j, k, :], start=(k == 0), stop=(k == KT - 1))
                last.then_inc(s_modp, 1)

            def mod_columns(n, j):
                pe.wait_ge(s_modr, n + 3)
                for u in range(2):
                    last = mm(ps[:, 7, bass.ds(2 * NSEQ * n + NSEQ * u, NSEQ)], mrow[:, j % 2, u * P:(u + 1) * P],
                              ident[0:NSEQ, 0:NSEQ], start=True, stop=True)
                last.then_inc(s_modt, 1)

            mod_rows(0, 0, 1)
            with pe.Fori(0, NMOD // RAW - 1) as i:
                for j in range(RAW):
                    mod_rows(RAW * i + (j + 1), (j + 1) % RAW, i + ((j + 1) // RAW + 1))
                    mod_columns(RAW * i + j, j)
            for n in range(NMOD - RAW, NMOD):
                if n + 1 < NMOD:
                    mod_rows(n + 1, (n + 1) % RAW, (n + 1) // RAW + 1)
                mod_columns(n, n % RAW)
            pe.wait_ge(s_hhi, KT)
            pe.wait_ge(s_hlo, KT)
            project(0, 1, one=True)
            project(1, NIN - 1)

            pe.wait_ge(s_rows, 1)
            pe.wait_ge(s_rowx, 1)
            for h in range(NH):
                if h >= 2:
                    pe.wait_ge(s_bce, h - 1)
                for i in range(2):
                    last = mm(ps[:, 4 + 2 * (h % 2) + i, 0:HF], sel[:, h, :], row_m[:, i * HF:(i + 1) * HF],
                              start=True, stop=True)
                last.then_inc(s_bc, 1)
            pe.wait_ge(s_ev, 2 * NIN - 1 + 1)
            for h in range(NH):
                last = mm(ps[:, 3, 40 * h:40 * h + TS + NB], sel[:, h, :], small[:, 10:50], start=True, stop=True)
            last.then_inc(s_bc, 1)
            for w, src in enumerate((row_r, row_li)):
                for i in range(NH + 1):
                    n = P if i < NH else TS
                    c = (w * (NH + 1) + i) * NH
                    last = nc.tensor.transpose(ps[0:n, 0, c:c + NH], src[0:NH, i * P:i * P + n], ident[0:NH, 0:NH])
            last.then_inc(s_col, 1)

            for h in range(NH):
                if h == 0:
                    pe.wait_ge(s_colc, 1)
                else:
                    pe.wait_ge(s_stc, h)
                    pe.wait_ge(s_hm, h)
                for i in range(NH):
                    nc.tensor.transpose(ps[:, 0, i * P:(i + 1) * P], zk[:, h, i * P:(i + 1) * P], ident[:])
                    nc.tensor.transpose(ps[:, 1, i * P:(i + 1) * P], zv[:, h, i * P:(i + 1) * P], ident[:])
                nc.tensor.transpose(ps[0:TS, 2, 0:P], zk[:, h, TP:T], ident[:])
                nc.tensor.transpose(ps[0:TS, 2, P:2 * P], zv[:, h, TP:T], ident[:]).then_inc(s_tok, 1)
                if h == 0:
                    pe.wait_ge(s_bce, NH + 1)
                for i, (b, c) in enumerate(((3, 0), (4, 0), (5, 0), (4, 384))):
                    mm(ps[:, b, c:c + TP - i * P], zk[:, h, i * P:(i + 1) * P], zq[:, h, i * P:TP], start=True, stop=True)
                mm(ps[0:TS, 5, 256:256 + TS], zk[:, h, TP:T], zq[:, h, TP:T], start=True, stop=True).then_inc(s_sp, 1)
                pe.wait_ge(s_tokc, h + 1)
                pe.wait_ge(s_p, h + 1)
                for i in range(NH):
                    mm(ps[:, 6, i * P:TP], vtok[:, i, :], er[:, EOFF[i]:EOFF[i] + TP - i * P],
                       start=(i == 0), stop=(i == NH - 1))
                pe.wait_ge(s_c0, 16 * (h + 1))
                pe.wait_ge(s_qn, 1)
                for b in range(NB):
                    mm(ps[:, 2, 256 + b * NL:256 + (b + 1) * NL], csb[:, b, :], qwi[:, h, b * NL:(b + 1) * NL],
                       start=(b == 0), stop=False)
                mm(ps[:, 2, 256:256 + TS], vtok[0:TS, NH, :], er[0:TS, EW:EW + TS], start=False, stop=True).then_inc(s_num, 1)
                for i in range(NH):
                    mm(ps[0:GR, 7, i * P:TP], dsel[:, h, :], er[:, EOFF[i]:EOFF[i] + TP - i * P],
                       start=(h == 0 and i == 0), stop=(h == NH - 1 and i == NH - 1))
                mm(ps[0:GR, 5, 288:288 + TS], dsel[:, h, :], qn[:, h, :], start=True, stop=False)
                mm(ps[0:GR, 5, 288:288 + TS], dsel[0:TS, h, :], er[0:TS, EW:EW + TS], start=False, stop=True).then_inc(s_den, 1)
                pe.wait_ge(s_vw, h + 1)
                for i in range(NH):
                    mm(ps[:, 0, 0:DH], ktok[:, i, :], vw[:, i, :], start=(i == 0), stop=(i == NH - 1))
                for i in range(NH):
                    mm(ps[:, 0, DH:DH + 1], ktok[:, i, :], rcol[:, 1, i, h:h + 1], start=(i == 0), stop=(i == NH - 1))
                mm(ps[:, 0, 136:136 + NB], ktok[0:TS, NH, :], wsm[:], start=True, stop=True)
                for i, b in enumerate((1, 3)):
                    last = mm(ps[:, b, :], ktok[0:TS, NH, :], vsm[:, 4 * i:4 * i + 4, :], start=True, stop=True)
                last.then_inc(s_stp, 1)

            pe.wait_ge(s_stc, NH)
            for i in range(CT + NH):
                pe.wait_ge(s_gsq, i + 1)
                for h in range(2):
                    last = mm(ps[0:GR, h, 0:HF], fsel[:, i, :], sq[:, i % 2, h * HF:(h + 1) * HF],
                              start=(i == 0), stop=(i == CT + NH - 1))
                last.then_inc(s_gst, 1)
            pe.wait_ge(s_grow, 1)
            for i in range(CT + NH):
                if i >= 2:
                    pe.wait_ge(s_y, i - 1)
                s = 2 + 2 * (i % 2)
                rows = slice(0, 8) if i < CT else slice(32, GR)
                for h in range(2):
                    last = mm(ps[:, s + h, 0:HF], bsel[rows, i % 4, :], grp[rows, h * HF:(h + 1) * HF], start=True, stop=True)
                last.then_inc(s_gbc, 1)
            pe.wait_ge(s_hhi, 2 * KT)
            pe.wait_ge(s_hlo, 2 * KT)
            project(NIN, NOUT)
            square_sum(1)
            pe.wait_ge(s_hhi, 3 * KT)
            pe.wait_ge(s_hlo, 3 * KT)
            project(NIN + NOUT, NPQ)
            pe.wait_ge(s_key, 16)
            pe.wait_ge(s_ev, 1 + 2 * (NIN + NOUT + NPQ) - 1)
            for i, t0 in enumerate(STILES):
                if i >= 2:
                    pe.wait_ge(s_sc, i - 1)
                for j in range(HP):
                    last = mm(ps[:, 4 * (i % 2) + j // 4, (j % 4) * NKEY:(j % 4 + 1) * NKEY], qT[:, j, t0:t0 + P],
                              keys[:, j, :], start=True, stop=True)
                last.then_inc(s_scp, 1)
            pe.wait_ge(s_sc, NST)

            def product(n, j, hi_in, lo_in, free):
                pe.wait_ge(s_tlo, n + 1)
                pe.wait_ge(*free)
                s = 2 * (j % 2)
                for k in range(KT):
                    hi, lo = tHi[:, j % 2, k, :], tLo[:, j % 2, k, :]
                    for w, x, first, end in ((lo, hi_in, k == 0, False), (hi, hi_in, False, False),
                                             (hi, lo_in, False, k == KT - 1)):
                        for h in range(2):
                            last = mm(ps[:, s + h, 0:HF], w, x[:, k, h * HF:(h + 1) * HF], start=first, stop=end)
                last.then_inc(s_prod, 1)

            def gate_product(st, j):
                pe.wait_ge(s_oh, st + 2)
                pe.wait_ge(s_gadd, st + 1)
                for t in range(STEP_TOK):
                    last = mm(ps[:, 4 + t // 2, (t % 2) * 2 * P:(t % 2 + 1) * 2 * P], oh2[:, j % 2, t, :],
                              w1[:, j % 2, t].rearrange("p w c -> p (w c)"), start=True, stop=True)
                last.then_inc(s_gmm, 1)

            with pe.Fori(0, Q_GATE) as i:
                for j in range(4):
                    product(4 * i + j, j, hHi, hLo, (s_gelu, 4 * i + (j + 1)))
            pe.wait_ge(s_best, 1)
            for q in range(3):
                for i in range(NST):
                    out = ps[:, 4 + q, i * P:(i + 1) * P] if i < 4 else ps[:, 7, q * P:(q + 1) * P]
                    last = nc.tensor.transpose(out, best[:, q, i, :], ident[:])
            last.then_inc(s_bestT, 1)
            pe.wait_ge(s_idx, 1)
            with pe.Fori(0, NTB) as i:
                for j in range(4):
                    product(4 * i + (4 * Q_GATE + j), j, hHi, hLo, (s_gelu, 4 * i + (4 * Q_GATE + j + 1)))
                    gate_product(4 * i + j, j)
            for n in range(4 * (Q_GATE + NTB), NCH):
                product(n, n % 4, hHi, hLo, (s_gelu, n + 1))
            pe.wait_ge(s_gelu, NCH + 2)
            with pe.Fori(0, NCH // GRP // 2) as i:
                for g in range(2):
                    pe.wait_ge(s_alo, 2 * GRP * i + GRP * (g + 1))
                    for j in range(KT):
                        n = 2 * GRP * i + (GRP * g + j)
                        product(n + NCH, j, actHi[g], actLo[g], (s_flush, n + (KT - 1)))
            square_sum(2)

        @block.scalar
        def _(act):
            link = linker(act, s_ach)
            f = nc.scalar.activation

            def squares(r):
                for k in range(KT):
                    if r:
                        act.wait_ge(s_x1, KT * (r - 1) + k + 1)
                    if k >= 2 or r:
                        act.wait_ge(s_squsd, KT * r + k - 1)
                    f(sq[:, k % 2], xT[:, k], ACT.Square).then_inc(s_sq, 1)

            def rms(r):
                act.wait_ge(s_nrm, r + 1)
                f(rs[:].rearrange("p (h t) -> p h t", h=2), ps[:, 4:6, 0:HF], ACT.Sqrt, bias=eps[:], scale=1.0 / D).then_inc(s_rms, 1)

            def hi_part(g):
                n = NMOD + g
                act.wait_ge(s_raw[n % RAW], 16 * (n // RAW + 1))
                if g >= 2:
                    act.wait_ge(s_wfree, g - 1)
                nc.scalar.copy(wHi[:, g % 2], raw[:, n % RAW]).then_inc(s_whi, 1)

            def make_h(r):
                act.wait_ge(s_mods, 1)
                for k in range(KT):
                    act.wait_ge(s_xn, KT * r + k + 1)
                    f(hf[:, k, 0:TP], hf[:, k, 0:TP], ACT.Identity, bias=mod[:, 3 * r * KT + k, 0:1],
                      scale=amod[:, r, k, 0:1]).then_inc(s_aff, 1)
                act.wait_ge(s_smp, r + 1)
                for k in range(KT):
                    act.wait_ge(s_aff, KT * r + k + 1)
                    nc.scalar.copy(hHi[:, k], hf[:, k]).then_inc(s_hhi, 1)

            def evacuate(n, out, func=ACT.Identity, scale=1.0):
                act.wait_ge(s_pj, n + 1)
                f(out.rearrange("p (h t) -> p h t", h=2), pair(n), func, scale=scale).then_inc(s_ev, 1)

            act.sem_inc(s_ev, 1)
            act.sem_inc(s_modr, 2)
            act.sem_inc(s_gelu, 2)
            act.wait_ge(s_vec, 48)
            f(cT[:], cT[:], ACT.Silu).then_inc(s_silu, 1)
            act.wait_ge(s_x, 16)
            squares(0)
            act.wait_ge(s_const, 2)
            rms(0)
            with act.Fori(0, NMOD // 2) as i:
                for j in range(2):
                    act.wait_ge(s_modp, 2 * i + (j + 1))
                    act.wait_ge(s_modt, 2 * i + (j + 1))
                    f(mrow[:, j], ps[0:NSEQ, j, 0:GC], ACT.Identity).then_inc(s_modr, 1)
            hi_part(0)
            hi_part(1)
            make_h(0)

            dest = {0: xc, 1: bg, 3: zq, 4: zk, 5: zv, 6: zo}
            for g in range(NIN):
                if g == 0:
                    evacuate(0, row_li[:])
                else:
                    for u in range(2):
                        n = 2 * g - 1 + u
                        kind, i = (n - 1) // 4, (n - 1) % 4
                        if kind == 2:
                            act.wait_ge(s_pj, n + 1)
                            s = 2 * (n % 2)
                            f(up[:, i, 2:2 + HF], ps[:, s, 0:HF], ACT.Identity)
                            f(up[:, i, 2 + HF:2 + TP], ps[:, s + 1, 0:TP - HF], ACT.Identity)
                            f(us[:, i, :, 2:2 + NL], ps[:, s + 1, TP - HF:HF].rearrange("p (b l) -> p b l", l=NL),
                              ACT.Identity).then_inc(s_ev, 1)
                        elif kind == 6:
                            evacuate(n, zo[:, i], ACT.Sigmoid)
                        else:
                            evacuate(n, dest[kind][:, i], scale=DH ** -0.5 if kind == 4 else 1.0)
                if g + 2 < NIN:
                    hi_part(g + 2)
                if g == 3:
                    act.wait_ge(s_rowa, 1)
                    link(f(row_t[:], row_t[:], ACT.Exp))
                    f(row_t[:], row_t[:], ACT.Ln, bias=1.0).then_inc(s_rowe, 1)
                if g == 5:
                    act.wait_ge(s_rows, 1)
                    f(row_t[:], row_t[:], ACT.Exp, scale=-1.0)
                    f(row_li[0:NH], row_li[0:NH], ACT.Exp)
                    f(small[:, 10:50], small[:, 10:50], ACT.Exp).then_inc(s_rowx, 1)

            act.wait_ge(s_conv, 1)
            for h in range(NH):
                act.wait_ge(s_bc, h + 1)
                s = 4 + 2 * (h % 2)
                f(mb[:, h].rearrange("p (h t) -> p h t", h=2), ps[:, s:s + 2, 0:HF], ACT.Identity).then_inc(s_bce, 1)
            act.wait_ge(s_bc, NH + 1)
            f(wib[:].rearrange("p h c -> p (h c)"), ps[:, 3, 0:NH * (TS + NB)], ACT.Identity).then_inc(s_bce, 1)
            act.wait_ge(s_col, 1)
            f(rcol[:, :, 0:NH, :], ps[:, 0, 0:40].rearrange("p (w i h) -> p w i h", w=2, h=NH)[:, :, 0:NH, :], ACT.Identity)
            f(rcol[0:TS, :, NH, :], ps[0:TS, 0, 0:40].rearrange("p (w i h) -> p w i h", w=2, h=NH)[:, :, NH, :],
              ACT.Identity).then_inc(s_colc, 1)
            for h in range(NH):
                act.wait_ge(s_tok, h + 1)
                if h:
                    act.wait_ge(s_stp, h)
                f(ktok[:, 0:NH, :], ps[:, 0, :].rearrange("p (i d) -> p i d", i=NH), ACT.Identity)
                f(vtok[:, 0:NH, :], ps[:, 1, :].rearrange("p (i d) -> p i d", i=NH), ACT.Identity)
                f(ktok[0:TS, NH, :], ps[0:TS, 2, 0:P], ACT.Identity)
                f(vtok[0:TS, NH, :], ps[0:TS, 2, P:2 * P], ACT.Identity).then_inc(s_tokc, 1)
                act.wait_ge(s_er, h + 1)
                f(er[:, 0:EW], er[:, 0:EW], ACT.Exp, scale=-1.0)
                f(er[0:TS, EW:EW + TS], er[0:TS, EW:EW + TS], ACT.Exp, scale=-1.0).then_inc(s_ex, 1)
            for i in range(CT + NH):
                if i == CT:
                    act.wait_ge(s_hm, NH)
                if i >= 2:
                    act.wait_ge(s_gst, i - 1)
                f(sq[:, i % 2], (xc if i < CT else zq)[:, i % 4], ACT.Square).then_inc(s_gsq, 1)
                if i == 1:
                    act.wait_ge(s_drow, 1)
                    f(grp[32:GR], drow[32:GR], ACT.Square, scale=1e-3).then_inc(s_dsq, 1)
            act.wait_ge(s_gsum, 1)
            f(grp[:], grp[:], ACT.Sqrt).then_inc(s_grms, 1)
            for k in range(KT):
                act.wait_ge(s_y, k + 1)
                nc.scalar.copy(hHi[:, k], (xc if k < CT else zq)[:, k % 4]).then_inc(s_hhi, 1)
            act.wait_ge(s_out, 160)
            act.wait_ge(s_y, KT)
            hi_part(NIN)
            hi_part(NIN + 1)
            for g in range(NIN, NIN + NOUT):
                for u in range(2):
                    n = 2 * g - 1 + u
                    evacuate(n, hf[:, 2 * (g - NIN) + u])
                if g + 2 < NIN + NOUT:
                    hi_part(g + 2)
            hi_part(NIN + NOUT)
            hi_part(NIN + NOUT + 1)
            squares(1)
            rms(1)
            make_h(1)
            for g in range(NIN + NOUT, NIN + NOUT + NPQ):
                for u in range(2):
                    evacuate(2 * g - 1 + u, qT[:, 2 * (g - NIN - NOUT) + u])
                if g + 2 < NIN + NOUT + NPQ:
                    hi_part(g + 2)
            for i in range(NST):
                act.wait_ge(s_scp, i + 1)
                f(sc[:, i].rearrange("p (b j) n -> p b (j n)", b=4), ps[:, 4 * (i % 2):4 * (i % 2) + 4, :], ACT.Identity).then_inc(s_sc, 1)

            def a_step(i, j):
                act.wait_ge(s_prod, 4 * i + (j + 1))
                act.wait_ge(s_gas[j % 2], 32 * i + 16 * (j // 2 + 1))
                f(ga[:, j % 2].rearrange("p (h t) -> p h t", h=2), pair(j), ACT.Gelu_apprx_tanh).then_inc(s_gelu, 1)
                act.wait_ge(s_tab[(j + 2) % 4], 16 * i + 16 * ((j + 2) // 4 + 1))
                nc.scalar.copy(tHi[:, j % 2], tab[:, (j + 2) % 4]).then_inc(s_thi, 1)
                c = 4 * i + j
                act.wait_ge(s_gelu, 4 * i + (j + 3))
                act.dma_start(ga_dram[c] if isinstance(c, int) else ga_dram[bass.ds(c, 1)].rearrange("a p t -> p (a t)"),
                              ga[:, j % 2]).then_inc(s_gas[j % 2], 16)

            act.sem_inc(s_gas[0], 16)
            act.sem_inc(s_gas[1], 16)
            for n in range(2):
                act.wait_ge(s_tab[n], 16)
                nc.scalar.copy(tHi[:, n], tab[:, n]).then_inc(s_thi, 1)
            with act.Fori(0, Q_EXP) as i:
                for j in range(4):
                    a_step(i, j)
            act.wait_ge(s_top, 1)
            f(best[:, 0], best[:, 0], ACT.Exp).then_inc(s_gexp, 1)
            for j in range(4):
                a_step(Q_EXP, j)
            act.wait_ge(s_idx, 1)
            act.sem_inc(s_gst2, 16)
            with act.Fori(0, NTB) as i:
                for j in range(4):
                    a_step(i + Q_GATE, j)
                    act.wait_ge(s_gmm, 4 * i + (j + 3))
                    f(stage[:, bass.ds(i % 2, 1), :, STEP_TOK * j:STEP_TOK * (j + 1)].rearrange("p s c t -> p t (s c)"),
                      ps[:, 4:8, :].rearrange("p b (t w c) -> p (b t) w c", w=2, c=P)[:, :, 0, :], ACT.Identity).then_inc(s_gev, 1)
                act.wait_ge(s_gadd, 4 * i + 5)
                act.wait_ge(s_gst2, 16 * i + 16)
                act.dma_start(gt_dram[:, :, bass.ds(i, 1), :].rearrange("q p a (c t) -> p (a q) c t", c=4),
                              stage[:, bass.ds(i % 2, 1)].rearrange("p s (q c) t -> p (s q) c t", c=4)).then_inc(s_gst2, 16)

            def act_hi(c, g, k):
                act.wait_ge(s_a32, c + 1)
                nc.scalar.copy(actHi[g][:, k], a32[:, k % 2]).then_inc(s_ahi, 1)

            for i in range(Q_GATE + NTB, NCH // 4):
                for j in range(4):
                    a_step(i, j)
                    n = 4 * (i - Q_GATE - NTB) + j
                    for c in range(n - 1, n) if 0 < n < GRP - 1 else range(n - 1, n + 1) if n else ():
                        act_hi(c, 0, c)

            def out_step(i, s, prep=True, split=True):
                if prep:
                    act_hi(16 * i + (s + GRP), (s // GRP + 1) % 2, s % GRP)
                if split:
                    act.wait_ge(s_prod, 16 * i + (NCH + s + 1))
                    act.wait_ge(s_tab[(s + 2) % 4], 64 * i + 16 * (NCH // 4 + (s + 2) // 4 + 1))
                    nc.scalar.copy(tHi[:, s % 2], tab[:, (s + 2) % 4]).then_inc(s_thi, 1)

            with act.Fori(0, NCH // 16 - 1) as i:
                for s in range(16):
                    out_step(i, s)
            for s in range(16):
                out_step(NCH // 16 - 1, s, prep=s < 8, split=s < 14)
            squares(2)
            rms(2)

        @block.vector
        def _(v):
            link = linker(v, s_dch)
            tt, tsc, stt = nc.vector.tensor_tensor, nc.vector.tensor_scalar, nc.vector.scalar_tensor_tensor

            def make_h(r):
                v.wait_ge(s_rms, r + 1)
                link(nc.vector.reciprocal(rs[:], rs[:]))
                for k in range(KT):
                    tt(hf[:, k], xT[:, k], rs[:], ALU.mult).then_inc(s_xn, 1)
                if r == 0:
                    v.wait_ge(s_modt, NMOD + 2)
                    link(tt(mod[:], ps[:, 7, 0:6 * KT * NSEQ].rearrange("p (k s) -> p k s", s=NSEQ), over(span("b_mod"), NSEQ), ALU.add))
                    stt(amod[:, 0], mod[:, KT:2 * KT], 1.0, over(span("g_mix"), NSEQ), ALU.add, ALU.mult)
                    link(stt(amod[:, 1], mod[:, 4 * KT:5 * KT], 1.0, over(span("g_ffn"), NSEQ), ALU.add, ALU.mult))
                    v.sem_inc(s_mods, 1)
                v.wait_ge(s_xn, KT * (r + 1))
                link(tt(smp(hf[:, :, TP:T]), smp(hf[:, :, TP:T]), over(amod[:, r, :, 1:NSEQ], NL), ALU.mult))
                tt(smp(hf[:, :, TP:T]), smp(hf[:, :, TP:T]), over(mod[:, 3 * r * KT:(3 * r + 1) * KT, 1:NSEQ], NL),
                   ALU.add).then_inc(s_smp, 1)
                for k in range(KT):
                    v.wait_ge(s_hhi, (2 * KT if r else 0) + k + 1)
                    tt(hLo[:, k], hf[:, k], hHi[:, k].bitcast(F32), ALU.subtract).then_inc(s_hlo, 1)

            nc.vector.memset(eps[:], 1e-6)
            nc.vector.memset(dsel[:], 0.0)
            link(nc.vector.memset(fsel[:], 0.0))
            for i in range(CT):
                for q in range(2):
                    nc.vector.memset(fsel[64 * q:64 * q + 64, i, 2 * i + q:2 * i + q + 1], 1.0 / 64)
            for h in range(NH):
                nc.vector.memset(fsel[:, CT + h, 32 + h:33 + h], 1.0 / DH)
                nc.vector.memset(dsel[:, h, 32 + h:33 + h], 1.0)
            nc.vector.memset(ones[:], 1.0).then_inc(s_const, 1)
            v.wait_ge(s_x, 16)
            v.wait_ge(s_vec, 48)
            make_h(0)

            link(nc.vector.memset(row_z, 1.0))
            nc.vector.memset(row_z[:, TP:T].rearrange("p (b l) -> p b l", l=NL)[:, :, 0:1], 0.0)
            v.wait_ge(s_ev, 1 + 1)
            link(nc.vector.tensor_copy(row_lf[:], row_li[32:32 + NH, :]))
            tsc(row_li[0:NH], row_li[0:NH], gbias[:, 0:1], None, ALU.add)
            link(tsc(row_lf[:], row_lf[:], gbias[:, 1:2], None, ALU.add))
            stt(row_t[:], row_lf[:], -1.0, row_lf[:], ALU.mult, ALU.min).then_inc(s_rowa, 1)
            v.wait_ge(s_rowe, 1)
            link(stt(row_lf[:], row_lf[:], 0.0, row_t[:], ALU.min, ALU.subtract))
            link(nc.vector.tensor_tensor_scan(row_b[:], row_z, row_lf[:], 0.0, ALU.mult, ALU.add))
            tsc(row_z, row_z, 1.0, BIG, ALU.subtract, ALU.mult)
            link(tt(row_r[:], row_li[0:NH], row_b[:], ALU.subtract))
            link(nc.vector.tensor_copy(row_t[:], row_r[:]))
            tsc(row_t[:, 0:1], row_r[:, 0:1], 0.0, None, ALU.max)
            first = row_t[:, TP:T].rearrange("p (b l) -> p b l", l=NL)[:, :, 0]
            link(tt(first, first, m0, ALU.max))
            link(nc.vector.tensor_tensor_scan(row_m[:], row_z, row_t[:], 0.0, ALU.add, ALU.max))
            ms = row_m[:, TP:T].rearrange("p (b l) -> p b l", l=NL)
            ml = ms[:, :, NL - 1]
            rsm = row_r[:, TP:T].rearrange("p (b l) -> p b l", l=NL)
            link(tt(row_t[:], row_b[:], row_m[:], ALU.add))
            nc.vector.tensor_copy(mout[:, 0:1], row_t[:, TP - 1:TP])
            nc.vector.tensor_copy(mout[:, 1:NSEQ], row_t[:, TP:T].rearrange("p (b l) -> p b l", l=NL)[:, :, NL - 1])
            tsc(row_li[0:NH, 0:TP], row_r[:, 0:TP], row_m[:, TP - 1:TP], None, ALU.subtract)
            tt(row_li[0:NH, TP:T].rearrange("p (b l) -> p b l", l=NL), rsm, over(ml, NL), ALU.subtract)
            tt(wold, m0, ml, ALU.subtract)
            tt(wi.rearrange("p (b l) -> p b l", l=NL), over(m0, NL), ms, ALU.subtract).then_inc(s_rows, 1)

            v.wait_ge(s_ev, 13 + 1)
            v.wait_ge(s_state, 16)
            nc.vector.memset(up[:, :, 0:2], 0.0)
            tt(up[:, :, 2:2 + TP], up[:, :, 2:2 + TP], xc[:, :, 0:TP], ALU.mult)
            link(tt(us[:, :, :, 2:2 + NL], us[:, :, :, 2:2 + NL], smp(xc[:, :, TP:T]), ALU.mult))
            v.sem_inc(s_convout, 1)
            for j in range(3):
                for i in range(CT):
                    w = col("w_conv", j * CT + i)
                    yp, ys = xc[:, i, 0:TP], xc[:, i, TP:T].rearrange("p (b l) -> p b l", l=NL)
                    if j == 0:
                        tsc(yp, up[:, i, j:j + TP], w, None, ALU.mult)
                        last = tsc(ys, us[:, i, :, j:j + NL], w, None, ALU.mult)
                    else:
                        stt(yp, up[:, i, j:j + TP], w, yp, ALU.mult, ALU.add)
                        last = stt(ys, us[:, i, :, j:j + NL], w, ys, ALU.mult, ALU.add)
                link(last)
            tt(xc[:], xc[:], bg[:], ALU.mult).then_inc(s_conv, 1)

            v.wait_ge(s_bce, NH + 1)
            nc.vector.memset(drow[:], 0.0)
            v.wait_ge(s_n0, 16)
            v.wait_ge(s_colc, 1)
            link(tt(qwi[:], zq[:, :, TP:T], wib[:, :, 0:TS], ALU.mult))
            tt(smp(qn[:]), smp(qwi[:]), over(n0[:], NL), ALU.mult).then_inc(s_qn, 1)
            for h in range(NH):
                if h:
                    v.wait_ge(s_den, h)
                for i in range(NH):
                    tsc(er[:, EOFF[i]:EOFF[i] + TP - i * P], mb[:, h, i * P:TP], rcol[:, 0, i, h:h + 1], 0.0,
                        ALU.subtract, ALU.max)
                tsc(er[0:TS, EW:EW + TS], mb[0:TS, h, TP:T], rcol[0:TS, 0, NH, h:h + 1], 0.0,
                    ALU.subtract, ALU.max).then_inc(s_er, 1)
                v.wait_ge(s_tokc, h + 1)
                if h:
                    v.wait_ge(s_stp, h)
                tt(vw[:], vtok[:, 0:NH, :], over(rcol[:, 1, 0:NH, h], DH), ALU.mult)
                tsc(wsm[:], bmask[:], rcol[0:TS, 1, NH, h:h + 1], None, ALU.mult)
                link(tsc(vsw[:], vtok[0:TS, NH, :], rcol[0:TS, 1, NH, h:h + 1], None, ALU.mult))
                tt(vsm[:], vsw[:].unsqueeze(1).broadcast_to([TS, NB, DH]), over(bmask[:], DH), ALU.mult).then_inc(s_vw, 1)
                v.wait_ge(s_ex, h + 1)
                v.wait_ge(s_sp, h + 1)
                for i in range(NH):
                    c = EOFF[i]
                    last = tt(er[:, c:c + P], er[:, c:c + P], cmask[:], ALU.mult)
                link(tt(er[0:TS, EW:EW + TS], er[0:TS, EW:EW + TS], smask[:], ALU.mult))
                for i, (b, c) in enumerate(((3, 0), (4, 0), (5, 0), (4, 384))):
                    e = er[:, EOFF[i]:EOFF[i] + TP - i * P]
                    tt(e, e, ps[:, b, c:c + TP - i * P], ALU.mult)
                tt(er[0:TS, EW:EW + TS], er[0:TS, EW:EW + TS], ps[0:TS, 5, 256:256 + TS], ALU.mult).then_inc(s_p, 1)
                v.wait_ge(s_num, h + 1)
                tt(zq[:, h, 0:TP], ps[:, 6, :], zo[:, h, 0:TP], ALU.mult)
                tt(zq[:, h, TP:T], ps[:, 2, 256:256 + TS], zo[:, h, TP:T], ALU.mult).then_inc(s_hm, 1)
                v.wait_ge(s_den, h + 1)
                tt(drow[32:GR, TP:T], drow[32:GR, TP:T], ps[32:GR, 5, 288:288 + TS], ALU.add)
                v.wait_ge(s_stp, h + 1)
                nc.vector.tensor_copy(cst[:, h], ps[:, 0, 0:DH])
                nc.vector.tensor_copy(npo[:, h:h + 1], ps[:, 0, DH:DH + 1])
                tt(nso[:, h], n0[:, h], wib[:, h, TS:TS + NB], ALU.mult)
                link(tt(csb[:], csb[:], over(wib[:, h, TS:TS + NB], DH), ALU.mult))
                tt(nso[:, h], nso[:, h], ps[:, 0, 136:136 + NB], ALU.add)
                tt(csb[:, 0:4], csb[:, 0:4], ps[:, 1, :].rearrange("p (b d) -> p b d", b=4), ALU.add)
                tt(csb[:, 4:8], csb[:, 4:8], ps[:, 3, :].rearrange("p (b d) -> p b d", b=4), ALU.add).then_inc(s_stc, 1)

            nc.vector.memset(grp[:], 1e-6)
            link(nc.vector.tensor_copy(bsel[32:GR], sel[:]))
            link(nc.vector.tensor_copy(grp[32:GR], row_t[:]))
            dp, dsm = drow[32:GR, 0:TP], drow[32:GR, TP:T]
            tt(dp, grp[32:GR, 0:TP], ps[32:GR, 7, :], ALU.max)
            link(stt(dsm, dsm, -1.0, dsm, ALU.mult, ALU.max))
            tt(dsm, grp[32:GR, TP:T], dsm, ALU.max)
            stt(dp, ps[32:GR, 7, :], -1.0, dp, ALU.mult, ALU.max).then_inc(s_drow, 1)
            v.wait_ge(s_dsq, 1)
            v.wait_ge(s_gst, CT + NH)
            gv = grp[:].rearrange("p (h t) -> p h t", h=2)
            tt(gv, gv, ps[0:GR, 0:2, 0:HF], ALU.add).then_inc(s_gsum, 1)
            v.wait_ge(s_grms, 1)
            nc.vector.reciprocal(grp[:], grp[:]).then_inc(s_grow, 1)
            for i in range(CT + NH):
                v.wait_ge(s_gbc, i + 1)
                s = 2 + 2 * (i % 2)
                y = (xc if i < CT else zq)[:, i % 4].rearrange("p (h t) -> p h t", h=2)
                stt(y, y, col("g_conv", i) if i < CT else col("g_mlstm", i - CT), ps[:, s:s + 2, 0:HF],
                    ALU.mult, ALU.mult).then_inc(s_y, 1)
            for k in range(KT):
                v.wait_ge(s_hhi, KT + k + 1)
                tt(hLo[:, k], (xc if k < CT else zq)[:, k % 4], hHi[:, k].bitcast(F32), ALU.subtract).then_inc(s_hlo, 1)
            for k in range(KT):
                v.wait_ge(s_ev, 1 + 2 * NIN - 1 + k + 1)
                xs = xT[:, k, TP:T].rearrange("p (b l) -> p b l", l=NL)
                ms_ = hf[:, k, TP:T].rearrange("p (b l) -> p b l", l=NL)
                stt(xT[:, k, 0:TP], hf[:, k, 0:TP], mod[:, 2 * KT + k, 0:1], xT[:, k, 0:TP], ALU.mult, ALU.add)
                link(tt(ms_, ms_, over(mod[:, 2 * KT + k, 1:NSEQ], NL), ALU.mult))
                tt(xs, xs, ms_, ALU.add).then_inc(s_x1, 1)
            v.wait_ge(s_x1, KT)
            make_h(1)

            CHAIN = 15

            def chain(i, n):
                v.wait_ge(s_tk, CHAIN * i + n)
                v.nop(nofuse=True)

            v.wait_ge(s_scp, NST)
            with v.Fori(0, NST) as i:
                def row(j):
                    return scur[:, j]
                v.wait_ge(s_sc, i + 1)
                nc.vector.tensor_copy(scur[:], sc[:, bass.ds(i, 1)].rearrange("p a j n -> p (a j) n")).then_inc(s_tk, 1)
                chain(i, 1)
                for j in range(HP):
                    last = nc.vector.max(m16[:, j, 0:8], row(j))
                last.then_inc(s_tk, 1)
                chain(i, 2)
                for j in range(HP):
                    nc.vector.max_index(ix[:, j, 0:8], m16[:, j, 0:8], row(j))
                    last = nc.vector.match_replace(row(j), m16[:, j, 0:8], row(j), LOWEST)
                last.then_inc(s_tk, 1)
                chain(i, 3)
                for j in range(HP):
                    last = nc.vector.max(m16[:, j, 8:16], row(j))
                last.then_inc(s_tk, 1)
                chain(i, 4)
                for j in range(HP):
                    last = nc.vector.max_index(ix[:, j, 8:16], m16[:, j, 8:16], row(j))
                last.then_inc(s_tk, 1)
                halves = m16[:].rearrange("p (h two) k -> p h two k", two=2)
                chain(i, 5)
                nc.vector.tensor_copy(ixf[:], ix[:])
                tt(cand[:], over(halves[:, :, 0, :], PK),
                   halves[:, :, 1, :].unsqueeze(2).broadcast_to([P, PH, PK, PK]), ALU.add).then_inc(s_tk, 1)
                chain(i, 6)

                def sums(h):
                    return cand[:, h].rearrange("p a b -> p (a b)")

                def top(h, r):
                    return tcur[:, h, r:r + 8]
                for h in range(PH):
                    last = nc.vector.max(top(h, 0), sums(h))
                last.then_inc(s_tk, 1)
                chain(i, 7)
                for h in range(PH):
                    nc.vector.max_index(pos16[:, h, 0:8], top(h, 0), sums(h))
                    last = nc.vector.match_replace(sums(h), top(h, 0), sums(h), LOWEST)
                last.then_inc(s_tk, 1)
                chain(i, 8)
                for h in range(PH):
                    last = nc.vector.max(top(h, 8), sums(h))
                last.then_inc(s_tk, 1)
                chain(i, 9)
                for h in range(PH):
                    last = nc.vector.max_index(pos16[:, h, 8:16], top(h, 8), sums(h))
                last.then_inc(s_tk, 1)
                chain(i, 10)
                flat = pos16[:].rearrange("p h k -> p (h k)")
                tsc(pab[:, 0], flat, 4, None, ALU.logical_shift_right)
                tsc(pab[:, 1], flat, PK - 1, None, ALU.bitwise_and).then_inc(s_tk, 1)
                tt(best[:, 0, bass.ds(i, 1), :].rearrange("p a (h k) -> p (a h) k", k=PK), tcur[:], over(tcur[:, :, 0], PK),
                   ALU.subtract)
                v.wait_ge(s_tk, CHAIN * i + 11)
                nc.vector.tensor_copy(pabf[:], pab[:]).then_inc(s_tk, 1)
                v.wait_ge(s_tk, CHAIN * i + 12)
                rank = iota[:, 0:PK].unsqueeze(1).broadcast_to([P, PH * PK, PK])
                half = ixf[:].rearrange("p (h two) k -> p h two k", two=2)
                e = (eqa, eqb)
                for w in range(2):
                    last = tt(e[w][:].rearrange("p h k a -> p (h k) a"), rank, over(pabf[:, w], PK), ALU.is_equal)
                last.then_inc(s_tk, 1)
                v.wait_ge(s_tk, CHAIN * i + 13)
                for w in range(2):
                    last = tt(e[w][:], e[w][:], half[:, :, w, :].unsqueeze(2).broadcast_to([P, PH, PK, PK]), ALU.mult)
                last.then_inc(s_tk, 1)
                v.wait_ge(s_tk, CHAIN * i + 14)
                for w in range(2):
                    last = nc.vector.tensor_reduce(best[:, 1 + w, bass.ds(i, 1), :].rearrange("p a n -> p (a n)"),
                                                   e[w][:].rearrange("p h k a -> p (h k) a"), AXX, ALU.add)
                last.then_inc(s_tk, 1)
                v.wait_ge(s_tk, CHAIN * i + 15)
            v.sem_inc(s_top, 1)
            v.wait_ge(s_gexp, 1)
            w_ = best[:, 0].rearrange("p i (h k) -> p (i h) k", k=PK)
            link(nc.vector.tensor_reduce(ssum[:], w_, AXX, ALU.add))
            link(nc.vector.reciprocal(ssum[:], ssum[:]))
            tt(w_, w_, over(ssum[:], PK), ALU.mult).then_inc(s_best, 1)
            v.wait_ge(s_bestT, 1)
            nc.vector.tensor_copy(idxT[:, 2, 0:TP], ps[:, 4, :])
            nc.vector.tensor_copy(idxT[:, 2, TP:T], ps[:, 7, P - TS:P])
            for q in range(2):
                nc.vector.tensor_copy(idxT[:, q, 0:TP], ps[:, 5 + q, :])
                last = nc.vector.tensor_copy(idxT[:, q, TP:T], ps[:, 7, (q + 2) * P - TS:(q + 2) * P])
            link(last)
            link(nc.vector.tensor_copy(gHr[:], idxT[:, 2, :]))
            link(tt(idxT[:, 3], idxT[:, 2], gHr[:].bitcast(F32), ALU.subtract))
            link(nc.vector.tensor_copy(idxT[:, 2], gHr[:].bitcast(F32)))
            v.sem_inc(s_idx, 1)

            def one_hots(i, j):
                def cols(q, n):
                    return over(idxT[:, q:q + n, bass.ds(TB * i + STEP_TOK * j, STEP_TOK)].rearrange("p w t -> p t w"), P)
                keys_ = iota[:].unsqueeze(1).broadcast_to([P, STEP_TOK, P])
                v.wait_ge(s_oh, 4 * i + (j + 1))
                tt(oh1[:].unsqueeze(2), keys_.unsqueeze(2), cols(0, 1), ALU.is_equal).then_inc(s_oh1, 1)
                v.wait_ge(s_gmm, 4 * i + (j + 1))
                tt(oh2[:, j % 2].unsqueeze(2), keys_.unsqueeze(2), cols(1, 1), ALU.is_equal)
                v.wait_ge(s_oh1, 4 * i + (j + 1))
                tt(w1[:, j % 2], oh1[:].unsqueeze(2).broadcast_to([P, STEP_TOK, 2, P]), cols(2, 2), ALU.mult).then_inc(s_oh, 1)

            def add_lo(i, j):
                v.wait_ge(s_gev, 4 * i + (j + 1))
                g_ = stage[:, bass.ds(i % 2, 1), :, STEP_TOK * j:STEP_TOK * (j + 1)].rearrange("p s c t -> p t (s c)")
                tt(g_, g_, ps[:, 4:8, :].rearrange("p b (t w c) -> p (b t) w c", w=2, c=P)[:, :, 1, :], ALU.add).then_inc(s_gadd, 1)

            v.sem_inc(s_gadd, 1)
            v.sem_inc(s_oh, 1)
            v.sem_inc(s_flush, KT)
            one_hots(0, 0)
            with v.Fori(0, NTB - 1) as i:
                for j in range(4):
                    one_hots(i + (j + 1) // 4, (j + 1) % 4)
                    add_lo(i, j)
            for j in range(4):
                if j < 3:
                    one_hots(NTB - 1, j + 1)
                add_lo(NTB - 1, j)

            def act_lo(g, k, count):
                v.wait_ge(s_ahi, count)
                tt(actLo[g][:, k], a32[:, k % 2], actHi[g][:, k].bitcast(F32), ALU.subtract).then_inc(s_alo, 1)

            link(nc.vector.memset(acc[:], 0.0))
            for c in range(GRP):
                v.wait_ge(s_gin[c % 4], 16 * (c // 4 + 1))
                v.wait_ge(s_gt[c // 4 % 2], 16)
                tt(a32[:, c % 2].rearrange("p (b t) -> p b t", t=TB), gin[:, c % 4].rearrange("p (b t) -> p b t", t=TB),
                   gt[:, c // 4 % 2, :, c % 4, :], ALU.mult).then_inc(s_a32, 1)
                act_lo(0, c, c + 1)

            def out_step(i, s, prep=True):
                if prep:
                    c = s + GRP
                    v.wait_ge(s_gin[c % 4], 64 * i + 16 * (c // 4 + 1))
                    v.wait_ge(s_gt[c // 4 % 2], 32 * i + 16 * (c // 8 + 1))
                    tt(a32[:, c % 2].rearrange("p (b t) -> p b t", t=TB), gin[:, c % 4].rearrange("p (b t) -> p b t", t=TB),
                       gt[:, c // 4 % 2, :, c % 4, :], ALU.mult).then_inc(s_a32, 1)
                    act_lo((s // GRP + 1) % 2, s % GRP, 16 * i + (c + 1))
                v.wait_ge(s_prod, 16 * i + (NCH + s + 1))
                k = s % KT
                av = acc[:, k].rearrange("p (h t) -> p h t", h=2)
                v.wait_ge(s_flush, 16 * i + (s + 1))
                tt(av, av, pair(s), ALU.add).then_inc(s_flush, 1)

            with v.Fori(0, NCH // 16 - 1) as i:
                for s in range(16):
                    out_step(i, s)
            for s in range(16):
                out_step(NCH // 16 - 1, s, prep=s < 8)
            for k in range(KT):
                xs = xT[:, k, TP:T].rearrange("p (b l) -> p b l", l=NL)
                ms_ = acc[:, k, TP:T].rearrange("p (b l) -> p b l", l=NL)
                stt(xT[:, k, 0:TP], acc[:, k, 0:TP], mod[:, 5 * KT + k, 0:1], xT[:, k, 0:TP], ALU.mult, ALU.add)
                link(tt(ms_, ms_, over(mod[:, 5 * KT + k, 1:NSEQ], NL), ALU.mult))
                tt(xs, xs, ms_, ALU.add).then_inc(s_x1, 1)
            v.wait_ge(s_rms, 3)
            link(nc.vector.reciprocal(rs[:], rs[:]))
            for k in range(KT):
                stt(acc[:, k], xT[:, k], col("g_final", k), rs[:], ALU.mult, ALU.mult).then_inc(s_yo, 1)


def kernel(**inputs):
    import numpy as np
    import concourse.bacc as bacc
    from concourse.bass_utils import run_bass_kernel_spmd

    i = {k: np.asarray(v) for k, v in inputs.items()}

    def tiles(v):
        return v.reshape(-1, P).T

    def granules(w):
        return w.reshape(KT, P, -1, GC).transpose(2, 1, 0, 3)

    w_in = i["w_in"][0]
    gates = np.zeros((D, GC), w_in.dtype)
    gates[:, 0:NH] = w_in[:, 3584:3588]
    gates[:, 32:32 + NH] = w_in[:, 3588:3592]
    arrays = {
        "xT": np.concatenate([i["x_prompt"].reshape(TP, D), i["x_sample"].reshape(TS, D)]).reshape(T, KT, P).transpose(2, 1, 0),
        "cT": np.concatenate([i["c_prompt"], i["c_sample"]]).reshape(NSEQ, KT, P).transpose(2, 1, 0),
        "vecs": np.concatenate([tiles(i["g_mix"][0]), tiles(i["g_ffn"][0]), tiles(i["g_final"]), tiles(i["g_conv"][0]),
                                tiles(i["g_mlstm"][0]), tiles(i["w_conv"][0].reshape(-1)), tiles(i["b_mod"][0])], axis=1),
        "rows": np.concatenate([i["b_i"].T, i["b_f"].T, i["state_mlstm_m"][0].T], axis=1),
        "sconv": i["state_conv"][0].reshape(NB, 2, CT, P).transpose(3, 2, 0, 1),
        "C0": i["state_mlstm_C"][0].transpose(2, 1, 0, 3),
        "n0": i["state_mlstm_n"][0].transpose(2, 1, 0),
        "w": np.concatenate([granules(i["w_mod"][0]), granules(gates), granules(w_in[:, 0:3584]),
                             granules(i["w_out"][0]), granules(i["w_pq"][0])]),
        "keys": i["sub_keys"][0].transpose(3, 1, 0, 2).reshape(P, HP, NKEY),
        "tab": np.concatenate([i["u_tab"][0].reshape(NCH, P, KT, P).transpose(0, 3, 2, 1).reshape(NCH, P, D),
                               i["v_tab"][0].reshape(NCH // GRP, GRP, P, KT, P).transpose(0, 3, 2, 1, 4).reshape(NCH, P, D)]),
    }
    outs = {"y": (P, KT, T), "conv_p": (P, CT, 2), "conv_s": (P, CT, NB, 2), "C_p": (P, NH, DH), "n_p": (P, NH),
            "C_s": (P, NH, NB, DH), "n_s": (P, NH, NB), "m": (NH, NSEQ)}
    nc = bacc.Bacc("TRN2", target_bir_lowering=False, num_devices=1)
    arrays = {k: np.ascontiguousarray(v) for k, v in arrays.items()}
    a = {k: nc.dram_tensor("in_" + k, v.shape, mybir.dt.from_np(v.dtype), kind="ExternalInput").ap() for k, v in arrays.items()}
    o = {k: nc.dram_tensor("out_" + k, s, F32, kind="ExternalOutput").ap() for k, s in outs.items()}
    build(nc, a, o)
    r = run_bass_kernel_spmd(nc, [{"in_" + k: v for k, v in arrays.items()}], core_ids=[0]).results[0]
    r = {k: np.asarray(r["out_" + k]) for k in outs}
    y = r["y"].transpose(2, 1, 0).reshape(T, D)
    return (y[:TP].reshape(1, TP, D), y[TP:].reshape(NB, NL, D),
            r["conv_p"].transpose(2, 1, 0).reshape(1, 1, 2, DC),
            r["C_p"].transpose(1, 0, 2).reshape(1, 1, NH, DH, DH),
            r["n_p"].T.reshape(1, 1, NH, DH), r["m"][:, 0].reshape(1, 1, NH),
            r["conv_s"].transpose(2, 3, 1, 0).reshape(1, NB, 2, DC),
            r["C_s"].transpose(2, 1, 0, 3).reshape(1, NB, NH, DH, DH),
            r["n_s"].transpose(2, 1, 0).reshape(1, NB, NH, DH), r["m"][:, 1:].T.reshape(1, NB, NH))
```

```python
from contextlib import ExitStack

import concourse.bass as bass
from concourse import mybir

F32 = mybir.dt.float32
F32R = mybir.dt.float32r
U32 = mybir.dt.uint32
ALU = mybir.AluOpType
ACT = mybir.ActivationFunctionType
AXX = mybir.AxisListType.X

P = 128
D = 1024
KT = D // P
TP = 512
NB, NL = 8, 4
TS = NB * NL
T = TP + TS
HF = T // 2
NH = 4
DH = 128
DC = 512
CT = DC // P
NSEQ = 1 + NB
PH, PK = 8, 16
NKEY = 128
HP = 2 * PH
GC = 256
NMOD = 6 * D // GC
NIN = 1 + 7 * 512 // GC
NOUT = D // GC
NPQ = HP * NKEY // GC
NMA = 2 * D // GC
NM1 = NMOD - (NIN - 1)
S_OUT = 2 * NIN - 1
S_PQ = S_OUT + NOUT
NS = S_PQ + NPQ
RAW = 4
GR = 32 + NH
LOWEST = -3.0e38
BIG = 1.0e30
EPS = 1e-6
VEC = {}
_at = 0
for _name, _n in (("g_mix", KT), ("g_ffn", KT), ("g_final", KT), ("g_conv", CT), ("g_mlstm", NH),
                  ("w_conv", 3 * CT), ("b_mod", 6 * KT)):
    VEC[_name] = (_at, _at + _n)
    _at += _n
NVEC = _at
EOFF = [0, 512, 896, 1152]
EW = 1280
NCH = NKEY
GRP = 8
NT = 2 * NCH
STILES = [0, 128, 256, 384, T - P]
NST = len(STILES)
TB = 32
NTB = T // TB
STEP_TOK = TB // 4
Q_EXP = 12
Q_GATE = Q_EXP + 1


def build(nc, a, o):
    with ExitStack() as ctx:
        base, top = 17408, 229344
        ctx.enter_context(nc.sbuf_tensor("arena", [P, (top - 16512) // 4 - 8], F32))

        def at(name, shape, offset, dt=F32):
            n = 4
            for s in shape[1:]:
                n *= s
            assert base <= offset and offset + n <= top and offset % 32 == 0, (name, offset, n)
            return nc.alloc_sbuf_tensor_at(name, shape, dt, offset=offset)

        pos = [base]

        def keep(name, shape, dt=F32):
            n = 4
            for s in shape[1:]:
                n *= s
            t = at(name, shape, pos[0], dt)
            pos[0] += -(-n // 32) * 32
            return t

        xT = keep("xT", [P, KT, T])
        mod = keep("mod", [P, 6 * KT, NSEQ])
        amod = keep("amod", [P, 2, KT, NSEQ])
        vec = keep("vec", [P, NVEC])
        ident = keep("ident", [P, P])
        ones = keep("ones", [P, P])
        iota = keep("iota", [P, P])
        cmask = keep("cmask", [P, P])
        smask = keep("smask", [TS, TS])
        bmask = keep("bmask", [TS, NB])
        sel = keep("sel", [NH, NH, P])
        eps = keep("eps", [P, 1])
        idle = keep("idle", [P, 2])
        cT = keep("cT", [P, KT, NSEQ])
        SQ_AT = pos[0]
        sq = keep("sq", [P, 2, T])
        rs = keep("rs", [P, T])
        fsel = keep("fsel", [P, CT + NH, GR])
        dsel = keep("dsel", [P, NH, GR])
        R0 = pos[0]
        RAW_AT = R0
        SPL_AT = RAW_AT + 32768
        H_AT = SPL_AT + 32768
        Z_AT = H_AT + 34816
        C_AT = Z_AT + 34816
        TAIL = C_AT + 17408 + 8224 + 768
        TAIL += -TAIL % 32

        raw = at("raw", [P, RAW, KT, GC], RAW_AT)
        wHi = at("wHi", [P, 2, KT, GC], SPL_AT, F32R)
        wLo = at("wLo", [P, 2, KT, GC], SPL_AT + 16384, F32R)
        hHi = at("hHi", [P, KT, T], H_AT, F32R)
        hLo = at("hLo", [P, KT, T], H_AT + 17408, F32R)
        zq = at("zq", [P, NH, T], Z_AT)
        zk = at("zk", [P, NH, T], Z_AT + 8704)
        zv = at("zv", [P, NH, T], Z_AT + 2 * 8704)
        zo = at("zo", [P, NH, T], Z_AT + 3 * 8704)
        hf = at("hf", [P, KT, T], C_AT)
        xc = at("xc", [P, CT, T], C_AT)
        bg = at("bg", [P, CT, T], C_AT + 8704)
        up = at("up", [P, CT, 2 + TP], C_AT + 17408)
        us = at("us", [P, CT, NB, 2 + NL], C_AT + 17408 + 8224)
        row_li = at("row_li", [P, T], TAIL)
        row_lf = at("row_lf", [NH, T], TAIL + 2176)
        row_t = at("row_t", [NH, T], TAIL + 2 * 2176)
        row_b = at("row_b", [NH, T], TAIL + 3 * 2176)
        row_r = at("row_r", [NH, T], TAIL + 4 * 2176)
        row_m = at("row_m", [NH, T], TAIL + 5 * 2176)
        row_z = rs[0:NH]
        small = at("small", [NH, 64], TAIL + 6 * 2176)
        gbias, m0 = small[:, 0:2], small[:, 2:10]
        wi = small[:, 10:10 + TS]
        wold = small[:, 42:50]
        mout = small[:, 50:59]

        bsel = at("bsel", [8, CT, P], TAIL + 6 * 2176 + 256)
        bselr = at("bselr", [GR, NH, P], TAIL + 6 * 2176 + 256 + 2048, F32R)
        c2 = at("c2", [P, KT, 2 * NSEQ], TAIL + 6 * 2176 + 256, F32R)
        id2 = at("id2", [2 * NSEQ, NSEQ], Z_AT + 4096)
        ident2 = at("ident2", [2 * NSEQ, NSEQ], TAIL + 6 * 2176 + 256 + 576)
        mrow2 = at("mrow2", [2 * NSEQ, 2, GC], SQ_AT)
        mrow = at("mrow", [NSEQ, 2, GC], Z_AT)
        grp = at("grp", [GR, T], C_AT + 17408)
        drow = at("drow", [GR, T], C_AT + 17408 + 2176)
        erow = at("erow", [GR, T], C_AT + 17408 + 2 * 2176)
        grHi = at("grHi", [GR, T], C_AT + 17408 + 2 * 2176, F32R)
        grLo = at("grLo", [GR, T], C_AT + 17408 + 3 * 2176, F32R)
        mp = [H_AT]

        def mix(name, shape, dt=F32):
            n = 4
            for s in shape[1:]:
                n *= s
            t = at(name, shape, mp[0], dt)
            mp[0] += -(-n // 32) * 32
            assert mp[0] <= H_AT + 34816, name
            return t

        ktok = mix("ktok", [P, NH + 1, DH])
        vtok = mix("vtok", [P, NH + 1, DH])
        vw = mix("vw", [P, NH, DH + 1])
        er = mix("er", [P, EW + TS])
        vsw = mix("vsw", [TS, DH])
        vsm = mix("vsm", [TS, NB, DH])
        csb = mix("csb", [P, NB, DH])
        cst = mix("cst", [P, NH, DH])
        rcol = mix("rcol", [P, 2, NH + 1, NH])
        wsm = mix("wsm", [TS, NB])
        npo = mix("npo", [P, NH])
        nso = mix("nso", [P, NH, NB])
        n0 = mix("n0", [P, NH, NB])
        qwi = mix("qwi", [P, NH, TS])
        qn = mix("qn", [P, NH, TS])
        wib = mix("wib", [P, NH, TS + NB])
        mb = at("mb", [P, NH, T], C_AT + 8704)

        qT = at("qT", [P, HP, T], Z_AT)
        keys = at("keys", [P, HP, NKEY], C_AT + 17408)
        sc = at("sc", [P, NST, HP, NKEY], RAW_AT)
        tHi = at("tHi", [P, 2, KT, P], SPL_AT + 16384, F32R)
        tLo = at("tLo", [P, 2, KT, P], SPL_AT + 24576, F32R)
        ga = at("ga", [P, 2, T], SPL_AT + 8192)
        tab = at("tab", [P, RAW, KT, P], TAIL)
        zp = [Z_AT]

        def peer(name, shape, dt=F32):
            n = 4
            for q in shape[1:]:
                n *= q
            t = at(name, shape, zp[0], dt)
            zp[0] += -(-n // 32) * 32
            assert zp[0] <= Z_AT + 34816, name
            return t

        m16 = peer("m16", [P, HP, PK])
        ix = peer("ix", [P, HP, PK], U32)
        ixf = peer("ixf", [P, HP, PK])
        cand = peer("cand", [P, PH, PK, PK])
        pos16 = peer("pos16", [P, PH, PK], U32)
        pab = peer("pab", [P, 2, PH * PK], U32)
        pabf = peer("pabf", [P, 2, PH * PK])
        eqa = peer("eqa", [P, PH, PK, PK])
        scur = peer("scur", [P, HP, NKEY])
        tcur = peer("tcur", [P, PH, PK])
        eqb = at("eqb", [P, PH, PK, PK], C_AT)
        best = at("best", [P, 3, NST, PH * PK], C_AT + 8192)
        ssum = at("ssum", [P, NST * PH], C_AT + 8192 + 7680)
        idxT = at("idxT", [P, 4, T], C_AT + 17408)
        gHr = at("gHr", [P, T], C_AT, F32R)
        zp[0] = Z_AT
        oh2 = peer("oh2", [P, 2, STEP_TOK, P], F32R)
        w1 = peer("w1", [P, 2, STEP_TOK, 2, P], F32R)
        oh1 = peer("oh1", [P, STEP_TOK, P])
        stage = at("stage", [P, 2, NKEY, TB], RAW_AT)
        actHi = [at("actHi0", [P, GRP, T], Z_AT, F32R), at("actHi1", [P, GRP, T], H_AT, F32R)]
        actLo = [at("actLo0", [P, GRP, T], Z_AT + 17408, F32R), at("actLo1", [P, GRP, T], H_AT + 17408, F32R)]
        gt = at("gt", [P, 2, NTB, 4, TB], RAW_AT)
        gin = at("gin", [P, 4, T], RAW_AT + 17408)
        a32 = at("a32", [P, 2, T], RAW_AT + 17408 + 8704)
        acc = at("acc", [P, KT, T], C_AT)
        ga_dram = nc.dram_tensor("gelu_scratch", (NCH, P, T), F32, kind="Internal").ap()
        gt_dram = nc.dram_tensor("gate_scratch", (NCH // 4, P, NTB, 4 * TB), F32, kind="Internal").ap()

        ps = ctx.enter_context(nc.psum_tensor("ps", [P, 8, 512], F32))

        def pair(n):
            s = 2 * (n % 2)
            return ps[:, s:s + 2, 0:HF]

        def bcast_pair(i):
            s = 2 * i if i < 2 else 4 + 2 * (i % 2)
            return ps[:, s:s + 2, 0:HF]

        def sem(name):
            return ctx.enter_context(nc.semaphore(name))

        s_vec = sem("small_inputs_landed")
        s_cond = sem("conditions_landed")
        s_x = sem("x_landed")
        s_const = sem("constants_ready")
        s_raw = [sem(f"raw_landed{i}") for i in range(RAW)]
        s_silu = sem("silu_ready")
        s_sq = sem("square_ready")
        s_ssq = sem("square_added")
        s_nrm = sem("square_sum_done")
        s_rms = sem("rms_ready")
        s_xn = sem("x_normed")
        s_modp = sem("mod_product_done")
        s_modr = sem("mod_rows_ready")
        s_modt = sem("mod_rows_transposed")
        s_mods = sem("mod_columns_read")
        s_c2 = sem("conditions_split")
        s_hhs = sem("h_hi_samples_ready")
        s_smp = sem("sample_affine_done")
        s_hhi = sem("h_hi_ready")
        s_hlo = sem("h_lo_ready")
        s_whi = sem("w_hi_ready")
        s_wlo = sem("w_lo_ready")
        s_pj = sem("projection_done")
        s_ev = sem("projection_evacuated")
        s_conv = sem("conv_done")
        s_state = sem("conv_state_landed")
        s_convout = sem("conv_state_copied")
        s_rowa = sem("row_neg_abs_ready")
        s_rowe = sem("row_softplus_ready")
        s_rows = sem("rows_ready")
        s_rowx = sem("row_exps_ready")
        s_bc = sem("row_broadcast_done")
        s_bce = sem("row_broadcast_evacuated")
        s_col = sem("columns_transposed")
        s_colc = sem("columns_ready")
        s_n0 = sem("n0_landed")
        s_qn = sem("q_weighted")
        s_tok = sem("kv_transposed")
        s_tokc = sem("kv_tokens_ready")
        s_sp = sem("scores_done")
        s_er = sem("decay_exponents_ready")
        s_ex = sem("decay_weights_ready")
        s_p = sem("weighted_scores_ready")
        s_num = sem("numerator_done")
        s_den = sem("denominator_done")
        s_drow = sem("denominator_rows_ready")
        s_dsq = sem("denominator_term_ready")
        s_gsum = sem("group_mean_squares_ready")
        s_grow = sem("group_rows_ready")
        s_ghi = sem("group_rows_hi_ready")
        s_glo = sem("group_rows_lo_ready")
        s_gacc = sem("group_sums_added")
        s_gbc = sem("group_rows_broadcast")
        s_hm = sem("head_output_ready")
        s_vw = sem("weighted_values_ready")
        s_stp = sem("state_product_done")
        s_stb = sem("state_banks_0_1_read")
        s_stc = sem("state_ready")
        s_c0 = sem("c0_landed")
        s_gsq = sem("group_square_ready")
        s_gst = sem("group_sum_done")
        s_grms = sem("group_rms_ready")
        s_y = sem("mixer_normed")
        s_x1 = sem("residual_added")
        s_key = sem("keys_landed")
        s_scp = sem("retrieval_scores_done")
        s_sc = sem("retrieval_scores_ready")
        s_tk = sem("retrieval_chain")
        s_top = sem("retrieved_scores_ready")
        s_gexp = sem("retrieved_exps_ready")
        s_best = sem("retrieved_ready")
        s_bestT = sem("retrieved_transposed")
        s_tab = [sem(f"table_landed{i}") for i in range(RAW)]
        s_thi = sem("table_hi_ready")
        s_tlo = sem("table_lo_ready")
        s_prod = sem("table_product_done")
        s_gelu = sem("gelu_ready")
        s_gas = [sem(f"gelu_stored{i}") for i in range(2)]
        s_oh = sem("one_hots_ready")
        s_oh1 = sem("first_one_hots_ready")
        s_gmm = sem("gate_product_done")
        s_gev = sem("gate_hi_evacuated")
        s_gadd = sem("gate_lo_added")
        s_gst2 = sem("gate_block_stored")
        s_gin = [sem(f"gelu_landed{i}") for i in range(4)]
        s_gt = [sem(f"gates_landed{i}") for i in range(2)]
        s_a32 = sem("act_ready")
        s_ahi = sem("act_hi_ready")
        s_alo = sem("act_lo_ready")
        s_flush = sem("product_added")
        s_yo = sem("y_ready")
        s_dch = sem("vector_chain")
        s_pch = sem("pool_chain")
        s_ach = sem("scalar_chain")
        s_out = sem("outputs_stored")

        def linker(eng, s):
            n = [0]

            def link(ins):
                n[0] += 1
                ins.then_inc(s, 1)
                eng.wait_ge(s, n[0])
            return link

        def col(name, i=0):
            return vec[:, VEC[name][0] + i:VEC[name][0] + i + 1]

        def span(name):
            return vec[:, VEC[name][0]:VEC[name][1]]

        def smp(ap):
            return ap.rearrange("p k (b l) -> p k b l", l=NL)

        def over(ap, n):
            return ap.unsqueeze(len(ap.shape)).broadcast_to(list(ap.shape) + [n])

        block = ctx.enter_context(nc.Block())

        @block.sync
        def _(sp):
            sp.dma_start(cT[:], a["cT"]).then_inc(s_cond, 16)

            def load(p):
                if p >= NM1 + RAW:
                    sp.wait_ge(s_wlo, 2 * (p - RAW - NM1 + 1))
                elif p >= RAW:
                    sp.wait_ge(s_modp, p - RAW + 1)
                sp.dma_start(raw[:, p % RAW], a["w"][p]).then_inc(s_raw[p % RAW], 16)

            for p in range(NM1 + RAW + 2):
                load(p)
                if p == 1:
                    sp.dma_start(xT[:], a["xT"]).then_inc(s_x, 16)
                    sp.dma_start(vec[:], a["vecs"]).then_inc(s_vec, 16)
                    sp.dma_start(small[:, 0:10], a["rows"]).then_inc(s_vec, 16)
            sp.wait_ge(s_hlo, KT)
            sp.dma_start(us[:, :, :, 0:2], a["sconv"]).then_inc(s_state, 16)
            P0 = NM1 + RAW + 2
            with sp.Fori(0, (NM1 + S_OUT - P0) // RAW) as i:
                for j in range(RAW):
                    sp.wait_ge(s_wlo, 2 * RAW * i + 2 * (P0 + j - RAW - NM1 + 1))
                    q = (P0 + j) % RAW
                    sp.dma_start(raw[:, q], a["w"][bass.ds(RAW * i + (P0 + j), 1)].rearrange("a p k e -> p (a k) e")).then_inc(s_raw[q], 16)
            for p in range(P0 + (NM1 + S_OUT - P0) // RAW * RAW, NM1 + S_OUT):
                load(p)
            sp.wait_ge(s_pj, 2 * NIN - 1)
            sp.dma_start(n0[:], a["n0"]).then_inc(s_n0, 16)
            sp.dma_start(csb[:], a["C0"][:, 0]).then_inc(s_c0, 16)
            sp.wait_ge(s_convout, 1)
            sp.dma_start(o["conv_p"], up[:, :, TP:TP + 2]).then_inc(s_out, 16)
            sp.dma_start(o["conv_s"], us[:, :, :, NL:NL + 2]).then_inc(s_out, 16)
            for p in range(NM1 + S_OUT, NM1 + S_OUT + NOUT):
                load(p)
            for h in range(NH):
                sp.wait_ge(s_stc, h + 1)
                sp.dma_start(o["C_s"][:, h], csb[:]).then_inc(s_out, 16)
                if h + 1 < NH:
                    sp.wait_ge(s_out, 16 * (3 + h))
                    sp.dma_start(csb[:], a["C0"][:, h + 1]).then_inc(s_c0, 16)
            sp.dma_start(o["C_p"], cst[:]).then_inc(s_out, 16)
            sp.dma_start(o["n_p"], npo[:]).then_inc(s_out, 16)
            sp.dma_start(o["n_s"], nso[:]).then_inc(s_out, 16)
            sp.dma_start(o["m"], mout).then_inc(s_out, 16)
            for p in range(NM1 + S_PQ, NM1 + S_PQ + 2):
                load(p)
            sp.wait_ge(s_gbc, CT + NH)
            sp.dma_start(keys[:], a["keys"]).then_inc(s_key, 16)
            for p in range(NM1 + S_PQ + 2, NM1 + NS):
                load(p)

            def table(n, j, wait=True):
                if wait:
                    sp.wait_ge(s_tlo, n - RAW + 1)
                sp.dma_start(tab[:, j], a["tab"][bass.ds(n, 1)].rearrange("a p (k e) -> p (a k) e", k=KT)).then_inc(s_tab[j], 16)

            def gelu_back(c, j, wait=True):
                if wait:
                    sp.wait_ge(s_a32, c - 3)
                sp.dma_start(gin[:, j], ga_dram[bass.ds(c, 1)].rearrange("a p t -> p (a t)")).then_inc(s_gin[j], 16)

            def gates_back(q, slot, wait=True):
                if wait:
                    sp.wait_ge(s_a32, 4 * q - 4)
                sp.dma_start(gt[:, slot], gt_dram[bass.ds(q, 1)].rearrange("a p b (c t) -> p (a b) c t", c=4)).then_inc(s_gt[slot], 16)

            sp.wait_ge(s_out, 160)
            for j in range(RAW):
                table(j, j, wait=False)
            QD = Q_GATE + NTB
            with sp.Fori(1, QD) as i:
                for j in range(4):
                    table(4 * i + j, j)
            for n in range(4 * QD, 4 * QD + 5):
                table(n, n % 4)
            sp.wait_ge(s_gst2, 16 * (NTB + 1))
            for s in s_gas:
                sp.wait_ge(s, 16 * (1 + 2 * QD - 2))
            gates_back(0, 0, wait=False)
            gelu_back(0, 0, wait=False)
            gelu_back(1, 1, wait=False)
            table(4 * QD + 5, 1)
            gates_back(1, 1, wait=False)
            gelu_back(2, 2, wait=False)
            gelu_back(3, 3, wait=False)
            table(4 * QD + 6, 2)
            gelu_back(4, 0)
            gelu_back(5, 1)
            table(4 * QD + 7, 3)
            gelu_back(6, 2)
            gelu_back(7, 3)
            for n in range(NCH, NCH + 4):
                table(n, n % 4)
                gelu_back(n - 4 * QD, n % 4)
            gates_back(2, 0)
            for s in s_gas:
                sp.wait_ge(s, 16 * (1 + 64))
            with sp.Fori(0, 14) as i2:
                for p in range(2):
                    for j in range(4):
                        table(8 * i2 + (4 * p + j + NCH + 4), j)
                        gelu_back(8 * i2 + (4 * p + j + 12), j)
                    gates_back(2 * i2 + (p + 3), 1 - p)
            for n in range(NCH + 4 + 112, NT):
                table(n, n % 4)
                if n - NCH + 8 < NCH:
                    gelu_back(n - NCH + 8, n % 4)
                if n == NCH + 4 + 115:
                    gates_back(31, 1)
            for k in range(KT):
                sp.wait_ge(s_yo, k + 1)
                sp.dma_start(o["y"][:, k], acc[:, k]).then_inc(s_out, 16)
            sp.wait_ge(s_out, 16 * (10 + KT))

        @block.gpsimd
        def _(pool):
            link = linker(pool, s_pch)
            pool.memset(ident[:], 0.0)
            pool.memset(cmask[:], 1.0)
            pool.memset(smask[:], 1.0)
            pool.memset(bmask[:], 1.0)
            pool.iota(iota[:], [[1, P]], base=0, channel_multiplier=0, allow_small_or_imprecise_dtypes=True)
            pool.memset(bsel[:], 1.0)
            pool.memset(id2[:], 0.0)
            link(pool.memset(sel[:], 0.0))
            link(pool.affine_select(out=bsel[:], in_=bsel[:], compare_op=ALU.is_ge, fill=0.0, base=0,
                                    pattern=[[P, CT], [1, P]], channel_multiplier=-64))
            pool.affine_select(out=bsel[:], in_=bsel[:], compare_op=ALU.is_ge, fill=0.0, base=63,
                               pattern=[[-P, CT], [-1, P]], channel_multiplier=64)
            pool.affine_select(out=ident[:], in_=ident[:], compare_op=ALU.not_equal, fill=1.0, base=0,
                               pattern=[[-1, P]], channel_multiplier=1)
            for q in range(2):
                link(pool.affine_select(out=id2[:], in_=id2[:], compare_op=ALU.not_equal, fill=1.0, base=-q * NSEQ,
                                        pattern=[[-1, NSEQ]], channel_multiplier=1))
            pool.affine_select(out=sel[:], in_=sel[:], compare_op=ALU.not_equal, fill=1.0, base=0,
                               pattern=[[-1, NH], [0, P]], channel_multiplier=1)
            pool.affine_select(out=cmask[:], in_=cmask[:], compare_op=ALU.is_ge, fill=0.0, base=0,
                               pattern=[[1, P]], channel_multiplier=-1)
            link(pool.affine_select(out=bmask[:], in_=bmask[:], compare_op=ALU.is_ge, fill=0.0, base=0,
                                    pattern=[[-NL, NB]], channel_multiplier=1))
            pool.affine_select(out=bmask[:], in_=bmask[:], compare_op=ALU.is_ge, fill=0.0, base=NL - 1,
                               pattern=[[NL, NB]], channel_multiplier=-1)
            link(pool.affine_select(out=smask[:], in_=smask[:], compare_op=ALU.is_ge, fill=0.0, base=0,
                                    pattern=[[-NL, NB], [0, NL]], channel_multiplier=1))
            pool.affine_select(out=smask[:], in_=smask[:], compare_op=ALU.is_ge, fill=0.0, base=0,
                               pattern=[[1, TS]], channel_multiplier=-1).then_inc(s_const, 1)
            def w_lo(g, q):
                for u in range(2):
                    pool.wait_ge(s_whi, 2 * g + (u + 1))
                    half = slice(u * P, (u + 1) * P)
                    pool.tensor_tensor(wLo[:, q % 2, :, half], raw[:, (NM1 + q) % RAW, :, half],
                                       wHi[:, q % 2, :, half].bitcast(F32), ALU.subtract).then_inc(s_wlo, 1)

            with pool.Fori(0, NS // 4) as i:
                for j in range(4):
                    w_lo(4 * i + j, j)
            for g in range(NS // 4 * 4, NS):
                w_lo(g, g)

            def lo_part(n, j):
                pool.wait_ge(s_thi, n + 1)
                pool.tensor_tensor(tLo[:, j % 2], tab[:, j], tHi[:, j % 2].bitcast(F32), ALU.subtract).then_inc(s_tlo, 1)

            lo_part(0, 0)
            lo_part(1, 1)
            with pool.Fori(0, NCH // 4) as i:
                for j in range(4):
                    lo_part(4 * i + (j + 2), (j + 2) % 4)
            with pool.Fori(NCH // 4, NT // 4 - 1) as i:
                for j in range(4):
                    lo_part(4 * i + (j + 2), (j + 2) % 4)
            for n in range(NT - 2, NT):
                lo_part(n, n % 4)

        @block.tensor
        def _(pe):
            mm = nc.tensor.matmul

            def square_sum(r):
                pe.wait_ge(s_ssq, KT * (r + 1))
                for h in range(2):
                    last = mm(ps[:, 4 + h, 0:HF], ones[:], rs[:, h * HF:(h + 1) * HF], start=True, stop=True)
                last.then_inc(s_nrm, 1)

            def granule(g, slot, units, n, made=None):
                for u in range(units):
                    pe.wait_ge(s_wlo, 2 * g + (u + 1))
                    if units == 2:
                        pe.wait_ge(s_ev, n + u)
                    s = 2 * ((1 + u) % 2) if units == 2 else 0
                    for k in range(KT):
                        if made is not None and u == 0:
                            pe.wait_ge(s_hlo, made + k + 1)
                        hi = wHi[:, slot, k, u * P:(u + 1) * P]
                        lo = wLo[:, slot, k, u * P:(u + 1) * P]
                        for w, x, first, end in ((lo, hHi, k == 0, False), (hi, hHi, False, False),
                                                 (hi, hLo, False, k == KT - 1)):
                            for h in range(2):
                                last = mm(ps[:, s + h, 0:HF], w, x[:, k, h * HF:(h + 1) * HF],
                                          start=first, stop=end)
                    last.then_inc(s_pj, 1)

            def project(g0, ng, n0, made):
                granule(g0, g0 % 2, 2, n0, made)
                granule(g0 + 1, (g0 + 1) % 2, 2, n0 + 2)
                with pe.Fori(0, ng // 2 - 1) as i:
                    for q in range(2):
                        granule(2 * i + (g0 + 2 + q), (g0 + q) % 2, 2, 4 * i + (n0 + 4 + 2 * q))

            pe.sem_inc(s_gmm, 2)
            pe.sem_inc(s_modt, 2)
            pe.wait_ge(s_const, 2)
            pe.wait_ge(s_silu, 1)

            def mod_rows(n, j, landed):
                pe.wait_ge(s_raw[j], 16 * landed)
                pe.wait_ge(s_modr, n + 1)
                for k in range(KT):
                    last = mm(ps[0:NSEQ, j % 2, 0:GC], cT[:, k, :], raw[:, j, k, :], start=(k == 0), stop=(k == KT - 1))
                last.then_inc(s_modp, 1)

            def mod_columns(n, j):
                bank, n0 = (6, 0) if n < NMA else (7, NMA)
                pe.wait_ge(s_modr, n + 3)
                for u in range(2):
                    last = mm(ps[:, bank, 2 * NSEQ * (n - n0) + NSEQ * u:2 * NSEQ * (n - n0) + NSEQ * (u + 1)], mrow[:, j % 2, u * P:(u + 1) * P],
                              ident[0:NSEQ, 0:NSEQ], start=True, stop=True)
                last.then_inc(s_modt, 1)

            for n in range(NM1):
                mod_rows(n, n % RAW, n // RAW + 1)
                if n:
                    mod_columns(n - 1, (n - 1) % RAW)
                if n == NMA - 3:
                    square_sum(0)
            mod_columns(NM1 - 1, (NM1 - 1) % RAW)

            def mod_rows_split(m, j, g):
                pe.wait_ge(s_wlo, 2 * g + 2)
                pe.wait_ge(s_modr, m + 1)
                for k in range(KT):
                    for w in (wLo, wHi):
                        last = mm(ps[0:2 * NSEQ, 4 + j, 0:GC], c2[:, k, :], w[:, 0, k, :],
                                  start=(k == 0 and w is wLo), stop=(k == KT - 1 and w is wHi))
                last.then_inc(s_modp, 1)

            def mod_columns_split(m, j):
                pe.wait_ge(s_modr, m + 3)
                for u in range(2):
                    last = mm(ps[:, 7, bass.ds(2 * NSEQ * (m - NMA) + NSEQ * u, NSEQ)], mrow2[:, j, u * P:(u + 1) * P],
                              ident2[:], start=True, stop=True)
                last.then_inc(s_modt, 1)

            granule(0, 0, 1, 0, 0)
            pe.wait_ge(s_c2, 1)
            granule(1, 1, 2, 1)
            mod_rows_split(NM1, 0, 2)
            with pe.Fori(0, (NIN - 3) // 2) as i:
                for q in range(2):
                    granule(4 * i + (3 + 2 * q), 1, 2, 4 * i + (3 + 2 * q))
                    mod_rows_split(2 * i + (NM1 + 1 + q), (1 + q) % 2, 4 * i + (4 + 2 * q))
                    mod_columns_split(2 * i + (NM1 + q), q)
            t = NIN - 2
            granule(2 * t + 1, 1, 2, 2 * t + 1)
            mod_rows_split(NM1 + t, t % 2, 2 * t + 2)
            mod_columns_split(NM1 + t - 1, (t - 1) % 2)
            mod_columns_split(NMOD - 1, 1)

            pe.wait_ge(s_rows, 1)
            pe.wait_ge(s_rowx, 1)
            for h in range(NH):
                if h == 1:
                    pe.wait_ge(s_mods, 1)
                if h >= 2:
                    pe.wait_ge(s_bce, h - 1)
                for i in range(2):
                    last = mm(ps[:, 4 + 2 * (h % 2) + i, 0:HF], sel[:, h, :], row_m[:, i * HF:(i + 1) * HF],
                              start=True, stop=True)
                last.then_inc(s_bc, 1)
            pe.wait_ge(s_ev, 2 * NIN - 1 + 1)
            for h in range(NH):
                last = mm(ps[:, 3, 40 * h:40 * h + TS + NB], sel[:, h, :], small[:, 10:50], start=True, stop=True)
            last.then_inc(s_bc, 1)
            for w, src in enumerate((row_r, row_li)):
                for i in range(NH + 1):
                    n = P if i < NH else TS
                    c = (w * (NH + 1) + i) * NH
                    last = nc.tensor.transpose(ps[0:n, 0, c:c + NH], src[0:NH, i * P:i * P + n], ident[0:NH, 0:NH])
            last.then_inc(s_col, 1)

            def group_sum(n, conv, head, banks):
                pe.wait_ge(s_gsq, n + 1)
                parts = []
                if conv is not None:
                    parts.append((conv, 0))
                if head is not None:
                    parts.append((CT + head, 1))
                for i, slot in parts:
                    for q in range(2):
                        last = mm(ps[0:GR, banks[q], 0:HF], fsel[:, i, :], sq[:, slot, q * HF:(q + 1) * HF],
                                  start=(i == parts[0][0]), stop=(i == parts[-1][0]))
                last.then_inc(s_gst, 1)

            for h in range(NH):
                if h == 0:
                    pe.wait_ge(s_colc, 1)
                else:
                    pe.wait_ge(s_stb, h)
                for i in range(NH):
                    nc.tensor.transpose(ps[:, 0, i * P:(i + 1) * P], zk[:, h, i * P:(i + 1) * P], ident[:])
                    nc.tensor.transpose(ps[:, 1, i * P:(i + 1) * P], zv[:, h, i * P:(i + 1) * P], ident[:])
                nc.tensor.transpose(ps[0:TS, 2, 0:P], zk[:, h, TP:T], ident[:])
                nc.tensor.transpose(ps[0:TS, 2, P:2 * P], zv[:, h, TP:T], ident[:]).then_inc(s_tok, 1)
                if h == 0:
                    pe.wait_ge(s_bce, NH + 1)
                else:
                    pe.wait_ge(s_stc, h)
                for i, (b, c) in enumerate(((3, 0), (4, 0), (5, 0), (4, 384))):
                    mm(ps[:, b, c:c + TP - i * P], zk[:, h, i * P:(i + 1) * P], zq[:, h, i * P:TP], start=True, stop=True)
                mm(ps[0:TS, 5, 256:256 + TS], zk[:, h, TP:T], zq[:, h, TP:T], start=True, stop=True).then_inc(s_sp, 1)
                pe.wait_ge(s_tokc, h + 1)
                group_sum(h, h, h - 1 if h else None, (0, 1))
                pe.wait_ge(s_p, h + 1)
                for i in range(NH):
                    mm(ps[:, 6, i * P:TP], vtok[:, i, :], er[:, EOFF[i]:EOFF[i] + TP - i * P],
                       start=(i == 0), stop=(i == NH - 1))
                pe.wait_ge(s_c0, 16 * (h + 1))
                pe.wait_ge(s_qn, 1)
                for b in range(NB):
                    mm(ps[:, 2, 256 + b * NL:256 + (b + 1) * NL], csb[:, b, :], qwi[:, h, b * NL:(b + 1) * NL],
                       start=(b == 0), stop=False)
                mm(ps[:, 2, 256:256 + TS], vtok[0:TS, NH, :], er[0:TS, EW:EW + TS], start=False, stop=True).then_inc(s_num, 1)
                for i in range(NH):
                    mm(ps[0:GR, 7, i * P:TP], dsel[:, h, :], er[:, EOFF[i]:EOFF[i] + TP - i * P],
                       start=(h == 0 and i == 0), stop=(h == NH - 1 and i == NH - 1))
                mm(ps[0:GR, 5, 288:288 + TS], dsel[:, h, :], qn[:, h, :], start=True, stop=False)
                mm(ps[0:GR, 5, 288:288 + TS], dsel[0:TS, h, :], er[0:TS, EW:EW + TS], start=False, stop=True).then_inc(s_den, 1)
                pe.wait_ge(s_vw, h + 1)
                pe.wait_ge(s_gacc, h + 1)
                for i in range(NH):
                    mm(ps[:, 0, 0:DH + 1], ktok[:, i, :], vw[:, i, :], start=(i == 0), stop=(i == NH - 1))
                mm(ps[:, 0, 136:136 + NB], ktok[0:TS, NH, :], wsm[:], start=True, stop=True)
                for i, b in enumerate((1, 3)):
                    last = mm(ps[:, b, :], ktok[0:TS, NH, :], vsm[:, 4 * i:4 * i + 4, :], start=True, stop=True)
                last.then_inc(s_stp, 1)

            pe.wait_ge(s_stc, NH)
            group_sum(NH, None, NH - 1, (4, 5))
            pe.wait_ge(s_glo, 1)
            for i in range(CT + NH):
                if i >= 4:
                    pe.wait_ge(s_y, i - 1)
                rows = slice(0, 8) if i < CT else slice(32, GR)
                for x in (grHi, grLo):
                    for h in range(2):
                        last = mm(bcast_pair(i)[:, h], bselr[rows, i % 4, :], x[rows, h * HF:(h + 1) * HF],
                                  start=(x is grHi), stop=(x is grLo))
                last.then_inc(s_gbc, 1)
            project(S_OUT, NOUT, 2 * NIN - 1, KT)
            square_sum(1)
            project(S_PQ, NPQ, 2 * (NIN + NOUT) - 1, 2 * KT)
            pe.wait_ge(s_key, 16)
            pe.wait_ge(s_ev, 1 + 2 * (NIN + NOUT + NPQ) - 1)
            for i, t0 in enumerate(STILES):
                if i >= 2:
                    pe.wait_ge(s_sc, i - 1)
                for j in range(HP):
                    last = mm(ps[:, 4 * ((i + 1) % 2) + j // 4, (j % 4) * NKEY:(j % 4 + 1) * NKEY], qT[:, j, t0:t0 + P],
                              keys[:, j, :], start=True, stop=True)
                last.then_inc(s_scp, 1)
            pe.wait_ge(s_sc, NST - 1)

            def product(n, j, hi_in, lo_in, free):
                pe.wait_ge(s_tlo, n + 1)
                pe.wait_ge(*free)
                s = 2 * (j % 2)
                for k in range(KT):
                    hi, lo = tHi[:, j % 2, k, :], tLo[:, j % 2, k, :]
                    for w, x, first, end in ((lo, hi_in, k == 0, False), (hi, hi_in, False, False),
                                             (hi, lo_in, False, k == KT - 1)):
                        for h in range(2):
                            last = mm(ps[:, s + h, 0:HF], w, x[:, k, h * HF:(h + 1) * HF], start=first, stop=end)
                last.then_inc(s_prod, 1)

            def gate_product(st, j):
                pe.wait_ge(s_oh, st + 2)
                pe.wait_ge(s_gadd, st + 1)
                for t in range(STEP_TOK):
                    last = mm(ps[:, 4 + t // 2, (t % 2) * 2 * P:(t % 2 + 1) * 2 * P], oh2[:, j % 2, t, :],
                              w1[:, j % 2, t].rearrange("p w c -> p (w c)"), start=True, stop=True)
                last.then_inc(s_gmm, 1)

            with pe.Fori(0, Q_GATE) as i:
                for j in range(4):
                    product(4 * i + j, j, hHi, hLo, (s_gelu, 4 * i + (j + 1)))
            pe.wait_ge(s_best, 1)
            for q in range(3):
                for i in range(NST):
                    out = ps[:, 4 + q, i * P:(i + 1) * P] if i < 4 else ps[:, 7, q * P:(q + 1) * P]
                    last = nc.tensor.transpose(out, best[:, q, i, :], ident[:])
            last.then_inc(s_bestT, 1)
            with pe.Fori(0, NTB) as i:
                for j in range(4):
                    product(4 * i + (4 * Q_GATE + j), j, hHi, hLo, (s_gelu, 4 * i + (4 * Q_GATE + j + 1)))
                    gate_product(4 * i + j, j)
            for n in range(4 * (Q_GATE + NTB), NCH):
                product(n, n % 4, hHi, hLo, (s_gelu, n + 1))
            pe.wait_ge(s_gelu, NCH + 1)
            with pe.Fori(0, NCH // GRP // 2 - 1) as i:
                for g in range(2):
                    pe.wait_ge(s_alo, 2 * GRP * i + GRP * (g + 1))
                    for j in range(KT):
                        n = 2 * GRP * i + (GRP * g + j)
                        product(n + NCH, j, actHi[g], actLo[g], (s_flush, n + (KT - 1)))
            for g in range(2):
                pe.wait_ge(s_alo, NCH - GRP * (1 - g))
                for j in range(KT):
                    n = NCH - 2 * GRP + GRP * g + j
                    product(n + NCH, j, actHi[g], actLo[g], (s_flush, n + (KT - 1)))
            square_sum(2)

        @block.scalar
        def _(act):
            link = linker(act, s_ach)
            f = nc.scalar.activation

            def square(r, k):
                if r:
                    act.wait_ge(s_x1, KT * (r - 1) + k + 1)
                if k >= 2 or r:
                    act.wait_ge(s_ssq, KT * r + k - 1)
                f(sq[:, k % 2], xT[:, k], ACT.Square).then_inc(s_sq, 1)

            def rms(r):
                act.wait_ge(s_nrm, r + 1)
                f(rs[:].rearrange("p (h t) -> p h t", h=2), ps[:, 4:6, 0:HF], ACT.Sqrt, bias=eps[:], scale=1.0 / D).then_inc(s_rms, 1)

            def hi_part(g, u):
                n = NM1 + g
                act.wait_ge(s_raw[n % RAW], 16 * (n // RAW + 1))
                last = g - 2
                if last == 0:
                    act.wait_ge(s_pj, 1)
                    act.wait_ge(s_wlo, 2)
                elif last >= S_OUT:
                    act.wait_ge(s_pj, 2 * (last - S_OUT + NIN) + u)
                elif last > 0 and last % 2:
                    act.wait_ge(s_pj, last + 1 + u)
                elif last > 0:
                    act.wait_ge(s_modp, NM1 + last // 2)
                half = slice(u * P, (u + 1) * P)
                nc.scalar.copy(wHi[:, g % 2, :, half], raw[:, n % RAW, :, half]).then_inc(s_whi, 1)

            def hi_parts(g):
                hi_part(g, 0)
                hi_part(g, 1)

            def h_hi_samples(r):
                act.wait_ge(s_smp, r + 1)
                nc.scalar.copy(hHi[:, :, TP:T], hf[:, :, TP:T]).then_inc(s_hhs, 1)

            def h_hi(r, k):
                act.wait_ge(s_xn, KT * r + k + 1)
                f(hHi[:, k, 0:TP], hf[:, k, 0:TP], ACT.Identity, bias=mod[:, 3 * r * KT + k, 0:1]).then_inc(s_hhi, 1)

            def evacuate(n, out, func=ACT.Identity, scale=1.0):
                act.wait_ge(s_pj, n + 1)
                f(out.rearrange("p (h t) -> p h t", h=2), pair(n), func, scale=scale).then_inc(s_ev, 1)

            act.sem_inc(s_ev, 1)
            act.sem_inc(s_modr, 2)
            act.sem_inc(s_gelu, 2)
            act.wait_ge(s_cond, 16)
            f(cT[:], cT[:], ACT.Silu).then_inc(s_silu, 1)

            def mod_rows_out(n, j):
                act.wait_ge(s_modp, n + 1)
                act.wait_ge(s_modt, n + 1)
                f(mrow[:, j], ps[0:NSEQ, j, 0:GC], ACT.Identity).then_inc(s_modr, 1)

            for n in range(NM1):
                mod_rows_out(n, n % 2)
                if n == 0:
                    act.wait_ge(s_x, 16)
                if n < KT // 2:
                    square(0, 2 * n)
                    square(0, 2 * n + 1)
                if n == NMA - 3:
                    act.wait_ge(s_const, 2)
                    rms(0)
                if n == NMA - 1:
                    hi_parts(0)
                if n == NMA:
                    h_hi_samples(0)
                    h_hi(0, 0)
                    h_hi(0, 1)
            for k in range(2, KT):
                h_hi(0, k)
                if k == 3:
                    hi_parts(1)

            def mod_rows2_out(m):
                act.wait_ge(s_modp, m + 1)
                act.wait_ge(s_modt, m + 1)
                f(mrow2[:, m % 2], ps[0:2 * NSEQ, 4 + m % 2, 0:GC], ACT.Identity).then_inc(s_modr, 1)

            dest = {0: xc, 1: bg, 3: zq, 4: zk, 5: zv, 6: zo}
            for g in range(NIN):
                if g == 0:
                    evacuate(0, row_li[:])
                else:
                    for u in range(2):
                        n = 2 * g - 1 + u
                        kind, i = (n - 1) // 4, (n - 1) % 4
                        if kind == 2:
                            act.wait_ge(s_pj, n + 1)
                            s = 2 * (n % 2)
                            f(up[:, i, 2:2 + HF], ps[:, s, 0:HF], ACT.Identity)
                            f(up[:, i, 2 + HF:2 + TP], ps[:, s + 1, 0:TP - HF], ACT.Identity)
                            f(us[:, i, :, 2:2 + NL], ps[:, s + 1, TP - HF:HF].rearrange("p (b l) -> p b l", l=NL),
                              ACT.Identity).then_inc(s_ev, 1)
                        elif kind == 6:
                            evacuate(n, zo[:, i], ACT.Sigmoid)
                        else:
                            evacuate(n, dest[kind][:, i], scale=DH ** -0.5 if kind == 4 else 1.0)
                        if 2 * g + 1 < S_OUT:
                            hi_part(2 * g + 1, u)
                if g:
                    mod_rows2_out(NM1 + g - 1)
                if 2 * g + 2 < S_OUT:
                    hi_parts(2 * g + 2)
                if g == 3:
                    act.wait_ge(s_rowa, 1)
                    link(f(row_t[:], row_t[:], ACT.Exp))
                    f(row_t[:], row_t[:], ACT.Ln, bias=1.0).then_inc(s_rowe, 1)
                if g == 5:
                    act.wait_ge(s_rows, 1)
                    f(row_t[:], row_t[:], ACT.Exp, scale=-1.0)
                    f(row_li[0:NH], row_li[0:NH], ACT.Exp)
                    f(small[:, 10:50], small[:, 10:50], ACT.Exp).then_inc(s_rowx, 1)

            act.wait_ge(s_conv, 1)
            for h in range(NH):
                act.wait_ge(s_bc, h + 1)
                s = 4 + 2 * (h % 2)
                f(mb[:, h].rearrange("p (h t) -> p h t", h=2), ps[:, s:s + 2, 0:HF], ACT.Identity).then_inc(s_bce, 1)
            act.wait_ge(s_bc, NH + 1)
            f(wib[:].rearrange("p h c -> p (h c)"), ps[:, 3, 0:NH * (TS + NB)], ACT.Identity).then_inc(s_bce, 1)
            act.wait_ge(s_col, 1)
            f(rcol[:, :, 0:NH, :], ps[:, 0, 0:40].rearrange("p (w i h) -> p w i h", w=2, h=NH)[:, :, 0:NH, :], ACT.Identity)
            f(rcol[0:TS, :, NH, :], ps[0:TS, 0, 0:40].rearrange("p (w i h) -> p w i h", w=2, h=NH)[:, :, NH, :],
              ACT.Identity).then_inc(s_colc, 1)
            for h in range(NH):
                if h:
                    act.wait_ge(s_gst, h)
                last = f(sq[:, 0], xc[:, h], ACT.Square)
                if h:
                    act.wait_ge(s_hm, h)
                    last = f(sq[:, 1], zq[:, h - 1], ACT.Square)
                last.then_inc(s_gsq, 1)
                act.wait_ge(s_tok, h + 1)
                if h:
                    act.wait_ge(s_stp, h)
                f(ktok[:, 0:NH, :], ps[:, 0, :].rearrange("p (i d) -> p i d", i=NH), ACT.Identity)
                f(vtok[:, 0:NH, :], ps[:, 1, :].rearrange("p (i d) -> p i d", i=NH), ACT.Identity)
                f(ktok[0:TS, NH, :], ps[0:TS, 2, 0:P], ACT.Identity)
                f(vtok[0:TS, NH, :], ps[0:TS, 2, P:2 * P], ACT.Identity).then_inc(s_tokc, 1)
                act.wait_ge(s_er, h + 1)
                f(er[:, 0:EW], er[:, 0:EW], ACT.Exp, scale=-1.0)
                f(er[0:TS, EW:EW + TS], er[0:TS, EW:EW + TS], ACT.Exp, scale=-1.0).then_inc(s_ex, 1)
                if h < 2:
                    hi_parts(S_OUT + h)
            f(idle[:, 0:1], eps[:], ACT.Sqrt)
            act.wait_ge(s_hm, NH)
            f(sq[:, 1], zq[:, NH - 1], ACT.Square).then_inc(s_gsq, 1)
            act.wait_ge(s_drow, 1)
            f(drow[32:GR], drow[32:GR], ACT.Square, scale=EPS ** 0.5).then_inc(s_dsq, 1)
            act.wait_ge(s_gsum, 1)
            f(grp[:], grp[:], ACT.Sqrt).then_inc(s_grms, 1)
            act.wait_ge(s_grow, 1)
            nc.scalar.copy(grHi[:], grp[:]).then_inc(s_ghi, 1)
            act.wait_ge(s_out, 160)
            for k in range(KT):
                act.wait_ge(s_y, k + 1)
                nc.scalar.copy(hHi[:, k], (xc if k < CT else zq)[:, k % 4]).then_inc(s_hhi, 1)
            for g in range(NIN, NIN + NOUT):
                for u in range(2):
                    n = 2 * g - 1 + u
                    k = 2 * (g - NIN) + u
                    evacuate(n, hf[:, k])
                    if k:
                        square(1, k - 1)
                    hi_part(S_OUT - NIN + g + 2, u)
            square(1, KT - 1)
            rms(1)
            h_hi_samples(1)
            for k in range(KT):
                h_hi(1, k)
            for g in range(NIN + NOUT, NIN + NOUT + NPQ):
                for u in range(2):
                    evacuate(2 * g - 1 + u, qT[:, 2 * (g - NIN - NOUT) + u])
                    if g + 2 < NIN + NOUT + NPQ:
                        hi_part(S_OUT - NIN + g + 2, u)
            for i in range(NST):
                act.wait_ge(s_scp, i + 1)
                s = 4 * ((i + 1) % 2)
                f(sc[:, i].rearrange("p (b j) n -> p b (j n)", b=4), ps[:, s:s + 4, :], ACT.Identity).then_inc(s_sc, 1)
                if i in (1, 2):
                    act.wait_ge(s_tab[i - 1], 16)
                    nc.scalar.copy(tHi[:, i - 1], tab[:, i - 1]).then_inc(s_thi, 1)

            def a_step(i, j):
                act.wait_ge(s_prod, 4 * i + (j + 1))
                act.wait_ge(s_gas[j % 2], 32 * i + 16 * (j // 2 + 1))
                f(ga[:, j % 2].rearrange("p (h t) -> p h t", h=2), pair(j), ACT.Gelu_apprx_tanh).then_inc(s_gelu, 1)
                act.wait_ge(s_tab[(j + 2) % 4], 16 * i + 16 * ((j + 2) // 4 + 1))
                nc.scalar.copy(tHi[:, j % 2], tab[:, (j + 2) % 4]).then_inc(s_thi, 1)
                c = 4 * i + j
                act.wait_ge(s_gelu, 4 * i + (j + 3))
                act.dma_start(ga_dram[c] if isinstance(c, int) else ga_dram[bass.ds(c, 1)].rearrange("a p t -> p (a t)"),
                              ga[:, j % 2]).then_inc(s_gas[j % 2], 16)

            act.sem_inc(s_gas[0], 16)
            act.sem_inc(s_gas[1], 16)
            with act.Fori(0, Q_EXP) as i:
                for j in range(4):
                    a_step(i, j)
            act.wait_ge(s_top, 1)
            f(best[:, 0], best[:, 0], ACT.Exp).then_inc(s_gexp, 1)
            for j in range(4):
                a_step(Q_EXP, j)
            act.sem_inc(s_gst2, 16)
            with act.Fori(0, NTB) as i:
                for j in range(4):
                    a_step(i + Q_GATE, j)
                    act.wait_ge(s_gmm, 4 * i + (j + 3))
                    f(stage[:, bass.ds(i % 2, 1), :, STEP_TOK * j:STEP_TOK * (j + 1)].rearrange("p s c t -> p t (s c)"),
                      ps[:, 4:8, :].rearrange("p b (t w c) -> p (b t) w c", w=2, c=P)[:, :, 0, :], ACT.Identity).then_inc(s_gev, 1)
                act.wait_ge(s_gadd, 4 * i + 5)
                act.wait_ge(s_gst2, 16 * i + 16)
                act.dma_start(gt_dram[:, :, bass.ds(i, 1), :].rearrange("q p a (c t) -> p (a q) c t", c=4),
                              stage[:, bass.ds(i % 2, 1)].rearrange("p s (q c) t -> p (s q) c t", c=4)).then_inc(s_gst2, 16)

            def act_hi(c, g, k):
                act.wait_ge(s_a32, c + 1)
                nc.scalar.copy(actHi[g][:, k], a32[:, k % 2]).then_inc(s_ahi, 1)

            for i in range(Q_GATE + NTB, NCH // 4):
                for j in range(4):
                    n = 4 * (i - Q_GATE - NTB) + j
                    for c in ((), (), (0,), (1,), (2,), (3,), (4, 5), (6, 7))[n]:
                        act_hi(c, 0, c)
                    a_step(i, j)

            def out_step(i, s, prep=True, split=True):
                if prep:
                    act_hi(16 * i + (s + GRP), (s // GRP + 1) % 2, s % GRP)
                if split:
                    act.wait_ge(s_prod, 16 * i + (NCH + s + 1))
                    act.wait_ge(s_tab[(s + 2) % 4], 64 * i + 16 * (NCH // 4 + (s + 2) // 4 + 1))
                    nc.scalar.copy(tHi[:, s % 2], tab[:, (s + 2) % 4]).then_inc(s_thi, 1)

            f(idle[:, 1:2], eps[:], ACT.Sqrt)
            with act.Fori(0, NCH // 16 - 1) as i:
                for s in range(16):
                    out_step(i, s)
            for s in range(16):
                out_step(NCH // 16 - 1, s, prep=s < 8, split=s < 14)
                if s >= 9:
                    square(2, s - 9)
            square(2, KT - 1)
            rms(2)

        @block.vector
        def _(v):
            link = linker(v, s_dch)
            tt, tsc, stt = nc.vector.tensor_tensor, nc.vector.tensor_scalar, nc.vector.scalar_tensor_tensor

            def add_square(r, k):
                v.wait_ge(s_sq, KT * r + k + 1)
                if k == 0:
                    nc.vector.tensor_copy(rs[:], sq[:, 0]).then_inc(s_ssq, 1)
                else:
                    v.wait_ge(s_ssq, KT * r + k)
                    tt(rs[:], rs[:], sq[:, k % 2], ALU.add).then_inc(s_ssq, 1)

            def sample_mod(r, func, m):
                hs = smp(hf[:, :, TP:T])
                return tt(hs, hs, over(m, NL), func)

            def norm_tile(r, k):
                stt(hf[:, k, 0:TP], xT[:, k, 0:TP], amod[:, r, k, 0:1], rs[:, 0:TP], ALU.mult, ALU.mult).then_inc(s_xn, 1)

            def lo_tile(r, k):
                v.wait_ge(s_hhi, (2 * KT if r else 0) + k + 1)
                stt(hLo[:, k, 0:TP], hf[:, k, 0:TP], mod[:, 3 * r * KT + k, 0:1], hHi[:, k, 0:TP].bitcast(F32),
                    ALU.add, ALU.subtract).then_inc(s_hlo, 1)

            def make_h(r):
                v.wait_ge(s_rms, r + 1)
                link(nc.vector.reciprocal(rs[:], rs[:]))
                link(tt(hf[:, :, TP:T], xT[:, :, TP:T], rs[:, TP:T].unsqueeze(1).broadcast_to([P, KT, TS]), ALU.mult))
                if r == 0:
                    v.wait_ge(s_modt, NMA + 2)
                    mod_part(0, 2 * KT, 6)
                    link(stt(amod[:, 0], mod[:, KT:2 * KT], 1.0, over(span("g_mix"), NSEQ), ALU.add, ALU.mult))
                link(sample_mod(r, ALU.mult, amod[:, r, :, 1:NSEQ]))
                sample_mod(r, ALU.add, mod[:, 3 * r * KT:(3 * r + 1) * KT, 1:NSEQ]).then_inc(s_smp, 1)
                norm_tile(r, 0)
                norm_tile(r, 1)
                v.wait_ge(s_hhs, r + 1)
                tt(hLo[:, :, TP:T], hf[:, :, TP:T], hHi[:, :, TP:T].bitcast(F32), ALU.subtract)
                for k in range(KT):
                    if k + 2 < KT:
                        norm_tile(r, k + 2)
                    lo_tile(r, k)

            def mod_part(k0, k1, bank):
                link(tt(mod[:, k0:k1], ps[:, bank, 0:(k1 - k0) * NSEQ].rearrange("p (k s) -> p k s", s=NSEQ),
                        over(vec[:, VEC["b_mod"][0] + k0:VEC["b_mod"][0] + k1], NSEQ), ALU.add))

            nc.vector.memset(eps[:], EPS)
            nc.vector.memset(dsel[:], 0.0)
            link(nc.vector.memset(fsel[:], 0.0))
            for i in range(CT):
                for q in range(2):
                    nc.vector.memset(fsel[64 * q:64 * q + 64, i, 2 * i + q:2 * i + q + 1], 1.0 / 64)
            for h in range(NH):
                nc.vector.memset(fsel[:, CT + h, 32 + h:33 + h], 1.0 / DH)
                nc.vector.memset(dsel[:, h, 32 + h:33 + h], 1.0)
            nc.vector.memset(ones[:], 1.0).then_inc(s_const, 1)
            v.wait_ge(s_const, 2)
            nc.vector.tensor_copy(bselr[32:GR], sel[:])
            link(nc.vector.tensor_copy(bselr[0:8], bsel[:]))
            v.wait_ge(s_silu, 1)
            nc.vector.tensor_copy(ident2[:], id2[:])
            link(nc.vector.tensor_copy(c2[:, :, 0:NSEQ], cT[:]))
            tt(c2[:, :, NSEQ:], cT[:], c2[:, :, 0:NSEQ].bitcast(F32), ALU.subtract).then_inc(s_c2, 1)
            v.wait_ge(s_x, 16)
            v.wait_ge(s_vec, 32)
            for k in range(KT):
                add_square(0, k)
            make_h(0)

            link(nc.vector.memset(row_z, 1.0))
            nc.vector.memset(row_z[:, TP:T].rearrange("p (b l) -> p b l", l=NL)[:, :, 0:1], 0.0)
            v.wait_ge(s_ev, 1 + 1)
            link(nc.vector.tensor_copy(row_lf[:], row_li[32:32 + NH, :]))
            tsc(row_li[0:NH], row_li[0:NH], gbias[:, 0:1], None, ALU.add)
            link(tsc(row_lf[:], row_lf[:], gbias[:, 1:2], None, ALU.add))
            stt(row_t[:], row_lf[:], -1.0, row_lf[:], ALU.mult, ALU.min).then_inc(s_rowa, 1)
            v.wait_ge(s_rowe, 1)
            link(stt(row_lf[:], row_lf[:], 0.0, row_t[:], ALU.min, ALU.subtract))
            link(nc.vector.tensor_tensor_scan(row_b[:], row_z, row_lf[:], 0.0, ALU.mult, ALU.add))
            tsc(row_z, row_z, 1.0, BIG, ALU.subtract, ALU.mult)
            link(tt(row_r[:], row_li[0:NH], row_b[:], ALU.subtract))
            link(nc.vector.tensor_copy(row_t[:], row_r[:]))
            tsc(row_t[:, 0:1], row_r[:, 0:1], 0.0, None, ALU.max)
            first = row_t[:, TP:T].rearrange("p (b l) -> p b l", l=NL)[:, :, 0]
            link(tt(first, first, m0, ALU.max))
            link(nc.vector.tensor_tensor_scan(row_m[:], row_z, row_t[:], 0.0, ALU.add, ALU.max))
            ms = row_m[:, TP:T].rearrange("p (b l) -> p b l", l=NL)
            ml = ms[:, :, NL - 1]
            rsm = row_r[:, TP:T].rearrange("p (b l) -> p b l", l=NL)
            link(tt(row_t[:], row_b[:], row_m[:], ALU.add))
            nc.vector.tensor_copy(mout[:, 0:1], row_t[:, TP - 1:TP])
            nc.vector.tensor_copy(mout[:, 1:NSEQ], row_t[:, TP:T].rearrange("p (b l) -> p b l", l=NL)[:, :, NL - 1])
            tsc(row_li[0:NH, 0:TP], row_r[:, 0:TP], row_m[:, TP - 1:TP], None, ALU.subtract)
            tt(row_li[0:NH, TP:T].rearrange("p (b l) -> p b l", l=NL), rsm, over(ml, NL), ALU.subtract)
            tt(wold, m0, ml, ALU.subtract)
            tt(wi.rearrange("p (b l) -> p b l", l=NL), over(m0, NL), ms, ALU.subtract).then_inc(s_rows, 1)

            v.wait_ge(s_ev, 13 + 1)
            v.wait_ge(s_state, 16)
            nc.vector.memset(up[:, :, 0:2], 0.0)
            tt(up[:, :, 2:2 + TP], up[:, :, 2:2 + TP], xc[:, :, 0:TP], ALU.mult)
            link(tt(us[:, :, :, 2:2 + NL], us[:, :, :, 2:2 + NL], smp(xc[:, :, TP:T]), ALU.mult))
            v.sem_inc(s_convout, 1)
            for j in range(3):
                for i in range(CT):
                    w = col("w_conv", j * CT + i)
                    yp, ys = xc[:, i, 0:TP], xc[:, i, TP:T].rearrange("p (b l) -> p b l", l=NL)
                    if j == 0:
                        tsc(yp, up[:, i, j:j + TP], w, None, ALU.mult)
                        last = tsc(ys, us[:, i, :, j:j + NL], w, None, ALU.mult)
                    else:
                        stt(yp, up[:, i, j:j + TP], w, yp, ALU.mult, ALU.add)
                        last = stt(ys, us[:, i, :, j:j + NL], w, ys, ALU.mult, ALU.add)
                link(last)
            tt(xc[:], xc[:], bg[:], ALU.mult).then_inc(s_conv, 1)

            v.wait_ge(s_modt, NMOD + 2)
            mod_part(2 * KT, 6 * KT, 7)
            link(stt(amod[:, 1], mod[:, 4 * KT:5 * KT], 1.0, over(span("g_ffn"), NSEQ), ALU.add, ALU.mult))
            v.sem_inc(s_mods, 1)

            gv = grp[:].rearrange("p (h t) -> p h t", h=2)
            v.wait_ge(s_bce, NH + 1)
            v.wait_ge(s_out, 32)
            nc.vector.memset(drow[:], 0.0)
            nc.vector.tensor_copy(erow[32:GR], row_t[:])
            link(nc.vector.memset(grp[:], EPS))
            link(nc.vector.memset(grp[32:GR], 0.0))
            v.wait_ge(s_n0, 16)
            v.wait_ge(s_colc, 1)
            link(tt(qwi[:], zq[:, :, TP:T], wib[:, :, 0:TS], ALU.mult))
            tt(smp(qn[:]), smp(qwi[:]), over(n0[:], NL), ALU.mult).then_inc(s_qn, 1)
            for h in range(NH):
                if h:
                    v.wait_ge(s_den, h)
                for i in range(NH):
                    tsc(er[:, EOFF[i]:EOFF[i] + TP - i * P], mb[:, h, i * P:TP], rcol[:, 0, i, h:h + 1], 0.0,
                        ALU.subtract, ALU.max)
                tsc(er[0:TS, EW:EW + TS], mb[0:TS, h, TP:T], rcol[0:TS, 0, NH, h:h + 1], 0.0,
                    ALU.subtract, ALU.max).then_inc(s_er, 1)
                v.wait_ge(s_tokc, h + 1)
                if h:
                    v.wait_ge(s_stp, h)
                tt(vw[:, :, 0:DH], vtok[:, 0:NH, :], over(rcol[:, 1, 0:NH, h], DH), ALU.mult)
                nc.vector.tensor_copy(vw[:, :, DH], rcol[:, 1, 0:NH, h])
                tsc(wsm[:], bmask[:], rcol[0:TS, 1, NH, h:h + 1], None, ALU.mult)
                link(tsc(vsw[:], vtok[0:TS, NH, :], rcol[0:TS, 1, NH, h:h + 1], None, ALU.mult))
                tt(vsm[:], vsw[:].unsqueeze(1).broadcast_to([TS, NB, DH]), over(bmask[:], DH), ALU.mult).then_inc(s_vw, 1)
                v.wait_ge(s_ex, h + 1)
                v.wait_ge(s_sp, h + 1)
                for i in range(NH):
                    c = EOFF[i]
                    last = tt(er[:, c:c + P], er[:, c:c + P], cmask[:], ALU.mult)
                link(tt(er[0:TS, EW:EW + TS], er[0:TS, EW:EW + TS], smask[:], ALU.mult))
                for i, (b, c) in enumerate(((3, 0), (4, 0), (5, 0), (4, 384))):
                    e = er[:, EOFF[i]:EOFF[i] + TP - i * P]
                    tt(e, e, ps[:, b, c:c + TP - i * P], ALU.mult)
                tt(er[0:TS, EW:EW + TS], er[0:TS, EW:EW + TS], ps[0:TS, 5, 256:256 + TS], ALU.mult).then_inc(s_p, 1)
                v.wait_ge(s_gst, h + 1)
                link(tt(gv, gv, ps[0:GR, 0:2, 0:HF], ALU.add))
                v.sem_inc(s_gacc, 1)
                v.wait_ge(s_num, h + 1)
                tt(zq[:, h, 0:TP], ps[:, 6, :], zo[:, h, 0:TP], ALU.mult)
                tt(zq[:, h, TP:T], ps[:, 2, 256:256 + TS], zo[:, h, TP:T], ALU.mult).then_inc(s_hm, 1)
                v.wait_ge(s_den, h + 1)
                tt(drow[32:GR, TP:T], drow[32:GR, TP:T], ps[32:GR, 5, 288:288 + TS], ALU.add)
                tt(nso[:, h], n0[:, h], wib[:, h, TS:TS + NB], ALU.mult)
                link(tt(csb[:], csb[:], over(wib[:, h, TS:TS + NB], DH), ALU.mult))
                v.wait_ge(s_stp, h + 1)
                tt(csb[:, 0:4], csb[:, 0:4], ps[:, 1, :].rearrange("p (b d) -> p b d", b=4), ALU.add)
                nc.vector.tensor_copy(cst[:, h], ps[:, 0, 0:DH])
                nc.vector.tensor_copy(npo[:, h:h + 1], ps[:, 0, DH:DH + 1])
                tt(nso[:, h], nso[:, h], ps[:, 0, 136:136 + NB], ALU.add).then_inc(s_stb, 1)
                tt(csb[:, 4:8], csb[:, 4:8], ps[:, 3, :].rearrange("p (b d) -> p b d", b=4), ALU.add).then_inc(s_stc, 1)

            dp, dsm = drow[32:GR, 0:TP], drow[32:GR, TP:T]
            tt(dp, erow[32:GR, 0:TP], ps[32:GR, 7, :], ALU.max)
            link(stt(dsm, dsm, -1.0, dsm, ALU.mult, ALU.max))
            tt(dsm, erow[32:GR, TP:T], dsm, ALU.max)
            stt(dp, ps[32:GR, 7, :], -1.0, dp, ALU.mult, ALU.max).then_inc(s_drow, 1)
            v.wait_ge(s_gst, NH + 1)
            link(tt(gv, gv, ps[0:GR, 4:6, 0:HF], ALU.add))
            v.wait_ge(s_dsq, 1)
            tt(grp[32:GR], grp[32:GR], drow[32:GR], ALU.add).then_inc(s_gsum, 1)
            v.wait_ge(s_grms, 1)
            nc.vector.reciprocal(grp[:], grp[:]).then_inc(s_grow, 1)
            v.wait_ge(s_ghi, 1)
            tt(grLo[:], grp[:], grHi[:].bitcast(F32), ALU.subtract).then_inc(s_glo, 1)
            def mixer_lo(k):
                v.wait_ge(s_hhi, KT + k + 1)
                tt(hLo[:, k], (xc if k < CT else zq)[:, k % 4], hHi[:, k].bitcast(F32), ALU.subtract).then_inc(s_hlo, 1)

            for i in range(CT + NH):
                v.wait_ge(s_gbc, i + 1)
                y = (xc if i < CT else zq)[:, i % 4].rearrange("p (h t) -> p h t", h=2)
                stt(y, y, col("g_conv", i) if i < CT else col("g_mlstm", i - CT), bcast_pair(i),
                    ALU.mult, ALU.mult).then_inc(s_y, 1)
                if i:
                    mixer_lo(i - 1)
            mixer_lo(KT - 1)
            for k in range(KT):
                v.wait_ge(s_ev, 1 + 2 * NIN - 1 + k + 1)
                xs = xT[:, k, TP:T].rearrange("p (b l) -> p b l", l=NL)
                ms_ = hf[:, k, TP:T].rearrange("p (b l) -> p b l", l=NL)
                stt(xT[:, k, 0:TP], hf[:, k, 0:TP], mod[:, 2 * KT + k, 0:1], xT[:, k, 0:TP], ALU.mult, ALU.add)
                link(tt(ms_, ms_, over(mod[:, 2 * KT + k, 1:NSEQ], NL), ALU.mult))
                tt(xs, xs, ms_, ALU.add).then_inc(s_x1, 1)
                if k:
                    add_square(1, k - 1)
            add_square(1, KT - 1)
            v.wait_ge(s_x1, KT)
            make_h(1)

            CHAIN = 15

            def chain(i, n):
                v.wait_ge(s_tk, CHAIN * i + n)
                v.nop(nofuse=True)

            v.wait_ge(s_scp, NST)
            with v.Fori(0, NST) as i:
                def row(j):
                    return scur[:, j]
                v.wait_ge(s_sc, i + 1)
                nc.vector.tensor_copy(scur[:], sc[:, bass.ds(i, 1)].rearrange("p a j n -> p (a j) n")).then_inc(s_tk, 1)
                chain(i, 1)
                for j in range(HP):
                    last = nc.vector.max(m16[:, j, 0:8], row(j))
                last.then_inc(s_tk, 1)
                chain(i, 2)
                for j in range(HP):
                    nc.vector.max_index(ix[:, j, 0:8], m16[:, j, 0:8], row(j))
                    last = nc.vector.match_replace(row(j), m16[:, j, 0:8], row(j), LOWEST)
                last.then_inc(s_tk, 1)
                chain(i, 3)
                for j in range(HP):
                    last = nc.vector.max(m16[:, j, 8:16], row(j))
                last.then_inc(s_tk, 1)
                chain(i, 4)
                for j in range(HP):
                    last = nc.vector.max_index(ix[:, j, 8:16], m16[:, j, 8:16], row(j))
                last.then_inc(s_tk, 1)
                halves = m16[:].rearrange("p (h two) k -> p h two k", two=2)
                chain(i, 5)
                nc.vector.tensor_copy(ixf[:], ix[:])
                tt(cand[:], over(halves[:, :, 0, :], PK),
                   halves[:, :, 1, :].unsqueeze(2).broadcast_to([P, PH, PK, PK]), ALU.add).then_inc(s_tk, 1)
                chain(i, 6)

                def sums(h):
                    return cand[:, h].rearrange("p a b -> p (a b)")

                def top(h, r):
                    return tcur[:, h, r:r + 8]
                for h in range(PH):
                    last = nc.vector.max(top(h, 0), sums(h))
                last.then_inc(s_tk, 1)
                chain(i, 7)
                for h in range(PH):
                    nc.vector.max_index(pos16[:, h, 0:8], top(h, 0), sums(h))
                    last = nc.vector.match_replace(sums(h), top(h, 0), sums(h), LOWEST)
                last.then_inc(s_tk, 1)
                chain(i, 8)
                for h in range(PH):
                    last = nc.vector.max(top(h, 8), sums(h))
                last.then_inc(s_tk, 1)
                chain(i, 9)
                for h in range(PH):
                    last = nc.vector.max_index(pos16[:, h, 8:16], top(h, 8), sums(h))
                last.then_inc(s_tk, 1)
                chain(i, 10)
                flat = pos16[:].rearrange("p h k -> p (h k)")
                tsc(pab[:, 0], flat, 4, None, ALU.logical_shift_right)
                tsc(pab[:, 1], flat, PK - 1, None, ALU.bitwise_and).then_inc(s_tk, 1)
                tt(best[:, 0, bass.ds(i, 1), :].rearrange("p a (h k) -> p (a h) k", k=PK), tcur[:], over(tcur[:, :, 0], PK),
                   ALU.subtract)
                v.wait_ge(s_tk, CHAIN * i + 11)
                nc.vector.tensor_copy(pabf[:], pab[:]).then_inc(s_tk, 1)
                v.wait_ge(s_tk, CHAIN * i + 12)
                rank = iota[:, 0:PK].unsqueeze(1).broadcast_to([P, PH * PK, PK])
                half = ixf[:].rearrange("p (h two) k -> p h two k", two=2)
                e = (eqa, eqb)
                for w in range(2):
                    last = tt(e[w][:].rearrange("p h k a -> p (h k) a"), rank, over(pabf[:, w], PK), ALU.is_equal)
                last.then_inc(s_tk, 1)
                v.wait_ge(s_tk, CHAIN * i + 13)
                for w in range(2):
                    last = tt(e[w][:], e[w][:], half[:, :, w, :].unsqueeze(2).broadcast_to([P, PH, PK, PK]), ALU.mult)
                last.then_inc(s_tk, 1)
                v.wait_ge(s_tk, CHAIN * i + 14)
                for w in range(2):
                    last = nc.vector.tensor_reduce(best[:, 1 + w, bass.ds(i, 1), :].rearrange("p a n -> p (a n)"),
                                                   e[w][:].rearrange("p h k a -> p (h k) a"), AXX, ALU.add)
                last.then_inc(s_tk, 1)
                v.wait_ge(s_tk, CHAIN * i + 15)
            v.sem_inc(s_top, 1)
            v.wait_ge(s_gexp, 1)
            w_ = best[:, 0].rearrange("p i (h k) -> p (i h) k", k=PK)
            link(nc.vector.tensor_reduce(ssum[:], w_, AXX, ALU.add))
            link(nc.vector.reciprocal(ssum[:], ssum[:]))
            tt(w_, w_, over(ssum[:], PK), ALU.mult).then_inc(s_best, 1)
            v.wait_ge(s_bestT, 1)
            nc.vector.tensor_copy(idxT[:, 2, 0:TP], ps[:, 4, :])
            nc.vector.tensor_copy(idxT[:, 2, TP:T], ps[:, 7, P - TS:P])
            for q in range(2):
                nc.vector.tensor_copy(idxT[:, q, 0:TP], ps[:, 5 + q, :])
                last = nc.vector.tensor_copy(idxT[:, q, TP:T], ps[:, 7, (q + 2) * P - TS:(q + 2) * P])
            link(last)
            link(nc.vector.tensor_copy(gHr[:], idxT[:, 2, :]))
            link(tt(idxT[:, 3], idxT[:, 2], gHr[:].bitcast(F32), ALU.subtract))
            link(nc.vector.tensor_copy(idxT[:, 2], gHr[:].bitcast(F32)))

            def one_hots(i, j):
                def cols(q, n):
                    return over(idxT[:, q:q + n, bass.ds(TB * i + STEP_TOK * j, STEP_TOK)].rearrange("p w t -> p t w"), P)
                keys_ = iota[:].unsqueeze(1).broadcast_to([P, STEP_TOK, P])
                v.wait_ge(s_oh, 4 * i + (j + 1))
                tt(oh1[:].unsqueeze(2), keys_.unsqueeze(2), cols(0, 1), ALU.is_equal).then_inc(s_oh1, 1)
                v.wait_ge(s_gmm, 4 * i + (j + 1))
                tt(oh2[:, j % 2].unsqueeze(2), keys_.unsqueeze(2), cols(1, 1), ALU.is_equal)
                v.wait_ge(s_oh1, 4 * i + (j + 1))
                tt(w1[:, j % 2], oh1[:].unsqueeze(2).broadcast_to([P, STEP_TOK, 2, P]), cols(2, 2), ALU.mult).then_inc(s_oh, 1)

            def add_lo(i, j):
                v.wait_ge(s_gev, 4 * i + (j + 1))
                g_ = stage[:, bass.ds(i % 2, 1), :, STEP_TOK * j:STEP_TOK * (j + 1)].rearrange("p s c t -> p t (s c)")
                tt(g_, g_, ps[:, 4:8, :].rearrange("p b (t w c) -> p (b t) w c", w=2, c=P)[:, :, 1, :], ALU.add).then_inc(s_gadd, 1)

            v.sem_inc(s_gadd, 1)
            v.sem_inc(s_oh, 1)
            v.sem_inc(s_flush, KT - 1)
            one_hots(0, 0)
            with v.Fori(0, NTB - 1) as i:
                for j in range(4):
                    one_hots(i + (j + 1) // 4, (j + 1) % 4)
                    add_lo(i, j)
            for j in range(4):
                if j < 3:
                    one_hots(NTB - 1, j + 1)
                add_lo(NTB - 1, j)

            def act_lo(g, k, count):
                v.wait_ge(s_ahi, count)
                tt(actLo[g][:, k], a32[:, k % 2], actHi[g][:, k].bitcast(F32), ALU.subtract).then_inc(s_alo, 1)

            link(nc.vector.memset(acc[:], 0.0))
            for c in range(GRP):
                v.wait_ge(s_gin[c % 4], 16 * (c // 4 + 1))
                v.wait_ge(s_gt[c // 4 % 2], 16)
                tt(a32[:, c % 2].rearrange("p (b t) -> p b t", t=TB), gin[:, c % 4].rearrange("p (b t) -> p b t", t=TB),
                   gt[:, c // 4 % 2, :, c % 4, :], ALU.mult).then_inc(s_a32, 1)
                act_lo(0, c, c + 1)

            def out_step(i, s, prep=True):
                if prep:
                    c = s + GRP
                    v.wait_ge(s_gin[c % 4], 64 * i + 16 * (c // 4 + 1))
                    v.wait_ge(s_gt[c // 4 % 2], 32 * i + 16 * (c // 8 + 1))
                    tt(a32[:, c % 2].rearrange("p (b t) -> p b t", t=TB), gin[:, c % 4].rearrange("p (b t) -> p b t", t=TB),
                       gt[:, c // 4 % 2, :, c % 4, :], ALU.mult).then_inc(s_a32, 1)
                    act_lo((s // GRP + 1) % 2, s % GRP, 16 * i + (c + 1))
                v.wait_ge(s_prod, 16 * i + (NCH + s + 1))
                k = s % KT
                av = acc[:, k].rearrange("p (h t) -> p h t", h=2)
                v.wait_ge(s_flush, 16 * i + (s + 1))
                tt(av, av, pair(s), ALU.add).then_inc(s_flush, 1)

            v.wait_ge(s_gelu, NCH + 2)
            v.sem_inc(s_flush, 1)
            with v.Fori(0, NCH // 16 - 1) as i:
                for s in range(16):
                    out_step(i, s)
            for s in range(16):
                out_step(NCH // 16 - 1, s, prep=s < 8)
                if s >= 8:
                    k = s - 8
                    xs = xT[:, k, TP:T].rearrange("p (b l) -> p b l", l=NL)
                    ms_ = acc[:, k, TP:T].rearrange("p (b l) -> p b l", l=NL)
                    v.wait_ge(s_flush, NCH - 8 + k + 1 + KT)
                    stt(xT[:, k, 0:TP], acc[:, k, 0:TP], mod[:, 5 * KT + k, 0:1], xT[:, k, 0:TP], ALU.mult, ALU.add)
                    link(tt(ms_, ms_, over(mod[:, 5 * KT + k, 1:NSEQ], NL), ALU.mult))
                    tt(xs, xs, ms_, ALU.add).then_inc(s_x1, 1)
                    if k:
                        add_square(2, k - 1)
            add_square(2, KT - 1)
            v.wait_ge(s_rms, 3)
            link(nc.vector.reciprocal(rs[:], rs[:]))
            for k in range(KT):
                stt(acc[:, k], xT[:, k], col("g_final", k), rs[:], ALU.mult, ALU.mult).then_inc(s_yo, 1)


def kernel(**inputs):
    import numpy as np
    import concourse.bacc as bacc
    from concourse.bass_utils import run_bass_kernel_spmd

    i = {k: np.asarray(v) for k, v in inputs.items()}

    def tiles(v):
        return v.reshape(-1, P).T

    def granules(w):
        return w.reshape(KT, P, -1, GC).transpose(2, 1, 0, 3)

    w_in = i["w_in"][0]
    gates = np.zeros((D, GC), w_in.dtype)
    gates[:, 0:NH] = w_in[:, 3584:3588]
    gates[:, 32:32 + NH] = w_in[:, 3588:3592]
    w_mod = granules(i["w_mod"][0])
    pairs = np.stack([granules(w_in[:, 0:3584]), w_mod[NM1:]], axis=1).reshape(-1, P, KT, GC)
    arrays = {
        "xT": np.concatenate([i["x_prompt"].reshape(TP, D), i["x_sample"].reshape(TS, D)]).reshape(T, KT, P).transpose(2, 1, 0),
        "cT": np.concatenate([i["c_prompt"], i["c_sample"]]).reshape(NSEQ, KT, P).transpose(2, 1, 0),
        "vecs": np.concatenate([tiles(i["g_mix"][0]), tiles(i["g_ffn"][0]), tiles(i["g_final"]), tiles(i["g_conv"][0]),
                                tiles(i["g_mlstm"][0]), tiles(i["w_conv"][0].reshape(-1)), tiles(i["b_mod"][0])], axis=1),
        "rows": np.concatenate([i["b_i"].T, i["b_f"].T, i["state_mlstm_m"][0].T], axis=1),
        "sconv": i["state_conv"][0].reshape(NB, 2, CT, P).transpose(3, 2, 0, 1),
        "C0": i["state_mlstm_C"][0].transpose(2, 1, 0, 3),
        "n0": i["state_mlstm_n"][0].transpose(2, 1, 0),
        "w": np.concatenate([w_mod[:NM1], granules(gates), pairs,
                             granules(i["w_out"][0]), granules(i["w_pq"][0])]),
        "keys": i["sub_keys"][0].transpose(3, 1, 0, 2).reshape(P, HP, NKEY),
        "tab": np.concatenate([i["u_tab"][0].reshape(NCH, P, KT, P).transpose(0, 3, 2, 1).reshape(NCH, P, D),
                               i["v_tab"][0].reshape(NCH // GRP, GRP, P, KT, P).transpose(0, 3, 2, 1, 4).reshape(NCH, P, D)]),
    }
    outs = {"y": (P, KT, T), "conv_p": (P, CT, 2), "conv_s": (P, CT, NB, 2), "C_p": (P, NH, DH), "n_p": (P, NH),
            "C_s": (P, NH, NB, DH), "n_s": (P, NH, NB), "m": (NH, NSEQ)}
    nc = bacc.Bacc("TRN2", target_bir_lowering=False, num_devices=1)
    arrays = {k: np.ascontiguousarray(v) for k, v in arrays.items()}
    a = {k: nc.dram_tensor("in_" + k, v.shape, mybir.dt.from_np(v.dtype), kind="ExternalInput").ap() for k, v in arrays.items()}
    o = {k: nc.dram_tensor("out_" + k, s, F32, kind="ExternalOutput").ap() for k, s in outs.items()}
    build(nc, a, o)
    r = run_bass_kernel_spmd(nc, [{"in_" + k: v for k, v in arrays.items()}], core_ids=[0]).results[0]
    r = {k: np.asarray(r["out_" + k]) for k in outs}
    y = r["y"].transpose(2, 1, 0).reshape(T, D)
    return (y[:TP].reshape(1, TP, D), y[TP:].reshape(NB, NL, D),
            r["conv_p"].transpose(2, 1, 0).reshape(1, 1, 2, DC),
            r["C_p"].transpose(1, 0, 2).reshape(1, 1, NH, DH, DH),
            r["n_p"].T.reshape(1, 1, NH, DH), r["m"][:, 0].reshape(1, 1, NH),
            r["conv_s"].transpose(2, 3, 1, 0).reshape(1, NB, 2, DC),
            r["C_s"].transpose(2, 1, 0, 3).reshape(1, NB, NH, DH, DH),
            r["n_s"].transpose(2, 1, 0).reshape(1, NB, NH, DH), r["m"][:, 1:].T.reshape(1, NB, NH))
```
